# Optimizing a Trainium2 kernel written in Bass

```python
import math
import jax, jax.numpy as jnp
from jax import lax
import numpy as np

D_MODEL = 2048
BATCH = 1
SEQ = 512
DEPTH = 1

GLA_HEADS = 4
GLA_DK = D_MODEL // 16
GLA_DV = D_MODEL // 8
GLA_KEY_WIDTH = GLA_HEADS * GLA_DK
GLA_VAL_WIDTH = GLA_HEADS * GLA_DV
GLA_GATE_RANK = 16
GLA_TAU = 16.0
GLA_CHUNK = 64
CONV_WIDTH = D_MODEL // 2
CONV_KERNEL = 31
MIX_WIDTH = GLA_VAL_WIDTH + CONV_WIDTH
IN_WIDTH = 2 * GLA_KEY_WIDTH + 2 * GLA_VAL_WIDTH + GLA_GATE_RANK + 2 * CONV_WIDTH
SPLIT_Q = GLA_KEY_WIDTH
SPLIT_K = 2 * GLA_KEY_WIDTH
SPLIT_V = 2 * GLA_KEY_WIDTH + GLA_VAL_WIDTH
SPLIT_R = 2 * GLA_KEY_WIDTH + 2 * GLA_VAL_WIDTH
SPLIT_A = 2 * GLA_KEY_WIDTH + 2 * GLA_VAL_WIDTH + GLA_GATE_RANK
PEER_HEADS = 8
PEER_NKEYS = 128
PEER_EXPERTS = PEER_NKEYS * PEER_NKEYS
PEER_QDIM = 256
PEER_TOPK = 16
PEER_BLOCK = 128
LN_EPS = 1e-5
DEEPNORM_ALPHA = (2.0 * DEPTH) ** 0.25
DEEPNORM_BETA = (8.0 * DEPTH) ** -0.25

kernel_name = "hymba_gla_conformer_peer_deepnorm"

def layer_norm(x, g, b=None):
    xf = x.astype(jnp.float32)
    mu = jnp.mean(xf, axis=-1, keepdims=True)
    var = jnp.mean(jnp.square(xf - mu), axis=-1, keepdims=True)
    out = (xf - mu) * lax.rsqrt(var + LN_EPS) * g.astype(jnp.float32)
    if b is not None:
        out = out + b.astype(jnp.float32)
    return out

def gla_chunked(q, k, v, log_a):
    B, L = q.shape[0], q.shape[1]
    C = GLA_CHUNK
    N = L // C

    def to_chunks(t):
        return t.reshape(B, N, C, GLA_HEADS, t.shape[-1]).transpose(0, 3, 1, 2, 4)

    q, k, v, log_a = to_chunks(q), to_chunks(k), to_chunks(v), to_chunks(log_a)
    q = q * (GLA_DK ** -0.5)
    b = jnp.cumsum(log_a, axis=3)
    b_ref = b[:, :, :, C // 2:C // 2 + 1, :]
    b_last = b[:, :, :, C - 1:C, :]
    q_in = q * jnp.exp(b - b_ref)
    k_in = k * jnp.exp(b_ref - b)
    scores = jnp.einsum('bhnid,bhnjd->bhnij', q_in, k_in)
    causal = jnp.tril(jnp.ones((C, C), dtype=bool))
    scores = jnp.where(causal, scores, 0.0)
    o_intra = jnp.einsum('bhnij,bhnjv->bhniv', scores, v)
    kv = jnp.einsum('bhnjd,bhnjv->bhndv', k * jnp.exp(b_last - b), v)
    decay = jnp.exp(b_last[:, :, :, 0, :])

    def step(S, inp):
        d_n, kv_n = inp
        return d_n[..., None] * S + kv_n, S

    S0 = jnp.zeros((B, GLA_HEADS, GLA_DK, GLA_DV), jnp.float32)
    _, S_prev = lax.scan(step, S0, (decay.transpose(2, 0, 1, 3), kv.transpose(2, 0, 1, 3, 4)))
    o_inter = jnp.einsum('bhnid,nbhdv->bhniv', q * jnp.exp(b), S_prev)
    o = o_intra + o_inter
    return o.transpose(0, 2, 3, 1, 4).reshape(B, L, GLA_HEADS, GLA_DV)

def hybrid_mixer(x, w_in, w_a2, b_a, gla_norm_g, conv_w, conv_b, conv_ln_g, conv_ln_b, w_out):
    B, L, _ = x.shape
    f32 = jnp.float32
    proj = x @ w_in
    q, k, v, r, a_lr, c = jnp.split(proj, [SPLIT_Q, SPLIT_K, SPLIT_V, SPLIT_R, SPLIT_A], axis=-1)
    log_a = jax.nn.log_sigmoid((a_lr @ w_a2 + b_a).astype(f32)) / GLA_TAU
    o = gla_chunked(q.astype(f32).reshape(B, L, GLA_HEADS, GLA_DK),
                    k.astype(f32).reshape(B, L, GLA_HEADS, GLA_DK),
                    v.astype(f32).reshape(B, L, GLA_HEADS, GLA_DV),
                    log_a.reshape(B, L, GLA_HEADS, GLA_DK))
    o = layer_norm(o, gla_norm_g.reshape(GLA_HEADS, GLA_DV))
    gla_out = (o.reshape(B, L, GLA_VAL_WIDTH) * jax.nn.silu(r.astype(f32))).astype(x.dtype)
    c_val, c_gate = jnp.split(c, 2, axis=-1)
    c = c_val * jax.nn.sigmoid(c_gate)
    c = lax.conv_general_dilated(
        c, conv_w[:, None, :], window_strides=(1,), padding=[(CONV_KERNEL - 1, 0)],
        dimension_numbers=('NWC', 'WIO', 'NWC'), feature_group_count=CONV_WIDTH) + conv_b
    conv_out = jax.nn.silu(layer_norm(c, conv_ln_g, conv_ln_b)).astype(x.dtype)
    return jnp.concatenate([gla_out, conv_out], axis=-1) @ w_out

def peer(h, w_q, sub_k1, sub_k2, u_tab, v_tab):
    B, L, D = h.shape
    T = B * L
    half = PEER_QDIM // 2
    hf = h.reshape(T, D)
    q = (hf @ w_q).reshape(T, PEER_HEADS, PEER_QDIM)
    s1 = jnp.einsum('thd,hkd->thk', q[..., :half], sub_k1).astype(jnp.float32)
    s2 = jnp.einsum('thd,hkd->thk', q[..., half:], sub_k2).astype(jnp.float32)
    s1t, i1 = lax.top_k(s1, PEER_TOPK)
    s2t, i2 = lax.top_k(s2, PEER_TOPK)
    cand = (s1t[..., :, None] + s2t[..., None, :]).reshape(T, PEER_HEADS, PEER_TOPK * PEER_TOPK)
    cidx = (i1[..., :, None] * PEER_NKEYS + i2[..., None, :]).reshape(T, PEER_HEADS, PEER_TOPK * PEER_TOPK)
    sc, pos = lax.top_k(cand, PEER_TOPK)
    eidx = jnp.take_along_axis(cidx, pos, axis=-1)
    gates = jax.nn.softmax(sc, axis=-1)
    n_blk = T // PEER_BLOCK
    HK = PEER_HEADS * PEER_TOPK

    def block(args):
        xb, ib, gb = args
        u = jnp.take(u_tab, ib, axis=0)
        act = jax.nn.gelu(jnp.einsum('pd,pkd->pk', xb, u).astype(jnp.float32), approximate=False)
        w = (gb * act).astype(xb.dtype)
        vv = jnp.take(v_tab, ib, axis=0)
        return jnp.einsum('pk,pkd->pd', w, vv)

    out = lax.map(block, (hf.reshape(n_blk, PEER_BLOCK, D),
                          eidx.reshape(n_blk, PEER_BLOCK, HK),
                          gates.reshape(n_blk, PEER_BLOCK, HK)))
    return out.reshape(B, L, D)

def setup_inputs(seed: int = 0) -> dict:
    key = jax.random.key(seed)
    ks = jax.random.split(key, 20)

    def nrm(k, shape, scale):
        return jax.random.normal(k, shape, jnp.float32) * scale

    return {
        "x": nrm(ks[0], (BATCH, SEQ, D_MODEL), 1.0),
        "w_in": nrm(ks[1], (DEPTH, D_MODEL, IN_WIDTH), D_MODEL ** -0.5),
        "w_a2": nrm(ks[2], (DEPTH, GLA_GATE_RANK, GLA_KEY_WIDTH), GLA_GATE_RANK ** -0.5),
        "b_a": nrm(ks[3], (DEPTH, GLA_KEY_WIDTH), 0.1),
        "gla_norm_g": 1.0 + nrm(ks[4], (DEPTH, GLA_VAL_WIDTH), 0.02),
        "conv_w": nrm(ks[5], (DEPTH, CONV_KERNEL, CONV_WIDTH), CONV_KERNEL ** -0.5),
        "conv_b": nrm(ks[6], (DEPTH, CONV_WIDTH), 0.02),
        "conv_ln_g": 1.0 + nrm(ks[7], (DEPTH, CONV_WIDTH), 0.02),
        "conv_ln_b": nrm(ks[8], (DEPTH, CONV_WIDTH), 0.02),
        "w_out": nrm(ks[9], (DEPTH, MIX_WIDTH, D_MODEL), DEEPNORM_BETA * MIX_WIDTH ** -0.5),
        "ln1_g": 1.0 + nrm(ks[10], (DEPTH, D_MODEL), 0.02),
        "ln1_b": nrm(ks[11], (DEPTH, D_MODEL), 0.02),
        "w_q": nrm(ks[12], (DEPTH, D_MODEL, PEER_HEADS * PEER_QDIM), D_MODEL ** -0.5),
        "sub_k1": nrm(ks[13], (DEPTH, PEER_HEADS, PEER_NKEYS, PEER_QDIM // 2), (PEER_QDIM // 2) ** -0.5),
        "sub_k2": nrm(ks[14], (DEPTH, PEER_HEADS, PEER_NKEYS, PEER_QDIM // 2), (PEER_QDIM // 2) ** -0.5),
        "u_tab": nrm(ks[15], (DEPTH, PEER_EXPERTS, D_MODEL), D_MODEL ** -0.5),
        "v_tab": nrm(ks[16], (DEPTH, PEER_EXPERTS, D_MODEL), DEEPNORM_BETA),
        "ln2_g": 1.0 + nrm(ks[17], (DEPTH, D_MODEL), 0.02),
        "ln2_b": nrm(ks[18], (DEPTH, D_MODEL), 0.02),
    }

def reference(x, w_in, w_a2, b_a, gla_norm_g, conv_w, conv_b, conv_ln_g, conv_ln_b, w_out,
              ln1_g, ln1_b, w_q, sub_k1, sub_k2, u_tab, v_tab, ln2_g, ln2_b):
    for l in range(DEPTH):
        mix = hybrid_mixer(x, w_in[l], w_a2[l], b_a[l], gla_norm_g[l], conv_w[l], conv_b[l],
                           conv_ln_g[l], conv_ln_b[l], w_out[l])
        h = layer_norm(DEEPNORM_ALPHA * x + mix, ln1_g[l], ln1_b[l]).astype(x.dtype)
        ffn = peer(h, w_q[l], sub_k1[l], sub_k2[l], u_tab[l], v_tab[l])
        x = layer_norm(DEEPNORM_ALPHA * h + ffn, ln2_g[l], ln2_b[l]).astype(x.dtype)
    return x


_drawn_inputs = setup_inputs


def setup_inputs(seed=0):
    import zlib

    import numpy as np

    out = dict(_drawn_inputs(seed))
    spreads = {}
    factors = {'gla_norm_g': 3.402,
     'conv_ln_g': 2.992,
     'conv_ln_b': 3.311,
     'ln2_g': 2.824,
     'ln2_b': 2.842}
    for name, (base, spread) in spreads.items():
        noise = np.random.default_rng([zlib.crc32(name.encode()), seed]).standard_normal(out[name].shape)
        drawn = base * np.exp(spread * noise) if base else spread * noise
        out[name] = __import__('jax').numpy.asarray(drawn.astype(out[name].dtype))
    for name, factor in factors.items():
        out[name] = (out[name] * factor).astype(out[name].dtype)
    return out
```

```python
from contextlib import ExitStack

import numpy as np

import concourse.bass as bass
from concourse import mybir
from concourse.alu_op_type import AluOpType as ALU

F32 = mybir.dt.float32
F32R = mybir.dt.float32r
U32 = mybir.dt.uint32
I32 = mybir.dt.int32
ACT = mybir.ActivationFunctionType
AX = mybir.AxisListType

P = 128
T = 512
D = 2048
KT = D // P
TB = T // P
CHUNK = 1024
HALF = CHUNK // P
HEADS = 4
DV = 256
GC = 64
NGC = T // GC
TAPS = 31
CT = 8
PH = 8
NK = 128
TOPK = 16
NRAW = 4
NSPLIT = 2
GRP = 8
NGRP = NK // GRP
TILES_IN = 1 + 10 * HEADS
TILES_OUT = KT
TILES_Q = 2 * PH
C_IN = 2 * TILES_IN
C_OUT = 2 * TILES_OUT
C_Q = 2 * TILES_Q
C_HEAD = C_IN + C_OUT + C_Q
C_GRP = 4 * GRP
C_ALL = C_HEAD + NGRP * C_GRP
TG = 64
NTG = T // TG
EPS = 1e-5
ALPHA = 2.0 ** 0.25
TAU = 16.0
LOWEST = -3.0e38


def build(nc, stream, xT, w_a2, b_a, conv_w, vecs_conv, gla_g, ln_vecs, sub_k, out):
    es = ExitStack()
    with es:
        def sem(name):
            return es.enter_context(nc.semaphore(name))

        def sb(name, shape, dt=F32, ctx=es):
            return ctx.enter_context(nc.sbuf_tensor(name, shape, dt))

        xhi = sb("xhi", [P, KT, T], F32R)
        xlo = sb("xlo", [P, KT, T], F32R)
        raw = sb("raw", [P, NRAW, CHUNK])
        whi = sb("whi", [P, NSPLIT, CHUNK], F32R)
        wlo = sb("wlo", [P, NSPLIT, CHUNK], F32R)
        ident = sb("ident", [P, P])
        iota = sb("iota", [P, P])
        lnv = sb("lnv", [P, 4, KT])
        subk = sb("subk", [P, TILES_Q, NK])
        keyT = sb("keyT", [P, 3, T])
        mean_of = sb("mean_of", [P, 3, P])
        rstd = sb("rstd", [P, T])
        eps_col = sb("eps_col", [P, 1])

        front = ExitStack()
        def fb(name, shape, dt=F32):
            return sb(name, shape, dt, front)
        conv_out = fb("conv_out", [P, CT, T])
        gla_out = fb("gla_out", [P, 2 * HEADS, T])
        a_lr = fb("a_lr", [P, T])
        wa2 = fb("wa2", [16, HEADS * P])
        fvec = fb("fvec", [P, HEADS + 2 * HEADS + 3 * CT])
        cw = fb("cw", [P, CT, TAPS])
        reset = fb("reset", [P, T])
        causal = fb("causal", [P, TB, P])
        qT = fb("qT", [P, T])
        kT = fb("kT", [P, T])
        vT = fb("vT", [P, 2, T])
        vtok = fb("vtok", [P, TB, DV])
        t0 = fb("t0", [P, T])
        t1 = fb("t1", [P, T])
        bcum = fb("bcum", [P, T])
        d1 = fb("d1", [P, T])
        ex = fb("ex", [P, 4, T])
        dec = ex[:, 3, :]
        sT = fb("sT", [P, TB, P])
        ktok = fb("ktok", [P, TB, P])
        states = fb("states", [P, NGC - 1, DV])
        o_sb = fb("o_sb", [P, 2, T])
        rr = fb("rr", [P, 2, T])
        cpad = fb("cpad", [P, 2, TAPS - 1 + T])
        front.close()
        d2 = t0
        sg = kT
        srr = states[:, 0:4, :].rearrange("p a b -> p (a b)").rearrange("p (j t) -> p j t", j=2)
        osq = vT

        mid = ExitStack()
        pre = sb("pre", [P, KT, T], F32, mid)
        lsq = sb("lsq", [P, 2, T], F32, mid)
        hful = sb("hful", [P, 2, T], F32, mid)
        mid.close()

        ret = ExitStack()
        def rb(name, shape, dt=F32):
            return sb(name, shape, dt, ret)
        score = rb("score", [P, TILES_Q, TB, NK])
        qk = rb("qk", [P, 2, T])
        cut = rb("cut", [P, NK])
        cand = rb("cand", [P, TOPK * TOPK])
        cut2 = rb("cut2", [P, TOPK * TOPK])
        topv = rb("topv", [P, TB, TILES_Q, TOPK])
        topi = rb("topi", [P, TB, TILES_Q, TOPK], U32)
        topf = rb("topf", [P, TB, TILES_Q, TOPK])
        posi = rb("posi", [P, TB, PH * TOPK], U32)
        posx = rb("posx", [P, TB, PH * TOPK], U32)
        posf = rb("posf", [P, TB, PH * TOPK])
        best = rb("best", [P, TB, PH * TOPK])
        pick = rb("pick", [P, PH * TOPK, TOPK])
        keyf = rb("keyf", [P, 3, TB, PH * TOPK])
        gsum = rb("gsum", [P, TB * PH, 1])
        gexp = rb("gexp", [P, TB, PH * TOPK])
        ret.close()

        gat = ExitStack()
        gstage = sb("gstage", [P, 2, NK, TG], F32, gat)
        hotL = sb("hotL", [P, 2, 4, P], F32, gat)
        hotR = sb("hotR", [P, 2, 4, P], F32, gat)
        gat.close()

        pee = ExitStack()
        acc = sb("acc", [P, KT, T], F32, pee)
        shi = sb("shi", [P, GRP, T], F32R, pee)
        slo = sb("slo", [P, GRP, T], F32R, pee)
        gtile = sb("gtile", [P, 4, T], F32, pee)
        act_u = sb("act_u", [P, 2, T], F32, pee)
        s_f = sb("s_f", [P, 2, T], F32, pee)
        ysq = sb("ysq", [P, 2, T], F32, pee)
        pee.close()

        ps = es.enter_context(nc.psum_tensor("ps", [P, 8, T], F32))
        gates = nc.dram_tensor("gates", (NTG, P, NK, TG), F32, kind="Internal").ap()

        raw_landed = [sem(f"raw_landed{s}") for s in range(NRAW)]
        hi_made, lo_made = sem("hi_made"), sem("lo_made")
        split_begun = sem("split_begun")
        chunk_used = sem("chunk_used")
        tile_done = sem("tile_done")
        bank_read = [sem("bank_read0"), sem("bank_read1")]
        x_landed = [sem(f"x_landed{i}") for i in range(4)]
        small_landed = sem("small_landed")
        consts = sem("consts")
        x_hi, x_lo = sem("x_hi"), sem("x_lo")
        z_done, z_read = sem("z_done"), sem("z_read")
        a_sum, a_exp = sem("a_sum"), sem("a_exp")
        q_copied, v_copied = sem("q_copied"), sem("v_copied")
        vdec = sem("vdec")
        qk_scaled = sem("qk_scaled")
        v_turned, vtok_copied = sem("v_turned"), sem("vtok_copied")
        k_turned, ktok_copied = sem("k_turned"), sem("ktok_copied")
        scored, masked = sem("scored"), sem("masked")
        kv_done, states_made = sem("kv_done"), sem("states_made")
        o_done, o_copied = sem("o_done"), sem("o_copied")
        mean_done, centred = sem("mean_done"), sem("centred")
        squared, var_done = sem("squared"), sem("var_done")
        rooted, head_done = sem("rooted"), sem("head_done")
        gate_ready, c_ready = sem("gate_ready"), sem("c_ready")
        r_copied = sem("r_copied")
        act_step, dve_step = sem("act_step"), sem("dve_step")
        silu_parts = sem("silu_parts")
        mixf, mix_hi, mix_lo = sem("mixf"), sem("mix_hi"), sem("mix_lo")
        res_landed, pre_made = sem("res_landed"), sem("pre_made")
        h_full, h_hi, h_lo = sem("h_full"), sem("h_hi"), sem("h_lo")
        qk_copied, s_done, s_copied = sem("qk_copied"), sem("s_done"), sem("s_copied")
        act_turn = sem("act_turn")
        sc_sub, sc_exp = sem("sc_sub"), sem("sc_exp")
        keys_made, keys_turned, keys_copied = sem("keys_made"), sem("keys_turned"), sem("keys_copied")
        hots_made, g_done, g_copied = sem("hots_made"), sem("g_done"), sem("g_copied")
        gstored = [sem("gstored0"), sem("gstored1")]
        g_landed = [sem(f"g_landed{i}") for i in range(4)]
        acc_ready = sem("acc_ready")
        u_act, s_prod, s_hi, s_lo = sem("u_act"), sem("s_prod"), sem("s_hi"), sem("s_lo")
        part_done, part_read = sem("part_done"), sem("part_read")
        y_sum, y_store, y_out = sem("y_sum"), sem("y_store"), sem("y_out")
        out_stored = sem("out_stored")

        BA, GG, CB, CG, CBB = 0, HEADS, 3 * HEADS, 3 * HEADS + CT, 3 * HEADS + 2 * CT

        HQ, HK, HV0, HV1, HG0, HC0, HG1, HC1, HR0, HR1 = range(10)

        def kv_of(n):
            return ps[:, 2 + 2 * (n % 2) + n // 4, (n // 2 % 2) * DV:(n // 2 % 2 + 1) * DV]

        def tile_of(h, which):
            return 1 + 10 * h + which

        block = es.enter_context(nc.Block())

        @block.sync
        def _(sp):
            for i in range(4):
                half = conv_out if i < 2 else gla_out
                sp.dma_start(half[:, 4 * (i % 2):4 * (i % 2) + 4, :], xT[:, 4 * i:4 * i + 4, :]).then_inc(x_landed[i], 16)
            for c in range(NRAW):
                sp.dma_start(raw[:, c, :], stream[c]).then_inc(raw_landed[c], 16)
            body = stream[NRAW:NRAW + (C_HEAD - NRAW) // NRAW * NRAW].rearrange("(i s) p f -> i s p f", s=NRAW)
            with sp.Fori(0, (C_HEAD - NRAW) // NRAW) as i:
                for s in range(NRAW):
                    sp.wait_ge(lo_made, NRAW * i + s + 1)
                    sp.dma_start(raw[:, s, :], body[i, s]).then_inc(raw_landed[s], 16)
            done = NRAW + (C_HEAD - NRAW) // NRAW * NRAW
            for c in range(done, C_HEAD):
                sp.wait_ge(lo_made, c - NRAW + 1)
                sp.dma_start(raw[:, c % NRAW, :], stream[c]).then_inc(raw_landed[c % NRAW], 16)
            table = stream[C_HEAD:C_ALL].rearrange("(g h s) p f -> g h s p f", g=NGRP, s=2 * NRAW)
            gview = gates.rearrange("n p (g i e) t -> g i e p n t", g=NGRP, e=4)

            def load(g, i, s, gates_too):
                slot = (C_HEAD + s) % NRAW
                sp.wait_ge(lo_made, C_GRP * g + 2 * NRAW * i + (C_HEAD - NRAW + s + 1))
                sp.dma_start(raw[:, slot, :], table[g, i, s]).then_inc(raw_landed[slot], 16)
                if gates_too and s % 2 == 0:
                    e = s // 2
                    sp.wait_ge(s_prod, GRP * g + 4 * i + (e + 1))
                    sp.dma_start(gtile[:, e, :].rearrange("p (n t) -> p n t", t=TG), gview[g, i, e]).then_inc(g_landed[e], 16)

            for half in range(2):
                sp.wait_ge(gstored[half], 16 * NTG // 2)
            with sp.Fori(0, NGRP) as g:
                with sp.Fori(0, GRP // 4) as i:
                    for s in range(2 * NRAW):
                        load(g, i, s, True)
                with sp.Fori(GRP // 4, GRP // 2) as i:
                    for s in range(2 * NRAW):
                        load(g, i, s, False)
            for i in range(4):
                sp.wait_ge(y_out, 4 * i + 4)
                sp.dma_start(out[:, 4 * i:4 * i + 4, :], acc[:, 4 * i:4 * i + 4, :]).then_inc(out_stored, 16)
            sp.wait_ge(out_stored, 64)

        @block.gpsimd
        def _(pool):
            pool.memset(ident[:, :], 0.0)
            pool.memset(causal[:, :, :], 1.0)
            pool.memset(reset[:, :], 1.0)
            pool.memset(eps_col[:, :], EPS)
            pool.memset(mean_of[:, 0, :], 1.0 / DV)
            pool.memset(mean_of[:, 1, :], 1.0 / (CT * P))
            pool.memset(mean_of[:, 2, :], 1.0 / D)
            pool.iota(iota[:, :], pattern=[[1, P]], base=0, channel_multiplier=0,
                      allow_small_or_imprecise_dtypes=True).then_inc(consts, 1)
            pool.wait_ge(consts, 1)
            pool.affine_select(out=ident[:, :], in_=ident[:, :], compare_op=ALU.not_equal, fill=1.0, base=0,
                               pattern=[[-1, P]], channel_multiplier=1)
            pool.memset(reset[:, :].rearrange("p (n c) -> p n c", c=GC)[:, :, 0:1], 0.0)
            pool.affine_select(out=causal[:, :, :], in_=causal[:, :, :], compare_op=ALU.is_ge, fill=0.0,
                               base=0, pattern=[[0, TB], [1, P]], channel_multiplier=-1).then_inc(consts, 1)
            pool.wait_ge(consts, 2)
            pool.memset(causal[0:GC, :, GC:P], 0.0).then_inc(consts, 1)
            pool.wait_ge(consts, 3)

            def split(slot, k, landed, c1):
                pool.wait_ge(chunk_used, c1)
                pool.wait_ge(raw_landed[slot], landed)
                pool.sem_inc(split_begun, 1)
                pool.tensor_scalar(whi[:, k, :], raw[:, slot, :], 1.0, 0.0, ALU.mult, ALU.add).then_inc(hi_made, 1)
                pool.wait_ge(hi_made, c1)
                pool.sem_inc(split_begun, 1)
                pool.tensor_tensor(wlo[:, k, :], raw[:, slot, :], whi[:, k, :].bitcast(F32),
                                   ALU.subtract).then_inc(lo_made, 1)

            total = C_ALL
            with pool.Fori(0, total // NRAW) as i:
                for s in range(NRAW):
                    split(s, s % NSPLIT, 16 * i + 16, NRAW * i + s + 1)
            for c in range(total // NRAW * NRAW, total):
                split(c % NRAW, c % NSPLIT, 16 * (c // NRAW + 1), c + 1)

        @block.tensor
        def _(pe):
            pe.sem_inc(chunk_used, NSPLIT)

            def tile(c0, bank, wait_x=None):
                for half in range(2):
                    pe.wait_ge(lo_made, c0 + half + 1)
                    for j in range(HALF):
                        k = half * HALF + j
                        if wait_x:
                            pe.wait_ge(wait_x, k + 1)
                        w, wl = whi[:, half, j * P:(j + 1) * P], wlo[:, half, j * P:(j + 1) * P]
                        pe.matmul(ps[:, bank, :], w, xhi[:, k, :], start=(k == 0), stop=False)
                        pe.matmul(ps[:, bank, :], w, xlo[:, k, :], start=False, stop=False)
                        last = pe.matmul(ps[:, bank, :], wl, xhi[:, k, :], start=False, stop=(k == KT - 1))
                        if j == HALF - 1 and half == 0:
                            last.then_inc(chunk_used, 1)
                last.then_inc(chunk_used, 1)

            def tile_n(n, wait_x=None):
                if n >= 2:
                    pe.wait_ge(bank_read[n % 2], n // 2)
                tile(2 * n, n % 2, wait_x)

            pe.wait_ge(consts, 3)
            pe.wait_ge(small_landed, 16 * 7)
            tile_n(0, x_lo)
            for h in range(HEADS):
                if h == 0:
                    pe.wait_ge(a_exp, 1)
                if h >= 1:
                    pe.wait_ge(head_done, h)
                pe.matmul(ps[:, 7, :], wa2[:, h * P:(h + 1) * P], a_lr[0:16, :], start=True,
                          stop=True).then_inc(z_done, 1)
                for w in (HQ, HK, HV0, HV1):
                    tile_n(tile_of(h, w))
                pe.wait_ge(v_copied, h + 1)
                for j in range(2):
                    for b in range(TB):
                        last = pe.transpose(ps[:, 2 + j, b * P:(b + 1) * P], vT[:, j, b * P:(b + 1) * P], ident[:, :])
                last.then_inc(v_turned, 1)
                tile_n(tile_of(h, HG0))
                pe.wait_ge(qk_scaled, h + 1)
                for b in range(TB):
                    last = pe.transpose(ps[:, 4, b * P:(b + 1) * P], ex[:, 2, b * P:(b + 1) * P], ident[:, :])
                last.then_inc(k_turned, 1)
                for b in range(TB):
                    last = pe.matmul(ps[:, 5, b * P:(b + 1) * P], ex[:, 1, b * P:(b + 1) * P],
                                     ex[:, 0, b * P:(b + 1) * P], start=True, stop=True)
                last.then_inc(scored, 1)
                tile_n(tile_of(h, HC0))
                pe.wait_ge(vtok_copied, h + 1)
                pe.wait_ge(ktok_copied, h + 1)
                pe.wait_ge(masked, h + 1)
                for n in range(NGC - 1):
                    r = slice((n % 2) * GC, (n % 2) * GC + GC)
                    last = pe.matmul(kv_of(n), ktok[r, n // 2, :],
                                     vtok[r, n // 2, :], start=True, stop=True)
                last.then_inc(kv_done, 1)
                tile_n(tile_of(h, HG1))
                pe.wait_ge(states_made, h + 1)
                for j in range(2):
                    for b in range(TB):
                        pe.matmul(ps[:, 6 + j, b * P:(b + 1) * P], vtok[:, b, j * P:(j + 1) * P],
                                  sT[:, b, :], start=True, stop=False)
                        for n in (2 * b, 2 * b + 1):
                            if n == 0:
                                continue
                            last = pe.matmul(ps[:, 6 + j, n * GC:(n + 1) * GC], states[:, n - 1, j * P:(j + 1) * P],
                                             ex[:, 3, n * GC:(n + 1) * GC], start=False, stop=(n % 2 == 1))
                last.then_inc(o_done, 1)
                tile_n(tile_of(h, HC1))
                pe.wait_ge(o_copied, h + 1)
                for j in range(2):
                    last = pe.matmul(ps[:, 2, :], mean_of[:, 0, :], o_sb[:, j, :], start=(j == 0), stop=(j == 1))
                last.then_inc(mean_done, 1)
                tile_n(tile_of(h, HR0))
                pe.wait_ge(squared, h + 1)
                for j in range(2):
                    last = pe.matmul(ps[:, 3, :], mean_of[:, 0, :], osq[:, j, :], start=(j == 0), stop=(j == 1))
                last.then_inc(var_done, 1)
                tile_n(tile_of(h, HR1))

            def column_mean(src, n, which, bank, made, made0, done, used=None):
                for k in range(n):
                    pe.wait_ge(made, made0 + k + 1)
                    last = pe.matmul(ps[:, bank, :], mean_of[:, which, :], src(k), start=(k == 0), stop=(k == n - 1))
                    if used is not None and k < n - 1:
                        last.then_inc(used, 1)
                last.then_inc(done, 1)

            pe.wait_ge(head_done, HEADS)
            column_mean(lambda k: conv_out[:, k, :], CT, 1, 2, vdec, 0, mean_done)
            for k in range(CT):
                pe.wait_ge(squared, HEADS + k + 1)
                last = pe.matmul(ps[:, 3, :], mean_of[:, 1, :], vT[:, k % 2, :], start=(k == 0), stop=(k == CT - 1))
                last.then_inc(v_turned, 1)
            last = None
            for m in range(TILES_OUT):
                tile_n(TILES_IN + m, mix_lo if m == 0 else None)
            column_mean(lambda k: pre[:, k, :], KT, 2, 2, pre_made, 0, mean_done)
            for k in range(KT):
                pe.wait_ge(squared, HEADS + CT + k + 1)
                pe.matmul(ps[:, 3, :], mean_of[:, 2, :], lsq[:, k % 2, :], start=(k == 0),
                          stop=(k == KT - 1)).then_inc(v_turned, 1)
            def key_scores(m):
                pe.wait_ge(qk_copied, m + 1)
                if m >= 2:
                    pe.wait_ge(s_copied, m - 1)
                for b in range(TB):
                    last = pe.matmul(ps[:, 2 + m % 2, b * P:(b + 1) * P], qk[:, m % 2, b * P:(b + 1) * P],
                                     subk[:, m, :], start=True, stop=True)
                last.then_inc(s_done, 1)

            for m in range(TILES_Q):
                tile_n(TILES_IN + TILES_OUT + m, h_lo if m == 0 else None)
                if m >= 1:
                    key_scores(m - 1)
            key_scores(TILES_Q - 1)
            pe.wait_ge(keys_made, 1)
            for i in range(3):
                for b in range(TB):
                    last = pe.transpose(ps[:, 4 + i, b * P:(b + 1) * P], keyf[:, i, b, :], ident[:, :])
            last.then_inc(keys_turned, 1)
            pe.wait_ge(keys_copied, 1)
            pe.sem_inc(g_done, 2)
            with pe.Fori(0, T // 8) as i:
                for s in range(2):
                    pe.wait_ge(hots_made, 2 * i + (s + 1))
                    pe.wait_ge(g_copied, 2 * i + (s + 1))
                    for q in range(4):
                        last = pe.matmul(ps[:, 4 + s, q * P:(q + 1) * P], hotL[:, s, q, :], hotR[:, s, q, :],
                                         start=True, stop=True)
                    last.then_inc(g_done, 1)
            with pe.Fori(0, NGRP) as g:
                with pe.Fori(0, GRP // 2) as i:
                    for e in range(2):
                        pe.wait_ge(u_act, GRP * g + 2 * i + (e + 1))
                        tile(C_GRP * g + 4 * i + (C_HEAD + 2 * e), e)
                with pe.Fori(0, GRP // 2) as i:
                    for j in range(2):
                        pe.wait_ge(part_read, GRP * g + 2 * i + (j + 1))
                        for q in range(2):
                            pe.wait_ge(lo_made, C_GRP * g + 4 * i + (C_HEAD + 2 * GRP + 2 * j + q + 1))
                            for ee in range(4):
                                e = 4 * q + ee
                                pe.wait_ge(s_lo, GRP * g + (e + 1))
                                for d in range(2):
                                    cols = slice((2 * ee + d) * P, (2 * ee + d + 1) * P)
                                    o = ps[:, 2 + 2 * j + d, :]
                                    pe.matmul(o, whi[:, q, cols], shi[:, e, :], start=(e == 0), stop=False)
                                    pe.matmul(o, whi[:, q, cols], slo[:, e, :], start=False, stop=False)
                                    last = pe.matmul(o, wlo[:, q, cols], shi[:, e, :], start=False, stop=(e == GRP - 1))
                            last.then_inc(chunk_used, 1)
            pe.wait_ge(y_sum, 1)
            for k in range(KT):
                last = pe.matmul(ps[:, 6, :], mean_of[:, 2, :], acc[:, k, :], start=(k == 0), stop=(k == KT - 1))
            last.then_inc(mean_done, 1)
            for k in range(KT):
                pe.wait_ge(squared, HEADS + CT + KT + k + 1)
                pe.matmul(ps[:, 7, :], mean_of[:, 2, :], ysq[:, k % 2, :], start=(k == 0),
                          stop=(k == KT - 1)).then_inc(v_turned, 1)

        @block.scalar
        def _(act):
            steps = [0]

            def step(ins):
                steps[0] += 1
                ins.then_inc(act_step, 1)
                act.wait_ge(act_step, steps[0])

            act.dma_start(wa2[:, :], w_a2).then_inc(small_landed, 16)
            act.dma_start(fvec[:, 0:HEADS], b_a).then_inc(small_landed, 16)
            act.dma_start(fvec[:, GG:CB], gla_g).then_inc(small_landed, 16)
            act.dma_start(fvec[:, CB:CB + 3 * CT], vecs_conv).then_inc(small_landed, 16)
            act.dma_start(cw[:, :, :], conv_w).then_inc(small_landed, 16)
            act.dma_start(lnv[:, :, :], ln_vecs).then_inc(small_landed, 16)
            act.dma_start(subk[:, :, :], sub_k).then_inc(small_landed, 16)
            act.wait_ge(small_landed, 16 * 7)

            def evacuate(n, out_ap, func=ACT.Copy, **kw):
                act.wait_ge(chunk_used, NSPLIT + 2 * n + 2)
                return act.activation(out_ap, ps[:, n % 2, :], func, **kw)

            for i in range(KT):
                act.wait_ge(x_landed[i // 4], 16)
                src = conv_out[:, i, :] if i < CT else gla_out[:, i - CT, :]
                act.activation(xhi[:, i, :], src, ACT.Copy).then_inc(x_hi, 1)
            evacuate(0, a_lr[:, :]).then_inc(bank_read[0], 1)
            act.wait_ge(bank_read[0], 1)
            act.sem_inc(a_exp, 1)
            for h in range(HEADS):
                def n_of(w):
                    return tile_of(h, w)
                act.wait_ge(z_done, h + 1)
                step(act.activation(t0[:, :], ps[:, 7, :], ACT.Identity, bias=fvec[:, BA + h:BA + h + 1]))
                step(act.activation(t1[:, :], t0[:, :], ACT.Abs))
                step(act.activation(t1[:, :], t1[:, :], ACT.Exp, scale=-1.0))
                act.activation(t1[:, :], t1[:, :], ACT.Ln, bias=1.0).then_inc(z_read, 1)
                act.wait_ge(a_sum, 2 * h + 1)
                act.activation(ex[:, 0, :], d1[:, :], ACT.Exp, scale=1.0 / TAU)
                act.activation(ex[:, 1, :], d1[:, :], ACT.Exp, scale=-1.0 / TAU)
                act.activation(ex[:, 3, :], bcum[:, :], ACT.Exp, scale=1.0 / TAU)
                act.wait_ge(a_sum, 2 * h + 2)
                act.activation(ex[:, 2, :], d2[:, :], ACT.Exp, scale=-1.0 / TAU).then_inc(a_exp, 1)
                evacuate(n_of(HQ), qT[:, :], scale=float(P) ** -0.5).then_inc(bank_read[n_of(HQ) % 2], 1)
                evacuate(n_of(HK), kT[:, :]).then_inc(bank_read[n_of(HK) % 2], 1)
                evacuate(n_of(HV0), vT[:, 0, :]).then_inc(bank_read[n_of(HV0) % 2], 1)
                evacuate(n_of(HV1), vT[:, 1, :]).then_inc(bank_read[n_of(HV1) % 2], 1)
                act.wait_ge(bank_read[n_of(HV1) % 2], (n_of(HV1)) // 2 + 1)
                act.wait_ge(bank_read[n_of(HV0) % 2], (n_of(HV0)) // 2 + 1)
                act.sem_inc(v_copied, 1)
                act.wait_ge(v_turned, h + 1)
                for j in range(2):
                    last = act.activation(vtok[:, :, j * P:(j + 1) * P],
                                          ps[:, 2 + j, :].rearrange("p (b v) -> p b v", v=P), ACT.Copy)
                last.then_inc(vtok_copied, 1)
                act.wait_ge(qk_scaled, h + 1)
                evacuate(n_of(HG0), sg[:, :], ACT.Sigmoid).then_inc(bank_read[n_of(HG0) % 2], 1)
                act.wait_ge(k_turned, h + 1)
                act.activation(ktok[:, :, :], ps[:, 4, :].rearrange("p (b k) -> p b k", k=P), ACT.Copy).then_inc(ktok_copied, 1)
                act.wait_ge(c_ready, 2 * h + 1)
                evacuate(n_of(HG1), sg[:, :], ACT.Sigmoid).then_inc(bank_read[n_of(HG1) % 2], 1)
                act.wait_ge(o_done, h + 1)
                act.activation(o_sb[:, :, :], ps[:, 6:8, :], ACT.Copy).then_inc(o_copied, 1)
                act.wait_ge(centred, h + 1)
                act.activation(osq[:, :, :], o_sb[:, :, :], ACT.Square).then_inc(squared, 1)
                for j in range(2):
                    evacuate(n_of(HR0 + j), srr[:, j, :], ACT.Sigmoid)
                    act.activation(rr[:, j, :], ps[:, n_of(HR0 + j) % 2, :], ACT.Copy).then_inc(bank_read[n_of(HR0 + j) % 2], 1)
                    if j == 0:
                        act.wait_ge(var_done, h + 1)
                        act.activation(rstd[:, :], ps[:, 3, :], ACT.Sqrt, bias=eps_col[:, 0:1]).then_inc(rooted, 1)
                act.wait_ge(bank_read[n_of(HR0) % 2], n_of(HR0) // 2 + 1)
                act.wait_ge(bank_read[n_of(HR1) % 2], n_of(HR1) // 2 + 1)
                act.sem_inc(r_copied, 1)
                act.wait_ge(head_done, h + 1)

            for k in range(CT):
                act.wait_ge(centred, HEADS + k + 1)
                if k >= 2:
                    act.wait_ge(v_turned, HEADS + k - 1)
                act.activation(vT[:, k % 2, :], conv_out[:, k, :], ACT.Square).then_inc(squared, 1)
            act.wait_ge(v_turned, HEADS + CT)
            act.activation(rstd[:, :], ps[:, 3, :], ACT.Sqrt, bias=eps_col[:, 0:1]).then_inc(rooted, 1)
            for k in range(CT):
                act.wait_ge(silu_parts, k + 1)
                if k >= 2:
                    act.wait_ge(mixf, k - 1)
                act.activation(rr[:, k % 2, :], conv_out[:, k, :], ACT.Identity, scale=fvec[:, CG + k:CG + k + 1],
                               bias=fvec[:, CBB + k:CBB + k + 1]).then_inc(r_copied, 1)
                act.activation(srr[:, k % 2, :], conv_out[:, k, :], ACT.Sigmoid, scale=fvec[:, CG + k:CG + k + 1],
                               bias=fvec[:, CBB + k:CBB + k + 1]).then_inc(r_copied, 1)
            for k in range(KT):
                if k >= CT:
                    act.wait_ge(mixf, k - CT + 1)
                src = gla_out[:, k, :] if k < CT else conv_out[:, k - CT, :]
                act.activation(xhi[:, k, :], src, ACT.Copy).then_inc(mix_hi, 1)
            act.wait_ge(mix_lo, KT)
            act.dma_start(pre[:, :, :], xT).then_inc(res_landed, 16)
            for k in range(KT):
                act.wait_ge(centred, HEADS + CT + k + 1)
                if k >= 2:
                    act.wait_ge(v_turned, HEADS + CT + k - 1)
                act.activation(lsq[:, k % 2, :], pre[:, k, :], ACT.Square).then_inc(squared, 1)
            act.wait_ge(v_turned, HEADS + CT + KT)
            act.activation(rstd[:, :], ps[:, 3, :], ACT.Sqrt, bias=eps_col[:, 0:1]).then_inc(rooted, 1)
            for k in range(KT):
                act.wait_ge(silu_parts, CT + k + 1)
                if k >= 2:
                    act.wait_ge(h_lo, k - 1)
                act.activation(hful[:, k % 2, :], pre[:, k, :], ACT.Identity, bias=lnv[:, 1, k:k + 1]).then_inc(h_full, 1)
                act.wait_ge(h_full, k + 1)
                act.activation(xhi[:, k, :], hful[:, k % 2, :], ACT.Copy).then_inc(h_hi, 1)
            def copy_scores(m):
                act.wait_ge(s_done, m + 1)
                act.activation(score[:, m, :, :], ps[:, 2 + m % 2, :].rearrange("p (b k) -> p b k", k=NK),
                               ACT.Copy).then_inc(s_copied, 1)

            for m in range(TILES_Q):
                n = TILES_IN + TILES_OUT + m
                if m == 0:
                    act.wait_ge(h_lo, KT)
                if m >= 2:
                    act.wait_ge(s_done, m - 1)
                evacuate(n, qk[:, m % 2, :]).then_inc(bank_read[n % 2], 1)
                act.wait_ge(bank_read[n % 2], n // 2 + 1)
                act.sem_inc(qk_copied, 1)
                if m >= 1:
                    copy_scores(m - 1)
            copy_scores(TILES_Q - 1)
            act.wait_ge(sc_sub, 1)
            act.activation(gexp[:, :, :], best[:, :, :], ACT.Exp).then_inc(sc_exp, 1)
            act.wait_ge(keys_turned, 1)
            act.activation(keyT[:, :, :], ps[:, 4:7, :], ACT.Copy).then_inc(keys_copied, 1)
            act.wait_ge(keys_copied, 1)
            act.sem_inc(g_copied, 2)

            def gate_stage(n, half):
                with act.Fori(0, TG // 8) as i:
                    for s in range(2):
                        act.wait_ge(g_done, 2 * i + TG // 4 * n + (s + 3))
                        act.sem_inc(act_turn, 1)
                        act.activation(gstage[:, half, :, :].rearrange("p k (i s q) -> p k i s q", s=2, q=4)[:, :, i, s, :],
                                       ps[:, 4 + s, :].rearrange("p (q k) -> p k q", q=4), ACT.Copy).then_inc(g_copied, 1)

            for n in range(NTG):
                half = n % 2
                if n >= 2:
                    act.wait_ge(gstored[half], 16 * (n // 2))
                gate_stage(n, half)
                act.wait_ge(g_copied, TG // 4 * (n + 1) + 2)
                act.dma_start(gates[n], gstage[:, half, :, :]).then_inc(gstored[half], 16)
            for half in range(2):
                act.wait_ge(gstored[half], 16 * NTG // 2)
            act.wait_ge(acc_ready, 1)
            act.sem_inc(u_act, 2)
            with act.Fori(0, NGRP) as g:
                for e in range(GRP):
                    act.wait_ge(chunk_used, C_GRP * g + (NSPLIT + C_HEAD + 2 * e + 2))
                    act.wait_ge(s_prod, GRP * g + (e + 3))
                    act.sem_inc(act_turn, 1)
                    act.activation(act_u[:, e % 2, :], ps[:, e % 2, :], ACT.Gelu).then_inc(u_act, 1)
                    act.wait_ge(s_prod, GRP * g + (e + 5))
                    act.sem_inc(act_turn, 1)
                    act.activation(shi[:, e, :], s_f[:, e % 2, :], ACT.Copy).then_inc(s_hi, 1)
            for k in range(KT):
                act.wait_ge(centred, HEADS + CT + KT + k + 1)
                if k >= 2:
                    act.wait_ge(v_turned, HEADS + CT + KT + k - 1)
                act.activation(ysq[:, k % 2, :], acc[:, k, :], ACT.Square).then_inc(squared, 1)
            act.wait_ge(v_turned, HEADS + CT + 2 * KT)
            act.activation(rstd[:, :], ps[:, 7, :], ACT.Sqrt, bias=eps_col[:, 0:1]).then_inc(rooted, 1)
            for k in range(KT):
                act.wait_ge(y_sum, k + 2)
                act.activation(acc[:, k, :], acc[:, k, :], ACT.Identity, bias=lnv[:, 3, k:k + 1]).then_inc(y_out, 1)

        @block.vector
        def _(dve):
            steps = [0]

            def step(ins):
                steps[0] += 1
                ins.then_inc(dve_step, 1)
                dve.wait_ge(dve_step, steps[0])

            for i in range(KT):
                dve.wait_ge(x_hi, i + 1)
                src = conv_out[:, i, :] if i < CT else gla_out[:, i - CT, :]
                dve.tensor_tensor(xlo[:, i, :], src, xhi[:, i, :].bitcast(F32), ALU.subtract).then_inc(x_lo, 1)
            dve.wait_ge(x_lo, KT)
            dve.wait_ge(small_landed, 16 * 7)
            dve.wait_ge(consts, 3)
            dve.memset(cpad[:, :, 0:TAPS - 1], 0.0)
            step(dve.memset(sT[:, :, :], 0.0))

            def chunks(a):
                return a.rearrange("p (n c) -> p n c", c=GC)

            def conv(m, j):
                acc_c = conv_out[:, m, :]
                step(dve.tensor_scalar(acc_c, cpad[:, j, 0:T], cw[:, m, 0:1], fvec[:, CB + m:CB + m + 1],
                                       ALU.mult, ALU.add))
                for k in range(1, TAPS):
                    ins = dve.scalar_tensor_tensor(out=acc_c, in0=cpad[:, j, k:k + T], scalar=cw[:, m, k:k + 1],
                                                   in1=acc_c, op0=ALU.mult, op1=ALU.add)
                    if k < TAPS - 1:
                        step(ins)
                ins.then_inc(vdec, 1)
                dve.wait_ge(vdec, m + 1)

            for h in range(HEADS):
                def n_of(w):
                    return tile_of(h, w)
                dve.wait_ge(z_read, h + 1)
                step(dve.scalar_tensor_tensor(out=t1[:, :], in0=t0[:, :], scalar=0.0, in1=t1[:, :],
                                              op0=ALU.min, op1=ALU.subtract))
                step(dve.tensor_tensor_scan(bcum[:, :], reset[:, :], t1[:, :], 0.0, ALU.mult, ALU.add))
                b3 = chunks(bcum[:, :])
                dve.tensor_tensor(chunks(d1[:, :]), b3, b3[:, :, GC // 2:GC // 2 + 1].to_broadcast([P, NGC, GC]),
                                  ALU.subtract).then_inc(a_sum, 1)
                dve.tensor_tensor(chunks(d2[:, :]), b3, b3[:, :, GC - 1:GC].to_broadcast([P, NGC, GC]),
                                  ALU.subtract).then_inc(a_sum, 1)
                dve.wait_ge(a_exp, h + 2)
                dve.wait_ge(bank_read[n_of(HQ) % 2], n_of(HQ) // 2 + 1)
                dve.wait_ge(bank_read[n_of(HK) % 2], n_of(HK) // 2 + 1)
                step(dve.tensor_copy(d1[:, 0:NGC], chunks(ex[:, 3, :])[:, :, GC - 1]))
                for i, src in ((0, qT), (1, kT), (2, kT), (3, qT)):
                    last = dve.tensor_tensor(ex[:, i, :], ex[:, i, :], src[:, :], ALU.mult)
                last.then_inc(qk_scaled, 1)
                dve.wait_ge(scored, h + 1)
                dve.copy_predicated(sT[:, :, :], causal[:, :, :].bitcast(U32),
                                    ps[:, 5, :].rearrange("p (b q) -> p b q", q=P)).then_inc(masked, 1)
                def gated(j, w):
                    dve.wait_ge(chunk_used, NSPLIT + 2 * n_of(w) + 2)
                    dve.wait_ge(bank_read[n_of(w - 1) % 2], n_of(w - 1) // 2 + 1)
                    dve.tensor_tensor(cpad[:, j, TAPS - 1:], ps[:, n_of(w) % 2, :], sg[:, :],
                                      ALU.mult).then_inc(bank_read[n_of(w) % 2], 1)
                    dve.wait_ge(bank_read[n_of(w) % 2], n_of(w) // 2 + 1)
                    dve.sem_inc(c_ready, 1)
                gated(0, HC0)
                dve.wait_ge(kv_done, h + 1)
                for n in range(NGC - 1):
                    kv = kv_of(n)
                    if n == 0:
                        step(dve.tensor_copy(states[:, 0, :], kv))
                    else:
                        ins = dve.scalar_tensor_tensor(out=states[:, n, :], in0=states[:, n - 1, :],
                                                       scalar=d1[:, n:n + 1], in1=kv, op0=ALU.mult, op1=ALU.add)
                        if n < NGC - 2:
                            step(ins)
                ins.then_inc(states_made, 1)
                conv(2 * h, 0)
                gated(1, HC1)
                dve.wait_ge(mean_done, h + 1)
                dve.wait_ge(o_copied, h + 1)
                for j in range(2):
                    last = dve.tensor_tensor(o_sb[:, j, :], o_sb[:, j, :], ps[:, 2, :], ALU.subtract)
                last.then_inc(centred, 1)
                conv(2 * h + 1, 1)
                dve.wait_ge(rooted, h + 1)
                step(dve.reciprocal(rstd[:, :], rstd[:, :]))
                dve.wait_ge(centred, h + 1)
                for j in range(2):
                    last = dve.scalar_tensor_tensor(out=o_sb[:, j, :], in0=o_sb[:, j, :],
                                                    scalar=fvec[:, GG + 2 * h + j:GG + 2 * h + j + 1],
                                                    in1=rstd[:, :], op0=ALU.mult, op1=ALU.mult)
                step(last)
                dve.wait_ge(r_copied, h + 1)
                step(dve.tensor_tensor(rr[:, :, :], rr[:, :, :], srr[:, :, :], ALU.mult))
                dve.tensor_tensor(gla_out[:, 2 * h:2 * h + 2, :], o_sb[:, :, :], rr[:, :, :],
                                  ALU.mult).then_inc(head_done, 1)

            def centre(buf, k, done0, count):
                dve.tensor_tensor(buf[:, k, :], buf[:, k, :], ps[:, 2, :], ALU.subtract).then_inc(centred, 1)

            dve.wait_ge(mean_done, HEADS + 1)
            for k in range(CT):
                centre(conv_out, k, 0, 0)
            dve.wait_ge(rooted, HEADS + 1)
            step(dve.reciprocal(rstd[:, :], rstd[:, :]))
            for k in range(CT):
                dve.wait_ge(squared, HEADS + k + 1)
                dve.tensor_tensor(conv_out[:, k, :], conv_out[:, k, :], rstd[:, :], ALU.mult).then_inc(silu_parts, 1)
            dve.wait_ge(head_done, HEADS)
            for k in range(CT):
                dve.wait_ge(r_copied, HEADS + 2 * k + 2)
                dve.tensor_tensor(conv_out[:, k, :], rr[:, k % 2, :], srr[:, k % 2, :], ALU.mult).then_inc(mixf, 1)
            for k in range(KT):
                dve.wait_ge(mix_hi, k + 1)
                src = gla_out[:, k, :] if k < CT else conv_out[:, k - CT, :]
                dve.tensor_tensor(xlo[:, k, :], src, xhi[:, k, :].bitcast(F32), ALU.subtract).then_inc(mix_lo, 1)
            dve.wait_ge(res_landed, 16)
            for m in range(TILES_OUT):
                n = TILES_IN + m
                dve.wait_ge(chunk_used, NSPLIT + 2 * n + 2)
                dve.scalar_tensor_tensor(out=pre[:, m, :], in0=pre[:, m, :], scalar=ALPHA, in1=ps[:, n % 2, :],
                                         op0=ALU.mult, op1=ALU.add).then_inc(bank_read[n % 2], 1)
                dve.wait_ge(bank_read[n % 2], n // 2 + 1)
                dve.sem_inc(pre_made, 1)
            dve.wait_ge(mean_done, HEADS + 2)
            for k in range(KT):
                centre(pre, k, 0, 0)
            dve.wait_ge(rooted, HEADS + 2)
            step(dve.reciprocal(rstd[:, :], rstd[:, :]))
            for k in range(KT):
                dve.wait_ge(squared, HEADS + CT + k + 1)
                dve.scalar_tensor_tensor(out=pre[:, k, :], in0=pre[:, k, :], scalar=lnv[:, 0, k:k + 1],
                                         in1=rstd[:, :], op0=ALU.mult, op1=ALU.mult).then_inc(silu_parts, 1)
            for k in range(KT):
                dve.wait_ge(h_hi, k + 1)
                dve.tensor_tensor(xlo[:, k, :], hful[:, k % 2, :], xhi[:, k, :].bitcast(F32),
                                  ALU.subtract).then_inc(h_lo, 1)

            def top16(src, spare, vals, idx):
                step(dve.max(vals[:, 0:8], src))
                dve.max_index(idx[:, 0:8], vals[:, 0:8], src)
                step(dve.match_replace(spare, vals[:, 0:8], src, LOWEST))
                step(dve.max(vals[:, 8:16], spare))
                step(dve.max_index(idx[:, 8:16], vals[:, 8:16], spare))

            dve.wait_ge(h_lo, KT)
            for m in range(TILES_Q):
                dve.wait_ge(s_copied, m + 1)
                for b in range(TB):
                    top16(score[:, m, b, :], cut[:, :], topv[:, b, m, :], topi[:, b, m, :])
                if m % 2 == 0:
                    continue
                h = m // 2
                for b in range(TB):
                    step(dve.tensor_tensor(cand[:, :].rearrange("p (i j) -> p i j", j=TOPK),
                                           topv[:, b, m - 1, :].unsqueeze(2).to_broadcast([P, TOPK, TOPK]),
                                           topv[:, b, m, :].unsqueeze(1).to_broadcast([P, TOPK, TOPK]), ALU.add))
                    r = slice(h * TOPK, (h + 1) * TOPK)
                    top16(cand[:, :], cut2[:, :], best[:, b, r], posi[:, b, r])
            step(dve.tensor_copy(topf[:, :, :, :], topi[:, :, :, :]))
            for half in range(2):
                if half == 0:
                    step(dve.tensor_single_scalar(posx[:, :, :], posi[:, :, :], 4, ALU.logical_shift_right))
                else:
                    step(dve.tensor_single_scalar(posx[:, :, :], posi[:, :, :], TOPK - 1, ALU.bitwise_and))
                step(dve.tensor_copy(posf[:, :, :], posx[:, :, :]))
                for b in range(TB):
                    step(dve.tensor_tensor(pick[:, :, :], posf[:, b, :].unsqueeze(2).to_broadcast([P, PH * TOPK, TOPK]),
                                           iota[:, 0:TOPK].unsqueeze(1).to_broadcast([P, PH * TOPK, TOPK]), ALU.is_equal))
                    p4 = pick[:, :, :].rearrange("p (h k) j -> p h k j", k=TOPK)
                    keys = topf[:, b, :, :].rearrange("p (h two) j -> p h two j", two=2)[:, :, half, :]
                    step(dve.tensor_tensor(p4, p4, keys.unsqueeze(2).to_broadcast([P, PH, TOPK, TOPK]), ALU.mult))
                    step(dve.tensor_reduce(keyf[:, half, b, :], pick[:, :, :], AX.X, ALU.add))
            b3 = best[:, :, :].rearrange("p b (h k) -> p (b h) k", k=TOPK)
            step(dve.tensor_copy(gsum[:, :, :], b3[:, :, 0:1]))
            dve.tensor_tensor(b3, b3, gsum[:, :, :].to_broadcast([P, TB * PH, TOPK]), ALU.subtract).then_inc(sc_sub, 1)
            dve.wait_ge(sc_exp, 1)
            e3 = gexp[:, :, :].rearrange("p b (h k) -> p (b h) k", k=TOPK)
            step(dve.tensor_reduce(gsum[:, :, 0], e3, AX.X, ALU.add))
            step(dve.reciprocal(gsum[:, :, 0], gsum[:, :, 0]))
            dve.tensor_tensor(keyf[:, 2, :, :].rearrange("p b (h k) -> p (b h) k", k=TOPK), e3,
                              gsum[:, :, :].to_broadcast([P, TB * PH, TOPK]), ALU.mult).then_inc(keys_made, 1)
            dve.wait_ge(keys_copied, 1)
            kv4 = keyT[:, :, :].rearrange("p c (i s q) -> p c i s q", s=2, q=4)
            with dve.Fori(0, T // 8) as i:
                for s in range(2):
                    dve.wait_ge(g_done, 2 * i + (s + 1))
                    for q in range(4):
                        dve.tensor_scalar(hotL[:, s, q, :], iota[:, :], kv4[:, 0, i, s, q:q + 1],
                                          kv4[:, 2, i, s, q:q + 1], ALU.is_equal, ALU.mult)
                        last = dve.tensor_scalar(hotR[:, s, q, :], iota[:, :], kv4[:, 1, i, s, q:q + 1], None, ALU.is_equal)
                    last.then_inc(hots_made, 1)
            for half in range(2):
                dve.wait_ge(gstored[half], 16 * NTG // 2)
            for k in range(KT):
                dve.tensor_scalar(acc[:, k, :], xhi[:, k, :].bitcast(F32), ALPHA, None, ALU.mult)
            last = None
            for k in range(KT):
                if k == 0:
                    step(dve.memset(act_u[:, :, :], 0.0))
                last = dve.scalar_tensor_tensor(out=acc[:, k, :], in0=xlo[:, k, :].bitcast(F32), scalar=ALPHA,
                                                in1=acc[:, k, :], op0=ALU.mult, op1=ALU.add)
            last.then_inc(acc_ready, 1)
            dve.wait_ge(acc_ready, 1)
            dve.sem_inc(s_prod, 4)
            dve.sem_inc(part_read, 2)
            with dve.Fori(0, NGRP) as g:
                for e in range(GRP):
                    dve.wait_ge(u_act, GRP * g + (e + 3))
                    dve.wait_ge(g_landed[e % 4], 32 * g + 16 * (e // 4 + 1))
                    dve.tensor_tensor(s_f[:, e % 2, :], act_u[:, e % 2, :], gtile[:, e % 4, :], ALU.mult).then_inc(s_prod, 1)
                    dve.wait_ge(s_hi, GRP * g + (e + 1))
                    dve.tensor_tensor(slo[:, e, :], s_f[:, e % 2, :], shi[:, e, :].bitcast(F32), ALU.subtract).then_inc(s_lo, 1)
                for j in range(GRP):
                    dve.wait_ge(chunk_used, C_GRP * g + (NSPLIT + C_HEAD + 2 * GRP + 2 * j + 2))
                    dve.tensor_tensor(acc[:, 2 * j:2 * j + 2, :], acc[:, 2 * j:2 * j + 2, :],
                                      ps[:, 2 + 2 * (j % 2):4 + 2 * (j % 2), :], ALU.add).then_inc(part_read, 1)
            dve.wait_ge(part_read, NGRP * GRP + 2)
            dve.sem_inc(y_sum, 1)
            dve.wait_ge(mean_done, HEADS + 3)
            for k in range(KT):
                dve.tensor_tensor(acc[:, k, :], acc[:, k, :], ps[:, 6, :], ALU.subtract).then_inc(centred, 1)
            dve.wait_ge(rooted, HEADS + 3)
            step(dve.reciprocal(rstd[:, :], rstd[:, :]))
            for k in range(KT):
                dve.wait_ge(squared, HEADS + CT + KT + k + 1)
                dve.scalar_tensor_tensor(out=acc[:, k, :], in0=acc[:, k, :], scalar=lnv[:, 2, k:k + 1],
                                         in1=rstd[:, :], op0=ALU.mult, op1=ALU.mult).then_inc(y_sum, 1)


def pack(w):
    m = w.shape[1] // P
    return w.reshape(2, HALF, P, m, P).transpose(3, 0, 2, 1, 4).reshape(2 * m, P, CHUNK)


def pack_tables(u, v):
    u = u.reshape(NK, NGRP, GRP, 2, HALF, P).transpose(1, 2, 3, 5, 4, 0).reshape(NGRP, 2 * GRP, P, CHUNK)
    v = v.reshape(NK, NGRP, 2, 4, KT // 2, 2 * P).transpose(1, 4, 2, 0, 3, 5).reshape(NGRP, KT, P, CHUNK)
    return np.concatenate([u, v], axis=1).reshape(NGRP * C_GRP, P, CHUNK)


def columns(v):
    return v.reshape(-1, P).T


def mixer_order(w_in):
    q, k, v, r, a, c_val, c_gate = np.split(w_in, [512, 1024, 2048, 3072, 3088, 4112], axis=1)
    tiles = [a, np.zeros((D, P - a.shape[1]), w_in.dtype)]
    for h in range(HEADS):
        tiles += [q[:, h * P:(h + 1) * P], k[:, h * P:(h + 1) * P], v[:, h * DV:(h + 1) * DV]]
        for m in (2 * h, 2 * h + 1):
            tiles += [c_gate[:, m * P:(m + 1) * P], c_val[:, m * P:(m + 1) * P]]
        tiles.append(r[:, h * DV:(h + 1) * DV])
    return np.concatenate(tiles, axis=1)


def kernel(x, w_in, w_a2, b_a, gla_norm_g, conv_w, conv_b, conv_ln_g, conv_ln_b, w_out,
           ln1_g, ln1_b, w_q, sub_k1, sub_k2, u_tab, v_tab, ln2_g, ln2_b):
    import concourse.bacc as bacc
    from concourse.bass_utils import run_bass_kernel_spmd

    a = {k: np.asarray(v)[0] for k, v in dict(
        x=x, w_in=w_in, w_a2=w_a2, b_a=b_a, gla_norm_g=gla_norm_g, conv_w=conv_w, conv_b=conv_b,
        conv_ln_g=conv_ln_g, conv_ln_b=conv_ln_b, w_out=w_out, ln1_g=ln1_g, ln1_b=ln1_b, w_q=w_q,
        sub_k1=sub_k1, sub_k2=sub_k2, u_tab=u_tab, v_tab=v_tab, ln2_g=ln2_g, ln2_b=ln2_b).items()}
    data = {
        "stream": np.concatenate([pack(mixer_order(a["w_in"])), pack(a["w_out"]), pack(a["w_q"]),
                                  pack_tables(a["u_tab"], a["v_tab"])]),
        "xT": a["x"].T.reshape(KT, P, T).transpose(1, 0, 2),
        "w_a2": a["w_a2"],
        "b_a": columns(a["b_a"]),
        "conv_w": a["conv_w"].T.reshape(CT, P, TAPS).transpose(1, 0, 2),
        "vecs_conv": np.concatenate([columns(a[k]) for k in ("conv_b", "conv_ln_g", "conv_ln_b")], axis=1),
        "gla_g": columns(a["gla_norm_g"]),
        "ln_vecs": np.stack([columns(a[k]) for k in ("ln1_g", "ln1_b", "ln2_g", "ln2_b")], axis=1),
        "sub_k": np.stack([a["sub_k1"], a["sub_k2"]], axis=1).reshape(2 * PH, NK, P).transpose(2, 0, 1),
    }
    nc = bacc.Bacc("TRN2", target_bir_lowering=False, num_devices=1)
    data = {k: np.ascontiguousarray(v) for k, v in data.items()}
    args = [nc.dram_tensor(k, v.shape, mybir.dt.from_np(v.dtype), kind="ExternalInput").ap()
            for k, v in data.items()]
    out = nc.dram_tensor("out", (P, KT, T), F32, kind="ExternalOutput").ap()
    build(nc, *args, out)
    r = run_bass_kernel_spmd(nc, [data], core_ids=[0])
    y = r.results[0]["out"]
    return np.ascontiguousarray(y.transpose(1, 0, 2).reshape(D, T).T).reshape(1, T, D)
```

```python
from contextlib import ExitStack

import numpy as np

import concourse.bass as bass
from concourse import mybir
from concourse.alu_op_type import AluOpType as ALU

F32 = mybir.dt.float32
F32R = mybir.dt.float32r
U32 = mybir.dt.uint32
I32 = mybir.dt.int32
ACT = mybir.ActivationFunctionType
AX = mybir.AxisListType

P = 128
T = 512
D = 2048
KT = D // P
TB = T // P
CHUNK = 1024
HALF = CHUNK // P
HEADS = 4
DV = 256
GC = 64
NGC = T // GC
TAPS = 31
CT = 8
PH = 8
NK = 128
TOPK = 16
NRAW = 4
NSPLIT = 2
GRP = 4
PARTS = KT // 2
NGRP = NK // GRP
TILES_IN = 1 + 10 * HEADS
TILES_OUT = KT
TILES_Q = 2 * PH
C_IN = 2 * TILES_IN
C_OUT = 2 * TILES_OUT
C_Q = 2 * TILES_Q
C_HEAD = C_IN + C_OUT + C_Q
C_GRP = 2 * GRP + PARTS
TD = 448
TR = T - TD
FOLD = P // TR
RANKS = PH * TOPK // FOLD
NTG = 8
TG = TD // NTG
QB = 4
BATCHES = (3, 2, 2, 3, 2, 2)
EARLY_FREE = 8
EARLY_TAIL = 8
EARLY = EARLY_FREE + NTG * len(BATCHES) // 2 + EARLY_TAIL
EGRP = EARLY // GRP
C_EARLY = C_HEAD
C_LATE = C_EARLY + 2 * EARLY
C_MAIN = C_LATE + EGRP * PARTS
ROWS_GRP = 8
PAIRS_G = RANKS // (2 * ROWS_GRP)
PAIRS = (NGRP - EGRP) // 2
C_ALL = C_MAIN + (NGRP - EGRP) * C_GRP
EPS = 1e-5
ALPHA = 2.0 ** 0.25
TAU = 16.0
LOWEST = -3.0e38


def build(nc, stream, xT, w_a2, b_a, conv_w, vecs_conv, gla_g, ln_vecs, sub_k, u_rows, v_rows, out):
    es = ExitStack()
    with es:
        def sem(name):
            return es.enter_context(nc.semaphore(name))

        def sb(name, shape, dt=F32, ctx=es):
            return ctx.enter_context(nc.sbuf_tensor(name, shape, dt))

        xhi = sb("xhi", [P, KT, T], F32R)
        xlo = sb("xlo", [P, KT, T], F32R)
        raw = sb("raw", [P, NRAW, CHUNK])
        whi = sb("whi", [P, NSPLIT, CHUNK], F32R)
        wlo = sb("wlo", [P, NSPLIT, CHUNK], F32R)
        ident = sb("ident", [P, P])
        iota = sb("iota", [P, P])
        lnv = sb("lnv", [P, 4, KT])
        mean_of = sb("mean_of", [P, 3, P])
        rstd = sb("rstd", [P, T])
        eps_col = sb("eps_col", [P, 1])

        kept = ExitStack()
        conv_out = sb("conv_out", [P, CT, T], F32, kept)
        fvec = sb("fvec", [P, HEADS + 2 * HEADS + 3 * CT], F32, kept)
        vT = sb("vT", [P, 2, T], F32, kept)
        states = sb("states", [P, NGC - 1, DV], F32, kept)
        rr = sb("rr", [P, 2, T], F32, kept)
        front = ExitStack()
        def fb(name, shape, dt=F32):
            return sb(name, shape, dt, front)
        gla_out = fb("gla_out", [P, 2 * HEADS, T])
        a_lr = fb("a_lr", [P, T])
        wa2 = fb("wa2", [16, HEADS * P])
        cw = fb("cw", [P, CT, TAPS])
        reset = fb("reset", [P, T])
        causal = fb("causal", [P, TB, P])
        qT = fb("qT", [P, T])
        kT = fb("kT", [P, T])
        vtok = fb("vtok", [P, TB, DV])
        t0 = fb("t0", [P, T])
        t1 = fb("t1", [P, T])
        bcum = fb("bcum", [P, T])
        d1 = fb("d1", [P, T])
        ex = fb("ex", [P, 4, T])
        sT = fb("sT", [P, TB, P])
        ktok = fb("ktok", [P, TB, P])
        o_sb = fb("o_sb", [P, 2, T])
        cpad = fb("cpad", [P, 2, TAPS - 1 + T])
        front.close()
        d2 = t0
        sg = kT
        srr = states[:, 0:4, :].rearrange("p a b -> p (a b)").rearrange("p (j t) -> p j t", j=2)
        osq = vT

        mid = ExitStack()
        pre = sb("pre", [P, KT, T], F32, mid)
        presum = sb("presum", [P, T], F32, mid)
        lsq = sb("lsq", [P, 2, T], F32, mid)
        hful = sb("hful", [P, 2, T], F32, mid)
        mid.close()
        kept.close()

        act_u = sb("act_u", [P, 2, TD])
        keyT = sb("keyT", [P, 3, T])

        chosen = sb("chosen", [P, 2, PH * TOPK])
        row_f = sb("row_f", [P, 2, RANKS])
        row_idx = sb("row_idx", [P, RANKS], U32)
        row_dot = sb("row_dot", [P, RANKS])
        dot_buf = sb("dot_buf", [P, ROWS_GRP])
        row_col = sb("row_col", [P, 2], U32)
        fold = sb("fold", [P, TR])

        ret = ExitStack()
        def rb(name, shape, dt=F32):
            return sb(name, shape, dt, ret)
        subk = rb("subk", [P, TILES_Q, NK])
        score = rb("score", [P, TILES_Q, TB, NK])
        qk = rb("qk", [P, 2, T])
        cut = rb("cut", [P, NK])
        cand = rb("cand", [P, TOPK * TOPK])
        cut2 = rb("cut2", [P, TOPK * TOPK])
        topv = rb("topv", [P, TB, TILES_Q, TOPK])
        topi = rb("topi", [P, TB, TILES_Q, TOPK], U32)
        topf = rb("topf", [P, TB, TILES_Q, TOPK])
        posi = rb("posi", [P, TB, PH * TOPK], U32)
        posx = rb("posx", [P, TB, PH * TOPK], U32)
        posf = rb("posf", [P, TB, PH * TOPK])
        best = rb("best", [P, TB, PH * TOPK])
        pick = rb("pick", [P, PH * TOPK, TOPK])
        keyf = rb("keyf", [P, 3, TB, PH * TOPK])
        gsum = rb("gsum", [P, TB * PH, 1])
        gexp = rb("gexp", [P, TB, PH * TOPK])
        ret.close()

        gat = ExitStack()
        gstage = sb("gstage", [P, 2, NK, TG], F32, gat)
        hotL = sb("hotL", [P, 4, QB, P], F32, gat)
        hotR = sb("hotR", [P, 4, QB, P], F32, gat)
        gat.close()

        pee = ExitStack()
        acc = sb("acc", [P, KT, T], F32, pee)
        shi = sb("shi", [P, 2, GRP, TD], F32R, pee)
        slo = sb("slo", [P, 2, GRP, TD], F32R, pee)
        gtile = sb("gtile", [P, 4, TD], F32, pee)
        s_f = sb("s_f", [P, 2, TD], F32, pee)
        tok = sb("tok", [P, D], F32, pee)
        rows = sb("rows", [P, 2, D], F32, pee)
        atile = rows[:, 1, 0:GRP * TD].rearrange("p (e t) -> p e t", e=GRP)
        h_twice = rows[:, 0, :].rearrange("p (k f t) -> p k f t", k=KT, f=FOLD)
        ysq = rows[:, 0, 0:2 * T].rearrange("p (j t) -> p j t", j=2)
        pee.close()

        ps = es.enter_context(nc.psum_tensor("ps", [P, 8, T], F32))
        gates = nc.dram_tensor("gates", (NTG, P, NK, TG), F32, kind="Internal").ap()
        early_acts = nc.dram_tensor("early_acts", (EARLY, P, TD), F32, kind="Internal").ap()

        raw_landed = [sem(f"raw_landed{s}") for s in range(NRAW)]
        hi_made, lo_made = sem("hi_made"), sem("lo_made")
        split_begun = sem("split_begun")
        chunk_used = sem("chunk_used")
        bank_read = [sem("bank_read0"), sem("bank_read1")]
        x_landed = [sem(f"x_landed{i}") for i in range(KT // 2)]
        small_landed, subk_landed = sem("small_landed"), sem("subk_landed")
        consts = sem("consts")
        x_hi, x_lo = sem("x_hi"), sem("x_lo")
        z_done, z_read = sem("z_done"), sem("z_read")
        a_sum, a_exp = sem("a_sum"), sem("a_exp")
        q_copied, v_copied = sem("q_copied"), sem("v_copied")
        vdec = sem("vdec")
        qk_scaled = sem("qk_scaled")
        v_turned, vtok_copied = sem("v_turned"), sem("vtok_copied")
        k_turned, ktok_copied = sem("k_turned"), sem("ktok_copied")
        scored, masked = sem("scored"), sem("masked")
        kv_done, states_made = sem("kv_done"), sem("states_made")
        o_done, o_copied = sem("o_done"), sem("o_copied")
        mean_done, centred = sem("mean_done"), sem("centred")
        squared, var_done = sem("squared"), sem("var_done")
        rooted, head_done = sem("rooted"), sem("head_done")
        gate_ready, c_ready = sem("gate_ready"), sem("c_ready")
        r_copied = sem("r_copied")
        act_step, dve_step = sem("act_step"), sem("dve_step")
        silu_parts = sem("silu_parts")
        mixf, mix_hi, mix_lo = sem("mixf"), sem("mix_hi"), sem("mix_lo")
        res_landed, pre_made = sem("res_landed"), sem("pre_made")
        h_full, h_hi, h_lo = sem("h_full"), sem("h_hi"), sem("h_lo")
        qk_copied, s_done, s_copied = sem("qk_copied"), sem("s_done"), sem("s_copied")
        act_turn = sem("act_turn")
        sc_sub, sc_exp = sem("sc_sub"), sem("sc_exp")
        keys_made, keys_turned, keys_copied = sem("keys_made"), sem("keys_turned"), sem("keys_copied")
        hots_made, g_done, g_copied = sem("hots_made"), sem("g_done"), sem("g_copied")
        gstored = [sem("gstored0"), sem("gstored1")]
        g_landed = [sem(f"g_landed{i}") for i in range(4)]
        a_landed = [sem(f"a_landed{i}") for i in range(4)]
        acts_stored = [sem("acts_stored0"), sem("acts_stored1")]
        acc_ready = sem("acc_ready")
        u_act, s_prod, s_hi, s_lo = sem("u_act"), sem("s_prod"), sem("s_hi"), sem("s_lo")
        part_done, part_read = sem("part_done"), sem("part_read")
        y_sum, y_out = sem("y_sum"), sem("y_out")
        chosen_made, row_f_landed = sem("chosen_made"), sem("row_f_landed")
        h_twice_made, tok_turned, tok_copied = sem("h_twice_made"), sem("tok_turned"), sem("tok_copied")
        rows_ready = sem("rows_ready")
        col_made, rows_used = sem("col_made"), sem("rows_used")
        rows_landed = [sem("rows_landed0"), sem("rows_landed1")]
        dots_kept, dots_gelu, tok_summed, tok_folded = sem("dots_kept"), sem("dots_gelu"), sem("tok_summed"), sem("tok_folded")
        out_stored = sem("out_stored")

        BA, GG, CB, CG, CBB = 0, HEADS, 3 * HEADS, 3 * HEADS + CT, 3 * HEADS + 2 * CT

        HQ, HK, HV0, HV1, HG0, HC0, HG1, HC1, HR0, HR1 = range(10)

        def kv_of(n):
            return ps[:, 2 + 2 * (n % 2) + n // 4, (n // 2 % 2) * DV:(n // 2 % 2 + 1) * DV]

        def used_by(n):
            if n < TILES_IN:
                return NSPLIT + 2 * n + 2
            if n < TILES_IN + 2 * TILES_OUT:
                return NSPLIT + C_IN + (n - TILES_IN) + 1
            return NSPLIT + C_IN + C_OUT + 2 * (n - TILES_IN - 2 * TILES_OUT) + 2

        def tile_of(h, which):
            return 1 + 10 * h + which

        block = es.enter_context(nc.Block())

        @block.sync
        def _(sp):
            for c in range(2):
                sp.dma_start(raw[:, c, :], stream[c]).then_inc(raw_landed[c], 16)
            for i in range(KT // 2):
                half = conv_out if i < KT // 4 else gla_out
                sp.dma_start(half[:, 2 * i % CT:2 * i % CT + 2, :], xT[:, 2 * i:2 * i + 2, :]).then_inc(x_landed[i], 16)
            for c in range(2, NRAW):
                sp.dma_start(raw[:, c, :], stream[c]).then_inc(raw_landed[c], 16)
            body = stream[NRAW:NRAW + (C_HEAD - NRAW) // NRAW * NRAW].rearrange("(i s) p f -> i s p f", s=NRAW)
            with sp.Fori(0, (C_HEAD - NRAW) // NRAW) as i:
                for s in range(NRAW):
                    sp.wait_ge(lo_made, NRAW * i + s + 1)
                    sp.dma_start(raw[:, s, :], body[i, s]).then_inc(raw_landed[s], 16)
            done = NRAW + (C_HEAD - NRAW) // NRAW * NRAW
            for c in range(done, C_HEAD):
                sp.wait_ge(lo_made, c - NRAW + 1)
                sp.dma_start(raw[:, c % NRAW, :], stream[c]).then_inc(raw_landed[c % NRAW], 16)
            gview = gates.rearrange("n p (g e) t -> g e p n t", e=GRP)
            aview = early_acts.rearrange("(g e) p t -> g e p t", e=GRP)

            def load(src, c, s):
                slot = (C_HEAD + s) % NRAW
                sp.wait_ge(lo_made, c - (NRAW - 1))
                sp.dma_start(raw[:, slot, :], src).then_inc(raw_landed[slot], 16)

            def load_gates(g, e):
                sp.wait_ge(s_prod, GRP * g + (e + 1))
                sp.dma_start(gtile[:, e, :].rearrange("p (n t) -> p n t", t=TG), gview[g, e]).then_inc(g_landed[e], 16)

            def load_early(g):
                for e in range(GRP):
                    load_gates(g, e)
                    sp.dma_start(atile[:, e, :], aview[g, e]).then_inc(a_landed[e], 16)

            early = stream[C_EARLY:C_LATE].rearrange("(i s) p f -> i s p f", s=NRAW)
            with sp.Fori(0, 2 * EARLY // NRAW) as i:
                for s in range(NRAW):
                    load(early[i, s], NRAW * i + (C_EARLY + s), s)
            for half in range(2):
                sp.wait_ge(gstored[half], 16 * NTG // 2)
                sp.wait_ge(acts_stored[half], 16 * (EARLY - EARLY_TAIL) // 2)
            load_early(0)
            for half in range(2):
                sp.wait_ge(acts_stored[half], 16 * EARLY // 2)
            late = stream[C_LATE:C_MAIN].rearrange("(g s) p f -> g s p f", g=EGRP)
            with sp.Fori(0, EGRP - 1) as g:
                load_early(g + 1)
                for s in range(PARTS):
                    load(late[g, s], PARTS * g + (C_LATE + s), s)
            for s in range(PARTS):
                load(late[EGRP - 1, s], PARTS * (EGRP - 1) + C_LATE + s, s)
            main = stream[C_MAIN:C_ALL].rearrange("(g s) p f -> g s p f", g=NGRP - EGRP)
            with sp.Fori(0, NGRP - EGRP) as g:
                for s in range(C_GRP):
                    load(main[g, s], C_GRP * g + (C_MAIN + s), s)
                    if s % 2 == 0 and s < 2 * GRP:
                        load_gates(g + EGRP, s // 2)
            for i in range(4):
                sp.wait_ge(y_out, 4 * i + 4)
                sp.dma_start(out[:, 4 * i:4 * i + 4, :], acc[:, 4 * i:4 * i + 4, :]).then_inc(out_stored, 16)
            sp.wait_ge(out_stored, 64)

        @block.gpsimd
        def _(pool):
            pool.memset(ident[:, :], 0.0)
            pool.memset(causal[:, :, :], 1.0)
            pool.memset(reset[:, :], 1.0)
            pool.memset(eps_col[:, :], EPS)
            pool.memset(mean_of[:, 0, :], 1.0 / DV)
            pool.memset(mean_of[:, 1, :], 1.0 / (CT * P))
            pool.memset(mean_of[:, 2, :], 1.0 / D)
            pool.iota(iota[:, :], pattern=[[1, P]], base=0, channel_multiplier=0,
                      allow_small_or_imprecise_dtypes=True).then_inc(consts, 1)
            pool.wait_ge(consts, 1)
            pool.affine_select(out=ident[:, :], in_=ident[:, :], compare_op=ALU.not_equal, fill=1.0, base=0,
                               pattern=[[-1, P]], channel_multiplier=1)
            pool.memset(reset[:, :].rearrange("p (n c) -> p n c", c=GC)[:, :, 0:1], 0.0)
            pool.affine_select(out=causal[:, :, :], in_=causal[:, :, :], compare_op=ALU.is_ge, fill=0.0,
                               base=0, pattern=[[0, TB], [1, P]], channel_multiplier=-1).then_inc(consts, 1)
            pool.wait_ge(consts, 2)
            pool.memset(causal[0:GC, :, GC:P], 0.0).then_inc(consts, 1)
            pool.wait_ge(consts, 3)

            def split(slot, k, landed, c1):
                pool.wait_ge(chunk_used, c1)
                pool.wait_ge(raw_landed[slot], landed)
                pool.sem_inc(split_begun, 1)
                pool.tensor_scalar(whi[:, k, :], raw[:, slot, :], 1.0, 0.0, ALU.mult, ALU.add).then_inc(hi_made, 1)
                pool.wait_ge(hi_made, c1)
                pool.sem_inc(split_begun, 1)
                pool.tensor_tensor(wlo[:, k, :], raw[:, slot, :], whi[:, k, :].bitcast(F32),
                                   ALU.subtract).then_inc(lo_made, 1)

            def gather(table, n, s, idx):
                pool.wait_ge(rows_used, n + 1)
                pool.sem_inc(split_begun, 1)
                pool.tensor_copy(row_col[:, s:s + 1], idx).then_inc(col_made, 1)
                pool.wait_ge(col_made, n + 1)
                pool.sem_inc(split_begun, 1)
                pool.indirect_dma_start(rows[:, s, :], None, table,
                                        bass.IndirectOffsetOnAxis(ap=row_col[:, s:s + 1], axis=0)).then_inc(rows_landed[s], 16)

            with pool.Fori(0, C_MAIN // NRAW) as i:
                for s in range(NRAW):
                    split(s, s % NSPLIT, 16 * i + 16, NRAW * i + s + 1)
            for c in range(C_MAIN // NRAW * NRAW, C_MAIN):
                split(c % NRAW, c % NSPLIT, 16 * (c // NRAW + 1), c + 1)
            pool.wait_ge(rows_ready, 1)
            numbers = row_idx[:, :].rearrange("p (i s) -> p i s", s=2)
            per = 2 * C_GRP * PAIRS_G // NRAW
            for t, table in enumerate((u_rows, v_rows)):
                with pool.Fori(0, per) as i:
                    for s in range(NRAW):
                        c = C_MAIN + t * 2 * C_GRP * PAIRS_G + s
                        split(c % NRAW, c % NSPLIT, 16 * i + 16 * (c // NRAW + 1), NRAW * i + c + 1)
                        if s % 2 == 1:
                            gather(table, 2 * i + (t * RANKS + s // 2), s // 2, numbers[:, i, s // 2:s // 2 + 1])
            with pool.Fori(0, 2 * C_GRP * (PAIRS - 2 * PAIRS_G) // NRAW) as i:
                for s in range(NRAW):
                    c = C_MAIN + 4 * C_GRP * PAIRS_G + s
                    split(c % NRAW, c % NSPLIT, 16 * i + 16 * (c // NRAW + 1), NRAW * i + c + 1)

        @block.tensor
        def _(pe):
            pe.sem_inc(chunk_used, NSPLIT)

            def tile(c0, bank, wait_x=None, between=None, tokens=T):
                o, hi, lo = ps[:, bank, 0:tokens], xhi[:, :, 0:tokens], xlo[:, :, 0:tokens]
                for half in range(2):
                    if between and half == 1:
                        between()
                    pe.wait_ge(lo_made, c0 + half + 1)
                    for j in range(HALF):
                        k = half * HALF + j
                        if wait_x:
                            pe.wait_ge(wait_x, k + 1)
                        w, wl = whi[:, half, j * P:(j + 1) * P], wlo[:, half, j * P:(j + 1) * P]
                        pe.matmul(o, w, hi[:, k, :], start=(k == 0), stop=False)
                        pe.matmul(o, w, lo[:, k, :], start=False, stop=False)
                        last = pe.matmul(o, wl, hi[:, k, :], start=False, stop=(k == KT - 1))
                        if j == HALF - 1 and half == 0:
                            last.then_inc(chunk_used, 1)
                last.then_inc(chunk_used, 1)

            def tile_n(n, wait_x=None):
                if n >= 2:
                    pe.wait_ge(bank_read[n % 2], n // 2)
                tile(used_by(n) - NSPLIT - 2, n % 2, wait_x)

            pe.wait_ge(consts, 3)
            pe.wait_ge(small_landed, 16 * 6)
            tile_n(0, x_lo)
            for h in range(HEADS):
                if h == 0:
                    pe.wait_ge(a_exp, 1)
                if h >= 1:
                    pe.wait_ge(o_copied, h)
                pe.matmul(ps[:, 7, :], wa2[:, h * P:(h + 1) * P], a_lr[0:16, :], start=True,
                          stop=True).then_inc(z_done, 1)
                for w in (HQ, HK, HV0, HV1):
                    tile_n(tile_of(h, w))
                if h >= 1:
                    pe.wait_ge(rooted, h)
                pe.wait_ge(v_copied, h + 1)
                for j in range(2):
                    for b in range(TB):
                        last = pe.transpose(ps[:, 2 + j, b * P:(b + 1) * P], vT[:, j, b * P:(b + 1) * P], ident[:, :])
                last.then_inc(v_turned, 1)
                tile_n(tile_of(h, HG0))
                pe.wait_ge(qk_scaled, h + 1)
                for b in range(TB):
                    last = pe.transpose(ps[:, 4, b * P:(b + 1) * P], ex[:, 2, b * P:(b + 1) * P], ident[:, :])
                last.then_inc(k_turned, 1)
                for b in range(TB):
                    last = pe.matmul(ps[:, 5, b * P:(b + 1) * P], ex[:, 1, b * P:(b + 1) * P],
                                     ex[:, 0, b * P:(b + 1) * P], start=True, stop=True)
                last.then_inc(scored, 1)
                tile_n(tile_of(h, HC0))
                pe.wait_ge(vtok_copied, h + 1)
                pe.wait_ge(ktok_copied, h + 1)
                pe.wait_ge(masked, h + 1)
                for n in range(NGC - 1):
                    r = slice((n % 2) * GC, (n % 2) * GC + GC)
                    last = pe.matmul(kv_of(n), ktok[r, n // 2, :],
                                     vtok[r, n // 2, :], start=True, stop=True)
                last.then_inc(kv_done, 1)
                tile_n(tile_of(h, HG1))
                pe.wait_ge(states_made, h + 1)
                for j in range(2):
                    for b in range(TB):
                        pe.matmul(ps[:, 6 + j, b * P:(b + 1) * P], vtok[:, b, j * P:(j + 1) * P],
                                  sT[:, b, :], start=True, stop=False)
                        for n in (2 * b, 2 * b + 1):
                            if n == 0:
                                continue
                            last = pe.matmul(ps[:, 6 + j, n * GC:(n + 1) * GC], states[:, n - 1, j * P:(j + 1) * P],
                                             ex[:, 3, n * GC:(n + 1) * GC], start=False, stop=(n % 2 == 1))
                last.then_inc(o_done, 1)
                tile_n(tile_of(h, HC1))
                pe.wait_ge(o_copied, h + 1)
                for j in range(2):
                    last = pe.matmul(ps[:, 2, :], mean_of[:, 0, :], o_sb[:, j, :], start=(j == 0), stop=(j == 1))
                last.then_inc(mean_done, 1)
                tile_n(tile_of(h, HR0))
                pe.wait_ge(squared, h + 1)
                for j in range(2):
                    last = pe.matmul(ps[:, 3, :], mean_of[:, 0, :], osq[:, j, :], start=(j == 0), stop=(j == 1))
                last.then_inc(var_done, 1)
                tile_n(tile_of(h, HR1))

            def column_mean(src, n, which, bank, made, made0, done, used=None):
                for k in range(n):
                    pe.wait_ge(made, made0 + k + 1)
                    last = pe.matmul(ps[:, bank, :], mean_of[:, which, :], src(k), start=(k == 0), stop=(k == n - 1))
                    if used is not None and k < n - 1:
                        last.then_inc(used, 1)
                last.then_inc(done, 1)

            def out_half(hm):
                n, c0 = TILES_IN + hm, C_IN + hm
                pe.wait_ge(bank_read[n % 2], n // 2)
                pe.wait_ge(lo_made, c0 + 1)
                for j in range(HALF):
                    k = hm // TILES_OUT * HALF + j
                    if hm % TILES_OUT == 0:
                        pe.wait_ge(mix_lo, k + 1)
                    w, wl = whi[:, c0 % NSPLIT, j * P:(j + 1) * P], wlo[:, c0 % NSPLIT, j * P:(j + 1) * P]
                    pe.matmul(ps[:, n % 2, :], w, xhi[:, k, :], start=(j == 0), stop=False)
                    pe.matmul(ps[:, n % 2, :], w, xlo[:, k, :], start=False, stop=False)
                    last = pe.matmul(ps[:, n % 2, :], wl, xhi[:, k, :], start=False, stop=(j == HALF - 1))
                last.then_inc(chunk_used, 1)

            for hm in range(0, 6):
                out_half(hm)
            for k in range(CT):
                pe.wait_ge(vdec, k + 1)
                last = pe.matmul(ps[:, 2, :], mean_of[:, 1, :], conv_out[:, k, :], start=(k == 0), stop=(k == CT - 1))
            last.then_inc(mean_done, 1)
            for hm in range(6, 9):
                out_half(hm)
            for k in range(CT):
                pe.wait_ge(squared, HEADS + k + 1)
                pe.matmul(ps[:, 3, :], mean_of[:, 1, :], vT[:, k % 2, :], start=(k == 0),
                          stop=(k == CT - 1)).then_inc(v_turned, 1)
            for hm in range(9, 2 * TILES_OUT):
                out_half(hm)
            pe.wait_ge(pre_made, 1)
            pe.matmul(ps[:, 2, :], mean_of[:, 2, :], presum[:, :], start=True, stop=True).then_inc(mean_done, 1)
            for k in range(KT):
                pe.wait_ge(squared, HEADS + CT + k + 1)
                pe.matmul(ps[:, 3, :], mean_of[:, 2, :], lsq[:, k % 2, :], start=(k == 0),
                          stop=(k == KT - 1)).then_inc(v_turned, 1)
            def key_scores(m):
                pe.wait_ge(subk_landed, 16)
                pe.wait_ge(qk_copied, m + 1)
                if m >= 2:
                    pe.wait_ge(s_copied, m - 1)
                for b in range(TB):
                    last = pe.matmul(ps[:, 2 + m % 2, b * P:(b + 1) * P], qk[:, m % 2, b * P:(b + 1) * P],
                                     subk[:, m, :], start=True, stop=True)
                last.then_inc(s_done, 1)

            for m in range(TILES_Q):
                tile_n(TILES_IN + 2 * TILES_OUT + m, h_lo if m == 0 else None)
                if m >= 1:
                    key_scores(m - 1)
            key_scores(TILES_Q - 1)
            with pe.Fori(0, EARLY_FREE // 2) as i:
                for e in range(2):
                    pe.wait_ge(u_act, 2 * i + (e + 1))
                    tile(4 * i + (C_EARLY + 2 * e), e, tokens=TD)
            pe.wait_ge(keys_made, 1)
            for i in range(3):
                for b in range(TB):
                    last = pe.transpose(ps[:, 4 + i, b * P:(b + 1) * P], keyf[:, i, b, :], ident[:, :])
            last.then_inc(keys_turned, 1)
            pe.wait_ge(keys_copied, 1)
            pe.sem_inc(g_done, 4)
            per = TG // QB
            et = len(BATCHES) // 2
            with pe.Fori(0, NTG // 2) as i:
                made = [0]

                def batches(n):
                    for _ in range(n):
                        s = made[0] % 4
                        pe.wait_ge(hots_made, 2 * per * i + (made[0] + 1))
                        pe.wait_ge(g_copied, 2 * per * i + (made[0] + 1))
                        for q in range(QB):
                            last = pe.matmul(ps[:, 4 + s, q * P:(q + 1) * P], hotL[:, s, q, :], hotR[:, s, q, :],
                                             start=True, stop=True)
                        last.then_inc(g_done, 1)
                        made[0] += 1

                for e in range(2 * et):
                    pe.wait_ge(u_act, 2 * et * i + (EARLY_FREE + e + 1))
                    tile(4 * et * i + (C_EARLY + 2 * EARLY_FREE + 2 * e), e % 2,
                         between=lambda: batches(BATCHES[2 * e % len(BATCHES)]), tokens=TD)
                    batches(BATCHES[(2 * e + 1) % len(BATCHES)])

            with pe.Fori(0, EARLY_TAIL // 2 - 1) as i:
                for e in range(2):
                    pe.wait_ge(u_act, 2 * i + (EARLY - EARLY_TAIL + e + 1))
                    tile(4 * i + (C_LATE - 2 * EARLY_TAIL + 2 * e), e, tokens=TD)
            pe.wait_ge(h_twice_made, 1)
            for k in range(KT):
                last = pe.transpose(ps[:, 2 + k // 4, k % 4 * P:(k % 4 + 1) * P],
                                    h_twice[:, k, :, :].rearrange("p f t -> p (f t)"), ident[:, :])
            last.then_inc(tok_turned, 1)
            for e in range(2):
                pe.wait_ge(u_act, EARLY - 2 + e + 1)
                tile(C_LATE - 4 + 2 * e, e, tokens=TD)

            def v_parts(g, slot, c0):
                with pe.Fori(0, PARTS // 2) as i:
                    for j in range(2):
                        pe.wait_ge(part_read, PARTS * g + 2 * i + (j + 1))
                        pe.wait_ge(lo_made, c0 + 2 * i + (j + 1))
                        for e in range(GRP):
                            pe.wait_ge(s_lo, GRP * g + (e + 1))
                            for d in range(2):
                                cols = slice((2 * e + d) * P, (2 * e + d + 1) * P)
                                o = ps[:, 2 + 2 * j + d, 0:TD]
                                pe.matmul(o, whi[:, j, cols], shi[:, slot, e, :], start=(e == 0), stop=False)
                                pe.matmul(o, whi[:, j, cols], slo[:, slot, e, :], start=False, stop=False)
                                last = pe.matmul(o, wlo[:, j, cols], shi[:, slot, e, :], start=False, stop=(e == GRP - 1))
                        last.then_inc(chunk_used, 1)

            with pe.Fori(0, EGRP // 2) as gg:
                for slot in range(2):
                    v_parts(2 * gg + slot, slot, 2 * PARTS * gg + (C_LATE + PARTS * slot))
            def pairs(lo, hi):
                with pe.Fori(lo, hi) as gg:
                    for slot in range(2):
                        c0 = 2 * C_GRP * gg + (C_MAIN + C_GRP * slot)
                        with pe.Fori(0, GRP // 2) as i:
                            for e in range(2):
                                pe.wait_ge(u_act, 2 * GRP * gg + 2 * i + (EGRP * GRP + GRP * slot + e + 1))
                                tile(c0 + 4 * i + 2 * e, e, tokens=TD)
                        v_parts(2 * gg + (EGRP + slot), slot, c0 + 2 * GRP)

            pairs(0, 2 * PAIRS_G + 1)
            pe.wait_ge(tok_summed, 1)
            for k in range(KT):
                last = pe.matmul(ps[:, 6 + k // 8, k % 8 * TR:(k % 8 + 1) * TR], tok[:, k * P:(k + 1) * P], fold[:, :],
                                 start=True, stop=True)
            last.then_inc(tok_folded, 1)
            pairs(2 * PAIRS_G + 1, PAIRS)
            pe.wait_ge(y_sum, 1)
            for k in range(KT):
                last = pe.matmul(ps[:, 6, :], mean_of[:, 2, :], acc[:, k, :], start=(k == 0), stop=(k == KT - 1))
            last.then_inc(mean_done, 1)
            for k in range(KT):
                pe.wait_ge(squared, HEADS + CT + KT + k + 1)
                pe.matmul(ps[:, 7, :], mean_of[:, 2, :], ysq[:, k % 2, :], start=(k == 0),
                          stop=(k == KT - 1)).then_inc(v_turned, 1)

        @block.scalar
        def _(act):
            steps = [0]

            def step(ins):
                steps[0] += 1
                ins.then_inc(act_step, 1)
                act.wait_ge(act_step, steps[0])

            act.dma_start(wa2[:, :], w_a2).then_inc(small_landed, 16)
            act.dma_start(fvec[:, 0:HEADS], b_a).then_inc(small_landed, 16)
            act.dma_start(fvec[:, GG:CB], gla_g).then_inc(small_landed, 16)
            act.dma_start(fvec[:, CB:CB + 3 * CT], vecs_conv).then_inc(small_landed, 16)
            act.dma_start(cw[:, :, :], conv_w).then_inc(small_landed, 16)
            act.dma_start(lnv[:, :, :], ln_vecs).then_inc(small_landed, 16)
            act.wait_ge(small_landed, 16 * 6)

            def evacuate(n, out_ap, func=ACT.Copy, **kw):
                act.wait_ge(chunk_used, used_by(n))
                return act.activation(out_ap, ps[:, n % 2, :], func, **kw)

            for i in range(KT):
                act.wait_ge(x_landed[i // 2], 16)
                src = conv_out[:, i, :] if i < CT else gla_out[:, i - CT, :]
                act.activation(xhi[:, i, :], src, ACT.Copy).then_inc(x_hi, 1)
            evacuate(0, a_lr[:, :]).then_inc(bank_read[0], 1)
            act.wait_ge(bank_read[0], 1)
            act.sem_inc(a_exp, 1)
            for h in range(HEADS):
                def n_of(w):
                    return tile_of(h, w)
                act.wait_ge(z_done, h + 1)
                step(act.activation(t0[:, :], ps[:, 7, :], ACT.Identity, bias=fvec[:, BA + h:BA + h + 1]))
                step(act.activation(t1[:, :], t0[:, :], ACT.Abs))
                step(act.activation(t1[:, :], t1[:, :], ACT.Exp, scale=-1.0))
                act.activation(t1[:, :], t1[:, :], ACT.Ln, bias=1.0).then_inc(z_read, 1)
                act.wait_ge(a_sum, 2 * h + 1)
                act.activation(ex[:, 0, :], d1[:, :], ACT.Exp, scale=1.0 / TAU)
                act.activation(ex[:, 1, :], d1[:, :], ACT.Exp, scale=-1.0 / TAU)
                act.activation(ex[:, 3, :], bcum[:, :], ACT.Exp, scale=1.0 / TAU)
                act.wait_ge(a_sum, 2 * h + 2)
                act.activation(ex[:, 2, :], d2[:, :], ACT.Exp, scale=-1.0 / TAU).then_inc(a_exp, 1)
                evacuate(n_of(HQ), qT[:, :], scale=float(P) ** -0.5).then_inc(bank_read[n_of(HQ) % 2], 1)
                if h >= 1:
                    act.wait_ge(c_ready, 2 * h)
                evacuate(n_of(HK), kT[:, :]).then_inc(bank_read[n_of(HK) % 2], 1)
                evacuate(n_of(HV0), vT[:, 0, :]).then_inc(bank_read[n_of(HV0) % 2], 1)
                evacuate(n_of(HV1), vT[:, 1, :]).then_inc(bank_read[n_of(HV1) % 2], 1)
                act.wait_ge(bank_read[n_of(HV1) % 2], (n_of(HV1)) // 2 + 1)
                act.wait_ge(bank_read[n_of(HV0) % 2], (n_of(HV0)) // 2 + 1)
                act.sem_inc(v_copied, 1)
                act.wait_ge(v_turned, h + 1)
                for j in range(2):
                    last = act.activation(vtok[:, :, j * P:(j + 1) * P],
                                          ps[:, 2 + j, :].rearrange("p (b v) -> p b v", v=P), ACT.Copy)
                last.then_inc(vtok_copied, 1)
                act.wait_ge(qk_scaled, h + 1)
                evacuate(n_of(HG0), sg[:, :], ACT.Sigmoid).then_inc(bank_read[n_of(HG0) % 2], 1)
                act.wait_ge(k_turned, h + 1)
                act.activation(ktok[:, :, :], ps[:, 4, :].rearrange("p (b k) -> p b k", k=P), ACT.Copy).then_inc(ktok_copied, 1)
                act.wait_ge(c_ready, 2 * h + 1)
                evacuate(n_of(HG1), sg[:, :], ACT.Sigmoid).then_inc(bank_read[n_of(HG1) % 2], 1)
                act.wait_ge(o_done, h + 1)
                if h >= 1:
                    act.wait_ge(head_done, h)
                act.activation(o_sb[:, :, :], ps[:, 6:8, :], ACT.Copy).then_inc(o_copied, 1)
                act.wait_ge(centred, h + 1)
                act.activation(osq[:, :, :], o_sb[:, :, :], ACT.Square).then_inc(squared, 1)
                for j in range(2):
                    evacuate(n_of(HR0 + j), srr[:, j, :], ACT.Sigmoid)
                    act.activation(rr[:, j, :], ps[:, n_of(HR0 + j) % 2, :], ACT.Copy).then_inc(bank_read[n_of(HR0 + j) % 2], 1)
                    if j == 0:
                        act.wait_ge(var_done, h + 1)
                        act.activation(rstd[:, :], ps[:, 3, :], ACT.Sqrt, bias=eps_col[:, 0:1]).then_inc(rooted, 1)
                act.wait_ge(bank_read[n_of(HR0) % 2], n_of(HR0) // 2 + 1)
                act.wait_ge(bank_read[n_of(HR1) % 2], n_of(HR1) // 2 + 1)
                act.sem_inc(r_copied, 1)

            act.wait_ge(head_done, HEADS)
            for k in range(CT):
                act.activation(xhi[:, k, :], gla_out[:, k, :], ACT.Copy).then_inc(mix_hi, 1)
            act.wait_ge(mix_lo, CT)
            act.dma_start(pre[:, :, :], xT).then_inc(res_landed, 16)
            for k in range(CT):
                act.wait_ge(centred, HEADS + k + 1)
                if k >= 2:
                    act.wait_ge(v_turned, HEADS + k - 1)
                act.activation(vT[:, k % 2, :], conv_out[:, k, :], ACT.Square).then_inc(squared, 1)
            act.wait_ge(v_turned, HEADS + CT)
            act.activation(rstd[:, :], ps[:, 3, :], ACT.Sqrt, bias=eps_col[:, 0:1]).then_inc(rooted, 1)
            for k in range(CT):
                act.wait_ge(silu_parts, k + 1)
                if k >= 2:
                    act.wait_ge(mixf, k - 1)
                act.activation(rr[:, k % 2, :], conv_out[:, k, :], ACT.Identity, scale=fvec[:, CG + k:CG + k + 1],
                               bias=fvec[:, CBB + k:CBB + k + 1]).then_inc(r_copied, 1)
                act.activation(srr[:, k % 2, :], conv_out[:, k, :], ACT.Sigmoid, scale=fvec[:, CG + k:CG + k + 1],
                               bias=fvec[:, CBB + k:CBB + k + 1]).then_inc(r_copied, 1)
            for k in range(CT):
                act.wait_ge(mixf, k + 1)
                act.activation(xhi[:, CT + k, :], conv_out[:, k, :], ACT.Copy).then_inc(mix_hi, 1)
            for k in range(KT):
                act.wait_ge(centred, HEADS + CT + k + 1)
                if k >= 2:
                    act.wait_ge(v_turned, HEADS + CT + k - 1)
                act.activation(lsq[:, k % 2, :], pre[:, k, :], ACT.Square).then_inc(squared, 1)
            act.wait_ge(v_turned, HEADS + CT + KT)
            act.activation(rstd[:, :], ps[:, 3, :], ACT.Sqrt, bias=eps_col[:, 0:1]).then_inc(rooted, 1)
            for k in range(KT):
                act.wait_ge(silu_parts, CT + k + 1)
                if k >= 2:
                    act.wait_ge(h_lo, k - 1)
                act.activation(hful[:, k % 2, :], pre[:, k, :], ACT.Identity, bias=lnv[:, 1, k:k + 1]).then_inc(h_full, 1)
                act.wait_ge(h_full, k + 1)
                act.activation(xhi[:, k, :], hful[:, k % 2, :], ACT.Copy).then_inc(h_hi, 1)
            def copy_scores(m):
                act.wait_ge(s_done, m + 1)
                act.activation(score[:, m, :, :], ps[:, 2 + m % 2, :].rearrange("p (b k) -> p b k", k=NK),
                               ACT.Copy).then_inc(s_copied, 1)

            for m in range(TILES_Q):
                n = TILES_IN + 2 * TILES_OUT + m
                if m == 0:
                    act.wait_ge(h_lo, KT)
                    act.dma_start(subk[:, :, :], sub_k).then_inc(subk_landed, 16)
                if m >= 2:
                    act.wait_ge(s_done, m - 1)
                evacuate(n, qk[:, m % 2, :]).then_inc(bank_read[n % 2], 1)
                act.wait_ge(bank_read[n % 2], n // 2 + 1)
                act.sem_inc(qk_copied, 1)
                if m >= 1:
                    copy_scores(m - 1)
            copy_scores(TILES_Q - 1)
            act.sem_inc(u_act, 2)

            def early_gelu(t, turn, e):
                act.wait_ge(chunk_used, 2 * t + (NSPLIT + C_EARLY + 2))
                if turn is not None:
                    act.wait_ge(acts_stored[e], turn)
                act.sem_inc(act_turn, 1)
                act.activation(act_u[:, e, :], ps[:, e, 0:TD], ACT.Gelu).then_inc(u_act, 1)
                act.wait_ge(u_act, t + 3)
                act.sem_inc(act_turn, 1)

            for t in range(2):
                early_gelu(t, None, t)
                act.dma_start(early_acts[t], act_u[:, t, :]).then_inc(acts_stored[t], 16)
            act.wait_ge(sc_sub, 1)
            act.activation(gexp[:, :, :], best[:, :, :], ACT.Exp).then_inc(sc_exp, 1)
            first = early_acts[0:EARLY_FREE].rearrange("(i e) p t -> i e p t", e=2)
            with act.Fori(1, EARLY_FREE // 2) as i:
                for e in range(2):
                    early_gelu(2 * i + e, 16 * i, e)
                    act.dma_start(first[i, e], act_u[:, e, :]).then_inc(acts_stored[e], 16)
            act.wait_ge(keys_turned, 1)
            act.activation(keyT[:, :, :], ps[:, 4:7, :], ACT.Copy).then_inc(keys_copied, 1)
            act.wait_ge(keys_copied, 1)
            act.sem_inc(g_copied, 4)
            act.wait_ge(chosen_made, 1)
            for f in range(FOLD):
                act.dma_start(row_f[f * TR:(f + 1) * TR, :, :],
                              chosen[P - TR:P, :, f * RANKS:(f + 1) * RANKS]).then_inc(row_f_landed, 16)
            per = TG // QB
            et = len(BATCHES) // 2
            rest = early_acts[EARLY_FREE:EARLY - EARLY_TAIL].rearrange("(i e) p t -> i e p t", e=2 * et)
            blocks = gates.rearrange("(i half) p k t -> i half p k t", half=2)

            def gate_stages(i, first_turn):
                made = [0]

                def batches(n):
                    for _ in range(n):
                        b = made[0]
                        half, q0 = b // per, b % per * QB
                        if b % per == 0 and not first_turn:
                            act.wait_ge(gstored[half], 16 * i)
                        act.wait_ge(g_done, 2 * per * i + (b + 5))
                        act.sem_inc(act_turn, 1)
                        act.activation(gstage[:, half, :, q0:q0 + QB], ps[:, 4 + b % 4, :].rearrange("p (q k) -> p k q", q=QB),
                                       ACT.Copy).then_inc(g_copied, 1)
                        made[0] += 1
                        if made[0] % per == 0:
                            act.wait_ge(g_copied, 2 * per * i + (made[0] + 4))
                            act.dma_start(blocks[i, half], gstage[:, half, :, :]).then_inc(gstored[half], 16)

                for e in range(2 * et):
                    batches(BATCHES[2 * e % len(BATCHES)])
                    early_gelu(2 * et * i + (EARLY_FREE + e), 16 * et * i + 16 * (EARLY_FREE // 2 + e // 2), e % 2)
                    act.dma_start(rest[i, e], act_u[:, e % 2, :]).then_inc(acts_stored[e % 2], 16)
                    batches(BATCHES[(2 * e + 1) % len(BATCHES)])

            gate_stages(0, True)
            with act.Fori(1, NTG // 2) as i:
                gate_stages(i, False)
            tail = early_acts[EARLY - EARLY_TAIL:EARLY].rearrange("(i e) p t -> i e p t", e=2)
            with act.Fori(0, EARLY_TAIL // 2 - 1) as i:
                for e in range(2):
                    early_gelu(2 * i + (EARLY - EARLY_TAIL + e), 16 * i + 16 * (EARLY - EARLY_TAIL) // 2, e)
                    act.dma_start(tail[i, e], act_u[:, e, :]).then_inc(acts_stored[e], 16)
            act.wait_ge(tok_turned, 1)
            act.activation(tok[:, :].rearrange("p (j t) -> p j t", j=4), ps[:, 2:6, :], ACT.Copy).then_inc(tok_copied, 1)
            for e in range(2):
                early_gelu(EARLY - 2 + e, 16 * (EARLY // 2 - 1), e)
                act.dma_start(early_acts[EARLY - 2 + e], act_u[:, e, :]).then_inc(acts_stored[e], 16)
            for half in range(2):
                act.wait_ge(gstored[half], 16 * NTG // 2)
                act.wait_ge(acts_stored[half], 16 * EARLY // 2)
            act.wait_ge(acc_ready, 1)

            def round_s(g, slot, e):
                act.wait_ge(s_prod, GRP * g + (e + GRP + 1))
                act.sem_inc(act_turn, 1)
                act.activation(shi[:, slot, e, :], s_f[:, e % 2, :], ACT.Copy).then_inc(s_hi, 1)

            with act.Fori(0, EGRP // 2) as gg:
                for slot in range(2):
                    act.wait_ge(chunk_used, 2 * PARTS * gg + (NSPLIT + C_LATE + PARTS * (slot - 1)))
                    for e in range(GRP):
                        round_s(2 * gg + slot, slot, e)
            def pairs(lo, hi):
                with act.Fori(lo, hi) as gg:
                    for slot in range(2):
                        for e in range(GRP):
                            idx = 2 * GRP * gg + (EGRP * GRP + GRP * slot + e)
                            act.wait_ge(chunk_used, 2 * C_GRP * gg + (NSPLIT + C_MAIN + C_GRP * slot + 2 * e + 2))
                            act.wait_ge(s_prod, idx + (GRP - 1))
                            act.sem_inc(act_turn, 1)
                            act.activation(act_u[:, e % 2, :], ps[:, e % 2, 0:TD], ACT.Gelu).then_inc(u_act, 1)
                            round_s(2 * gg + (EGRP + slot), slot, e)

            pairs(0, PAIRS_G)
            act.wait_ge(dots_kept, 2 * PAIRS_G)
            act.activation(row_dot[:, :], row_dot[:, :], ACT.Gelu).then_inc(dots_gelu, 1)
            pairs(PAIRS_G, PAIRS)
            for k in range(KT):
                act.wait_ge(centred, HEADS + CT + KT + k + 1)
                if k >= 2:
                    act.wait_ge(v_turned, HEADS + CT + KT + k - 1)
                act.activation(ysq[:, k % 2, :], acc[:, k, :], ACT.Square).then_inc(squared, 1)
            act.wait_ge(v_turned, HEADS + CT + 2 * KT)
            act.activation(rstd[:, :], ps[:, 7, :], ACT.Sqrt, bias=eps_col[:, 0:1]).then_inc(rooted, 1)
            for k in range(KT):
                act.wait_ge(y_sum, k + 2)
                act.activation(acc[:, k, :], acc[:, k, :], ACT.Identity, bias=lnv[:, 3, k:k + 1]).then_inc(y_out, 1)

        @block.vector
        def _(dve):
            steps = [0]

            def step(ins):
                steps[0] += 1
                ins.then_inc(dve_step, 1)
                dve.wait_ge(dve_step, steps[0])

            for i in range(KT):
                dve.wait_ge(x_hi, i + 1)
                src = conv_out[:, i, :] if i < CT else gla_out[:, i - CT, :]
                dve.tensor_tensor(xlo[:, i, :], src, xhi[:, i, :].bitcast(F32), ALU.subtract).then_inc(x_lo, 1)
            dve.wait_ge(x_lo, KT)
            dve.wait_ge(small_landed, 16 * 6)
            dve.wait_ge(consts, 3)
            dve.memset(cpad[:, :, 0:TAPS - 1], 0.0)
            step(dve.memset(sT[:, :, :], 0.0))

            def chunks(a):
                return a.rearrange("p (n c) -> p n c", c=GC)

            def conv(m, j):
                acc_c = conv_out[:, m, :]
                step(dve.tensor_scalar(acc_c, cpad[:, j, 0:T], cw[:, m, 0:1], fvec[:, CB + m:CB + m + 1],
                                       ALU.mult, ALU.add))
                for k in range(1, TAPS):
                    ins = dve.scalar_tensor_tensor(out=acc_c, in0=cpad[:, j, k:k + T], scalar=cw[:, m, k:k + 1],
                                                   in1=acc_c, op0=ALU.mult, op1=ALU.add)
                    if k < TAPS - 1:
                        step(ins)
                ins.then_inc(vdec, 1)
                dve.wait_ge(vdec, m + 1)

            for h in range(HEADS):
                def n_of(w):
                    return tile_of(h, w)
                dve.wait_ge(z_read, h + 1)
                step(dve.scalar_tensor_tensor(out=t1[:, :], in0=t0[:, :], scalar=0.0, in1=t1[:, :],
                                              op0=ALU.min, op1=ALU.subtract))
                step(dve.tensor_tensor_scan(bcum[:, :], reset[:, :], t1[:, :], 0.0, ALU.mult, ALU.add))
                b3 = chunks(bcum[:, :])
                dve.tensor_tensor(chunks(d1[:, :]), b3, b3[:, :, GC // 2:GC // 2 + 1].to_broadcast([P, NGC, GC]),
                                  ALU.subtract).then_inc(a_sum, 1)
                dve.tensor_tensor(chunks(d2[:, :]), b3, b3[:, :, GC - 1:GC].to_broadcast([P, NGC, GC]),
                                  ALU.subtract).then_inc(a_sum, 1)
                dve.wait_ge(a_exp, h + 2)
                dve.wait_ge(bank_read[n_of(HQ) % 2], n_of(HQ) // 2 + 1)
                dve.wait_ge(bank_read[n_of(HK) % 2], n_of(HK) // 2 + 1)
                step(dve.tensor_copy(d1[:, 0:NGC], chunks(ex[:, 3, :])[:, :, GC - 1]))
                for i, src in ((0, qT), (1, kT), (2, kT), (3, qT)):
                    last = dve.tensor_tensor(ex[:, i, :], ex[:, i, :], src[:, :], ALU.mult)
                last.then_inc(qk_scaled, 1)
                dve.wait_ge(scored, h + 1)
                dve.copy_predicated(sT[:, :, :], causal[:, :, :].bitcast(U32),
                                    ps[:, 5, :].rearrange("p (b q) -> p b q", q=P)).then_inc(masked, 1)
                def gated(j, w):
                    dve.wait_ge(chunk_used, used_by(n_of(w)))
                    dve.wait_ge(bank_read[n_of(w - 1) % 2], n_of(w - 1) // 2 + 1)
                    dve.tensor_tensor(cpad[:, j, TAPS - 1:], ps[:, n_of(w) % 2, :], sg[:, :],
                                      ALU.mult).then_inc(bank_read[n_of(w) % 2], 1)
                    dve.wait_ge(bank_read[n_of(w) % 2], n_of(w) // 2 + 1)
                    dve.sem_inc(c_ready, 1)
                gated(0, HC0)
                dve.wait_ge(kv_done, h + 1)
                for n in range(NGC - 1):
                    kv = kv_of(n)
                    if n == 0:
                        step(dve.tensor_copy(states[:, 0, :], kv))
                    else:
                        ins = dve.scalar_tensor_tensor(out=states[:, n, :], in0=states[:, n - 1, :],
                                                       scalar=d1[:, n:n + 1], in1=kv, op0=ALU.mult, op1=ALU.add)
                        if n < NGC - 2:
                            step(ins)
                ins.then_inc(states_made, 1)
                conv(2 * h, 0)
                gated(1, HC1)
                dve.wait_ge(mean_done, h + 1)
                dve.wait_ge(o_copied, h + 1)
                for j in range(2):
                    last = dve.tensor_tensor(o_sb[:, j, :], o_sb[:, j, :], ps[:, 2, :], ALU.subtract)
                last.then_inc(centred, 1)
                conv(2 * h + 1, 1)
                dve.wait_ge(rooted, h + 1)
                step(dve.reciprocal(rstd[:, :], rstd[:, :]))
                dve.wait_ge(centred, h + 1)
                for j in range(2):
                    last = dve.scalar_tensor_tensor(out=o_sb[:, j, :], in0=o_sb[:, j, :],
                                                    scalar=fvec[:, GG + 2 * h + j:GG + 2 * h + j + 1],
                                                    in1=rstd[:, :], op0=ALU.mult, op1=ALU.mult)
                step(last)
                dve.wait_ge(r_copied, h + 1)
                step(dve.tensor_tensor(rr[:, :, :], rr[:, :, :], srr[:, :, :], ALU.mult))
                dve.tensor_tensor(gla_out[:, 2 * h:2 * h + 2, :], o_sb[:, :, :], rr[:, :, :],
                                  ALU.mult).then_inc(head_done, 1)

            def centre(buf, k):
                dve.tensor_tensor(buf[:, k, :], buf[:, k, :], ps[:, 2, :], ALU.subtract).then_inc(centred, 1)

            def split_mix(k):
                dve.wait_ge(mix_hi, k + 1)
                src = gla_out[:, k, :] if k < CT else conv_out[:, k - CT, :]
                dve.tensor_tensor(xlo[:, k, :], src, xhi[:, k, :].bitcast(F32), ALU.subtract).then_inc(mix_lo, 1)

            def add_half(hm):
                n, m = TILES_IN + hm, hm % TILES_OUT
                dve.wait_ge(chunk_used, used_by(n))
                if hm < TILES_OUT:
                    ins = dve.scalar_tensor_tensor(out=pre[:, m, :], in0=pre[:, m, :], scalar=ALPHA, in1=ps[:, n % 2, :],
                                                   op0=ALU.mult, op1=ALU.add)
                else:
                    ins = dve.tensor_tensor(pre[:, m, :], pre[:, m, :], ps[:, n % 2, :], ALU.add)
                ins.then_inc(bank_read[n % 2], 1)

            for k in range(CT):
                split_mix(k)
            dve.wait_ge(res_landed, 16)
            for hm in range(0, 6):
                add_half(hm)
            dve.wait_ge(mean_done, HEADS + 1)
            for k in range(CT):
                centre(conv_out, k)
            for hm in range(6, 9):
                add_half(hm)
            dve.wait_ge(rooted, HEADS + 1)
            step(dve.reciprocal(rstd[:, :], rstd[:, :]))
            for k in range(CT):
                dve.wait_ge(squared, HEADS + k + 1)
                dve.tensor_tensor(conv_out[:, k, :], conv_out[:, k, :], rstd[:, :], ALU.mult).then_inc(silu_parts, 1)
            for k in range(CT):
                dve.wait_ge(r_copied, HEADS + 2 * k + 2)
                dve.tensor_tensor(conv_out[:, k, :], rr[:, k % 2, :], srr[:, k % 2, :], ALU.mult).then_inc(mixf, 1)
                if k % 2 == 1 and 9 + k // 2 < 12:
                    add_half(9 + k // 2)
            for k in range(CT, KT):
                split_mix(k)
                if k % 2 == 1 and 12 + (k - CT) // 2 < TILES_OUT:
                    add_half(12 + (k - CT) // 2)
            for m in range(TILES_OUT):
                n = TILES_IN + TILES_OUT + m
                add_half(TILES_OUT + m)
                dve.wait_ge(bank_read[n % 2], n // 2 + 1)
                if m == 0:
                    ins = dve.tensor_copy(presum[:, :], pre[:, 0, :])
                else:
                    ins = dve.tensor_tensor(presum[:, :], presum[:, :], pre[:, m, :], ALU.add)
                if m < TILES_OUT - 1:
                    step(ins)
            ins.then_inc(pre_made, 1)
            dve.wait_ge(mean_done, HEADS + 2)
            for k in range(KT):
                centre(pre, k)
            dve.wait_ge(rooted, HEADS + 2)
            step(dve.reciprocal(rstd[:, :], rstd[:, :]))
            for k in range(KT):
                dve.wait_ge(squared, HEADS + CT + k + 1)
                dve.scalar_tensor_tensor(out=pre[:, k, :], in0=pre[:, k, :], scalar=lnv[:, 0, k:k + 1],
                                         in1=rstd[:, :], op0=ALU.mult, op1=ALU.mult).then_inc(silu_parts, 1)
            for k in range(KT):
                dve.wait_ge(h_hi, k + 1)
                dve.tensor_tensor(xlo[:, k, :], hful[:, k % 2, :], xhi[:, k, :].bitcast(F32),
                                  ALU.subtract).then_inc(h_lo, 1)

            def top16(src, spare, vals, idx):
                step(dve.max(vals[:, 0:8], src))
                dve.max_index(idx[:, 0:8], vals[:, 0:8], src)
                step(dve.match_replace(spare, vals[:, 0:8], src, LOWEST))
                step(dve.max(vals[:, 8:16], spare))
                step(dve.max_index(idx[:, 8:16], vals[:, 8:16], spare))

            dve.wait_ge(h_lo, KT)
            for m in range(TILES_Q):
                dve.wait_ge(s_copied, m + 1)
                for b in range(TB):
                    top16(score[:, m, b, :], cut[:, :], topv[:, b, m, :], topi[:, b, m, :])
                if m % 2 == 0:
                    continue
                h = m // 2
                for b in range(TB):
                    step(dve.tensor_tensor(cand[:, :].rearrange("p (i j) -> p i j", j=TOPK),
                                           topv[:, b, m - 1, :].unsqueeze(2).to_broadcast([P, TOPK, TOPK]),
                                           topv[:, b, m, :].unsqueeze(1).to_broadcast([P, TOPK, TOPK]), ALU.add))
                    r = slice(h * TOPK, (h + 1) * TOPK)
                    top16(cand[:, :], cut2[:, :], best[:, b, r], posi[:, b, r])
            b3 = best[:, :, :].rearrange("p b (h k) -> p (b h) k", k=TOPK)
            step(dve.tensor_copy(gsum[:, :, :], b3[:, :, 0:1]))
            dve.tensor_tensor(b3, b3, gsum[:, :, :].to_broadcast([P, TB * PH, TOPK]), ALU.subtract).then_inc(sc_sub, 1)
            step(dve.tensor_copy(topf[:, :, :, :], topi[:, :, :, :]))
            for half in range(2):
                if half == 0:
                    step(dve.tensor_single_scalar(posx[:, :, :], posi[:, :, :], 4, ALU.logical_shift_right))
                else:
                    step(dve.tensor_single_scalar(posx[:, :, :], posi[:, :, :], TOPK - 1, ALU.bitwise_and))
                step(dve.tensor_copy(posf[:, :, :], posx[:, :, :]))
                for b in range(TB):
                    step(dve.tensor_tensor(pick[:, :, :], posf[:, b, :].unsqueeze(2).to_broadcast([P, PH * TOPK, TOPK]),
                                           iota[:, 0:TOPK].unsqueeze(1).to_broadcast([P, PH * TOPK, TOPK]), ALU.is_equal))
                    p4 = pick[:, :, :].rearrange("p (h k) j -> p h k j", k=TOPK)
                    keys = topf[:, b, :, :].rearrange("p (h two) j -> p h two j", two=2)[:, :, half, :]
                    step(dve.tensor_tensor(p4, p4, keys.unsqueeze(2).to_broadcast([P, PH, TOPK, TOPK]), ALU.mult))
                    step(dve.tensor_reduce(keyf[:, half, b, :], pick[:, :, :], AX.X, ALU.add))
            dve.wait_ge(sc_exp, 1)
            e3 = gexp[:, :, :].rearrange("p b (h k) -> p (b h) k", k=TOPK)
            step(dve.tensor_reduce(gsum[:, :, 0], e3, AX.X, ALU.add))
            step(dve.reciprocal(gsum[:, :, 0], gsum[:, :, 0]))
            dve.tensor_tensor(keyf[:, 2, :, :].rearrange("p b (h k) -> p (b h) k", k=TOPK), e3,
                              gsum[:, :, :].to_broadcast([P, TB * PH, TOPK]), ALU.mult).then_inc(keys_made, 1)
            dve.wait_ge(keys_made, 1)
            dve.scalar_tensor_tensor(out=chosen[:, 0, :], in0=keyf[:, 0, TB - 1, :], scalar=float(NK),
                                     in1=keyf[:, 1, TB - 1, :], op0=ALU.mult, op1=ALU.add)
            dve.tensor_copy(chosen[:, 1, :], keyf[:, 2, TB - 1, :]).then_inc(chosen_made, 1)
            dve.tensor_tensor(fold[:, :], ident[:, 0:TR], ident[:, TR:2 * TR], ALU.add)
            dve.wait_ge(keys_copied, 1)
            kv4 = keyT[:, :, :].rearrange("p c (i s q) -> p c i s q", s=4, q=QB)
            with dve.Fori(0, TD // (4 * QB)) as i:
                for s in range(4):
                    dve.wait_ge(g_done, 4 * i + (s + 1))
                    for q in range(QB):
                        dve.tensor_scalar(hotL[:, s, q, :], iota[:, :], kv4[:, 0, i, s, q:q + 1],
                                          kv4[:, 2, i, s, q:q + 1], ALU.is_equal, ALU.mult)
                        last = dve.tensor_scalar(hotR[:, s, q, :], iota[:, :], kv4[:, 1, i, s, q:q + 1], None, ALU.is_equal)
                    last.then_inc(hots_made, 1)
            for half in range(2):
                dve.wait_ge(gstored[half], 16 * NTG // 2)
            for f in range(FOLD):
                last = dve.tensor_tensor(h_twice[:, :, f, :], xhi[:, :, TD:T].bitcast(F32), xlo[:, :, TD:T].bitcast(F32), ALU.add)
            last.then_inc(h_twice_made, 1)
            dve.wait_ge(row_f_landed, 16 * FOLD)
            dve.tensor_copy(row_idx[:, :], row_f[:, 0, :]).then_inc(rows_ready, 1)
            for k in range(KT):
                last = dve.tensor_scalar(acc[:, k, :], xhi[:, k, :].bitcast(F32), ALPHA, None, ALU.mult)
            step(last)
            for k in range(KT):
                last = dve.scalar_tensor_tensor(out=acc[:, k, :], in0=xlo[:, k, :].bitcast(F32), scalar=ALPHA,
                                                in1=acc[:, k, :], op0=ALU.mult, op1=ALU.add)
            last.then_inc(acc_ready, 1)
            dve.wait_ge(acc_ready, 1)
            dve.sem_inc(s_prod, GRP)
            dve.wait_ge(tok_copied, 1)
            dve.sem_inc(part_read, 2)

            def multiply(g, e, src):
                dve.wait_ge(g_landed[e], 16 * g + 16)
                dve.tensor_tensor(s_f[:, e % 2, :], src, gtile[:, e, :], ALU.mult).then_inc(s_prod, 1)

            def rest_of_s(g, slot, e):
                dve.wait_ge(s_hi, GRP * g + (e + 1))
                dve.tensor_tensor(slo[:, slot, e, :], s_f[:, e % 2, :], shi[:, slot, e, :].bitcast(F32),
                                  ALU.subtract).then_inc(s_lo, 1)

            def add_part(j, used):
                dve.wait_ge(chunk_used, used)
                dve.tensor_tensor(acc[:, 2 * j:2 * j + 2, 0:TD], acc[:, 2 * j:2 * j + 2, 0:TD],
                                  ps[:, 2 + 2 * (j % 2):4 + 2 * (j % 2), 0:TD], ALU.add).then_inc(part_read, 1)

            def early_s(g, slot, e):
                dve.wait_ge(a_landed[e], 16 * g + 16)
                multiply(g, e, atile[:, e, :])
                rest_of_s(g, slot, e)

            for e in range(GRP):
                early_s(0, 0, e)
            with dve.Fori(0, EGRP // 2 - 1) as gg:
                for slot in range(2):
                    for j in range(PARTS):
                        add_part(j, 2 * PARTS * gg + (NSPLIT + C_LATE + PARTS * slot + j + 1))
                        if j < GRP:
                            early_s(2 * gg + (slot + 1), 1 - slot, j)
            for slot in range(2):
                for j in range(PARTS):
                    add_part(j, PARTS * (EGRP - 2 + slot) + (NSPLIT + C_LATE + j + 1))
                    if j < GRP and slot == 0:
                        early_s(EGRP - 1, 1, j)
                if slot == 0:
                    dve.sem_inc(rows_used, 2)
            weight = row_dot[:, :].rearrange("p (g n) -> p g n", n=2 * ROWS_GRP)

            def dot(gg, r):
                dve.wait_ge(rows_landed[r % 2], 16 * ROWS_GRP * gg + 16 * (r // 2 + 1))
                dve.tensor_tensor_reduce(rows[:, r % 2, :], rows[:, r % 2, :], tok[:, :], 1.0, 0.0, ALU.mult, ALU.add,
                                         accum_out=dot_buf[:, r % ROWS_GRP:r % ROWS_GRP + 1]).then_inc(rows_used, 1)

            def add_row(gg, r):
                dve.wait_ge(rows_landed[r % 2], 16 * ROWS_GRP * gg + 16 * (r // 2 + 1))
                dve.wait_ge(rows_used, 2 * ROWS_GRP * gg + (r + 2))
                dve.scalar_tensor_tensor(out=tok[:, :], in0=rows[:, r % 2, :], scalar=weight[:, gg - PAIRS_G, r:r + 1],
                                         in1=tok[:, :], op0=ALU.mult, op1=ALU.add).then_inc(rows_used, 1)

            def pairs(lo, hi, use_row=None, keep=False):
                with dve.Fori(lo, hi) as gg:
                    for slot in range(2):
                        for e in range(GRP):
                            g = 2 * gg + (EGRP + slot)
                            dve.wait_ge(u_act, 2 * GRP * gg + (EGRP * GRP + GRP * slot + e + 3))
                            multiply(g, e, act_u[:, e % 2, :])
                            rest_of_s(g, slot, e)
                            if use_row:
                                use_row(gg, slot * ROWS_GRP + e)
                        for j in range(PARTS):
                            add_part(j, 2 * C_GRP * gg + (NSPLIT + C_MAIN + C_GRP * slot + 2 * GRP + j + 1))
                            if use_row and j % 2 == 1:
                                use_row(gg, slot * ROWS_GRP + GRP + j // 2)
                        if keep:
                            dve.wait_ge(rows_used, 2 * ROWS_GRP * gg + (ROWS_GRP * (slot + 1) + 2))
                            dve.tensor_copy(weight[:, gg, slot * ROWS_GRP:(slot + 1) * ROWS_GRP],
                                            dot_buf[:, :]).then_inc(dots_kept, 1)
                            dve.wait_ge(dots_kept, 2 * gg + (slot + 1))

            pairs(0, PAIRS_G, dot, keep=True)
            dve.memset(tok[:, :], 0.0)
            dve.wait_ge(dots_gelu, 1)
            step(dve.tensor_tensor(row_dot[:, :], row_dot[:, :], row_f[:, 1, :], ALU.mult))
            pairs(PAIRS_G, 2 * PAIRS_G, add_row)
            dve.wait_ge(rows_used, 2 * RANKS + 2)
            dve.sem_inc(tok_summed, 1)
            pairs(2 * PAIRS_G, 2 * PAIRS_G + 1)
            dve.wait_ge(tok_folded, 1)
            step(dve.tensor_tensor(acc[:, :, TD:T], acc[:, :, TD:T],
                                   ps[:, 6:8, :].rearrange("p j (k t) -> p (j k) t", t=TR), ALU.add))
            pairs(2 * PAIRS_G + 1, PAIRS)
            dve.wait_ge(part_read, NGRP * PARTS + 2)
            dve.sem_inc(y_sum, 1)
            dve.wait_ge(mean_done, HEADS + 3)
            for k in range(KT):
                dve.tensor_tensor(acc[:, k, :], acc[:, k, :], ps[:, 6, :], ALU.subtract).then_inc(centred, 1)
            dve.wait_ge(rooted, HEADS + 3)
            step(dve.reciprocal(rstd[:, :], rstd[:, :]))
            for k in range(KT):
                dve.wait_ge(squared, HEADS + CT + KT + k + 1)
                dve.scalar_tensor_tensor(out=acc[:, k, :], in0=acc[:, k, :], scalar=lnv[:, 2, k:k + 1],
                                         in1=rstd[:, :], op0=ALU.mult, op1=ALU.mult).then_inc(y_sum, 1)


def pack(w):
    m = w.shape[1] // P
    return w.reshape(2, HALF, P, m, P).transpose(3, 0, 2, 1, 4).reshape(2 * m, P, CHUNK)


def halves(chunks):
    return np.concatenate([chunks[0::2], chunks[1::2]])


def pack_tables(u, v):
    u = u.reshape(NK, NGRP, GRP, 2, HALF, P).transpose(1, 2, 3, 5, 4, 0).reshape(NGRP, 2 * GRP, P, CHUNK)
    v = v.reshape(NK, NGRP, GRP, PARTS, 2 * P).transpose(1, 3, 0, 2, 4).reshape(NGRP, PARTS, P, CHUNK)
    parts = [u[:EGRP], v[:EGRP], np.concatenate([u[EGRP:], v[EGRP:]], axis=1)]
    return np.concatenate([p.reshape(-1, P, CHUNK) for p in parts])


def columns(v):
    return v.reshape(-1, P).T


def mixer_order(w_in):
    q, k, v, r, a, c_val, c_gate = np.split(w_in, [512, 1024, 2048, 3072, 3088, 4112], axis=1)
    tiles = [a, np.zeros((D, P - a.shape[1]), w_in.dtype)]
    for h in range(HEADS):
        tiles += [q[:, h * P:(h + 1) * P], k[:, h * P:(h + 1) * P], v[:, h * DV:(h + 1) * DV]]
        for m in (2 * h, 2 * h + 1):
            tiles += [c_gate[:, m * P:(m + 1) * P], c_val[:, m * P:(m + 1) * P]]
        tiles.append(r[:, h * DV:(h + 1) * DV])
    return np.concatenate(tiles, axis=1)


def kernel(x, w_in, w_a2, b_a, gla_norm_g, conv_w, conv_b, conv_ln_g, conv_ln_b, w_out,
           ln1_g, ln1_b, w_q, sub_k1, sub_k2, u_tab, v_tab, ln2_g, ln2_b):
    import concourse.bacc as bacc
    from concourse.bass_utils import run_bass_kernel_spmd

    a = {k: np.asarray(v)[0] for k, v in dict(
        x=x, w_in=w_in, w_a2=w_a2, b_a=b_a, gla_norm_g=gla_norm_g, conv_w=conv_w, conv_b=conv_b,
        conv_ln_g=conv_ln_g, conv_ln_b=conv_ln_b, w_out=w_out, ln1_g=ln1_g, ln1_b=ln1_b, w_q=w_q,
        sub_k1=sub_k1, sub_k2=sub_k2, u_tab=u_tab, v_tab=v_tab, ln2_g=ln2_g, ln2_b=ln2_b).items()}
    data = {
        "stream": np.concatenate([pack(mixer_order(a["w_in"])), halves(pack(a["w_out"])), pack(a["w_q"]),
                                  pack_tables(a["u_tab"], a["v_tab"])]),
        "xT": a["x"].T.reshape(KT, P, T).transpose(1, 0, 2),
        "w_a2": a["w_a2"],
        "b_a": columns(a["b_a"]),
        "conv_w": a["conv_w"].T.reshape(CT, P, TAPS).transpose(1, 0, 2),
        "vecs_conv": np.concatenate([columns(a[k]) for k in ("conv_b", "conv_ln_g", "conv_ln_b")], axis=1),
        "gla_g": columns(a["gla_norm_g"]),
        "ln_vecs": np.stack([columns(a[k]) for k in ("ln1_g", "ln1_b", "ln2_g", "ln2_b")], axis=1),
        "sub_k": np.stack([a["sub_k1"], a["sub_k2"]], axis=1).reshape(2 * PH, NK, P).transpose(2, 0, 1),
        "u_rows": a["u_tab"],
        "v_rows": a["v_tab"],
    }
    nc = bacc.Bacc("TRN2", target_bir_lowering=False, num_devices=1)
    data = {k: np.ascontiguousarray(v) for k, v in data.items()}
    args = [nc.dram_tensor(k, v.shape, mybir.dt.from_np(v.dtype), kind="ExternalInput").ap()
            for k, v in data.items()]
    out = nc.dram_tensor("out", (P, KT, T), F32, kind="ExternalOutput").ap()
    build(nc, *args, out)
    r = run_bass_kernel_spmd(nc, [data], core_ids=[0])
    y = r.results[0]["out"]
    return np.ascontiguousarray(y.transpose(1, 0, 2).reshape(D, T).T).reshape(1, T, D)
```

```python
from contextlib import ExitStack

import numpy as np

import concourse.bass as bass
from concourse import mybir
from concourse.alu_op_type import AluOpType as ALU

F32 = mybir.dt.float32
F32R = mybir.dt.float32r
U32 = mybir.dt.uint32
ACT = mybir.ActivationFunctionType
AX = mybir.AxisListType

P = 128
T = 512
D = 2048
KT = D // P
TB = T // P
CHUNK = 1024
HALF = CHUNK // P
HEADS = 4
DV = 256
GC = 64
NGC = T // GC
TAPS = 31
CUT1, CUT2 = 12, 20
CT = 8
PH = 8
NK = 128
TOPK = 16
NRAW = 4
NSPLIT = 2
GRP = 4
PARTS = KT // 2
NGRP = NK // GRP
TILES_IN = 1 + 10 * HEADS
TILES_OUT = KT
TILES_Q = 2 * PH
C_IN = 2 * TILES_IN
C_OUT = 2 * TILES_OUT
C_Q = 2 * TILES_Q
C_HEAD = C_IN + C_OUT + C_Q
C_GRP = 2 * GRP + PARTS
TD = 448
TR = T - TD
FOLD = P // TR
RANKS = PH * TOPK // FOLD
NTG = 8
TG = TD // NTG
QB = 4
BATCHES = (3, 2, 2, 3, 2, 2)
EARLY_FREE = 10
EARLY_TAIL = 6
EARLY = EARLY_FREE + NTG * len(BATCHES) // 2 + EARLY_TAIL
EGRP = EARLY // GRP
C_EARLY = C_HEAD
C_LATE = C_EARLY + 2 * EARLY
C_MAIN = C_LATE + EGRP * PARTS
ROWS_GRP = 8
PAIRS_G = RANKS // (2 * ROWS_GRP)
PAIRS = (NGRP - EGRP) // 2
C_ALL = C_MAIN + (NGRP - EGRP) * C_GRP
EPS = 1e-5
ALPHA = 2.0 ** 0.25
TAU = 16.0
LOWEST = -3.0e38


def build(nc, stream, xT, w_a2, b_a, conv_w, vecs_conv, gla_g, ln_vecs, sub_k, u_rows, v_rows, out):
    es = ExitStack()
    with es:
        def sem(name):
            return es.enter_context(nc.semaphore(name))

        def sb(name, shape, dt=F32, ctx=es):
            return ctx.enter_context(nc.sbuf_tensor(name, shape, dt))

        xhi = sb("xhi", [P, KT, T], F32R)
        xlo = sb("xlo", [P, KT, T], F32R)
        raw = sb("raw", [P, NRAW, CHUNK])
        whi = sb("whi", [P, NSPLIT, CHUNK], F32R)
        wlo = sb("wlo", [P, NSPLIT, CHUNK], F32R)
        ident = sb("ident", [P, P])
        iota = sb("iota", [P, P])
        lnv = sb("lnv", [P, 4, KT])
        mean_of = sb("mean_of", [P, 3, P])
        rstd = sb("rstd", [P, T])
        eps_col = sb("eps_col", [P, 1])
        warm = sb("warm", [P, 1])

        kept = ExitStack()
        conv_out = sb("conv_out", [P, CT, T], F32, kept)
        fvec = sb("fvec", [P, HEADS + 2 * HEADS + 3 * CT], F32, kept)
        vT = sb("vT", [P, 2, T], F32, kept)
        states = sb("states", [P, NGC - 1, DV], F32, kept)
        rr = sb("rr", [P, 2, T], F32, kept)
        front = ExitStack()
        def fb(name, shape, dt=F32):
            return sb(name, shape, dt, front)
        gla_out = fb("gla_out", [P, 2 * HEADS, T])
        a_lr = fb("a_lr", [P, T])
        wa2 = fb("wa2", [16, HEADS * P])
        reset = fb("reset", [P, T])
        causal = fb("causal", [P, TB, P])
        qT = fb("qT", [P, T])
        kT = fb("kT", [P, T])
        vtok = fb("vtok", [P, TB, DV])
        t0 = fb("t0", [P, T])
        t1 = fb("t1", [P, T])
        bcum = fb("bcum", [P, T])
        d1 = fb("d1", [P, T])
        ex = fb("ex", [P, 4, T])
        sT = fb("sT", [P, TB, P])
        ktok = fb("ktok", [P, TB, P])
        o_sb = fb("o_sb", [P, 2, T])
        cpad = fb("cpad", [P, 2, TAPS - 1 + T])
        cw = fb("cw", [P, CT, TAPS])
        front.close()
        d2 = t0
        sg = kT
        srr = states[:, 0:4, :].rearrange("p a b -> p (a b)").rearrange("p (j t) -> p j t", j=2)
        osq = vT

        mid = ExitStack()
        pre = sb("pre", [P, KT, T], F32, mid)
        presum = sb("presum", [P, T], F32, mid)
        lsq = sb("lsq", [P, 2, T], F32, mid)
        mid.close()
        kept.close()

        act_u = sb("act_u", [P, 2, TD])
        keyT = sb("keyT", [P, 3, T])

        chosen = sb("chosen", [P, 2, PH * TOPK])
        row_f = sb("row_f", [P, 2, RANKS])
        row_idx = sb("row_idx", [P, RANKS], U32)
        row_dot = sb("row_dot", [P, RANKS])
        dot_buf = sb("dot_buf", [P, ROWS_GRP])
        row_col = sb("row_col", [P, 2], U32)
        fold = sb("fold", [P, TR])

        ret = ExitStack()
        def rb(name, shape, dt=F32):
            return sb(name, shape, dt, ret)
        subk = rb("subk", [P, TILES_Q, NK])
        score = rb("score", [P, TILES_Q, TB, NK])
        qk = rb("qk", [P, 2, T])
        cut = rb("cut", [P, NK])
        cand = rb("cand", [P, TOPK * TOPK])
        cut2 = rb("cut2", [P, TOPK * TOPK])
        topv = rb("topv", [P, TB, TILES_Q, TOPK])
        topi = rb("topi", [P, TB, TILES_Q, TOPK], U32)
        topf = rb("topf", [P, TB, TILES_Q, TOPK])
        posi = rb("posi", [P, TB, PH * TOPK], U32)
        posx = rb("posx", [P, TB, PH * TOPK], U32)
        posf = rb("posf", [P, TB, PH * TOPK])
        best = rb("best", [P, TB, PH * TOPK])
        pick = rb("pick", [P, PH * TOPK, TOPK])
        keyf = rb("keyf", [P, 3, TB, PH * TOPK])
        gsum = rb("gsum", [P, TB * PH, 1])
        gexp = rb("gexp", [P, TB, PH * TOPK])
        ret.close()

        gat = ExitStack()
        gstage = sb("gstage", [P, 2, NK, TG], F32, gat)
        hotL = sb("hotL", [P, 4, QB, P], F32, gat)
        hotR = sb("hotR", [P, 4, QB, P], F32, gat)
        gat.close()

        pee = ExitStack()
        acc = sb("acc", [P, KT, T], F32, pee)
        shi = sb("shi", [P, 2, GRP, TD], F32R, pee)
        slo = sb("slo", [P, 2, GRP, TD], F32R, pee)
        gtile = sb("gtile", [P, 4, TD], F32, pee)
        s_f = sb("s_f", [P, 2, TD], F32, pee)
        tok = sb("tok", [P, D], F32, pee)
        rows = sb("rows", [P, 2, D], F32, pee)
        atile = rows[:, 1, 0:GRP * TD].rearrange("p (e t) -> p e t", e=GRP)
        h_twice = rows[:, 0, :].rearrange("p (k f t) -> p k f t", k=KT, f=FOLD)
        tile_sum = tok[:, 0:T]
        ysq = rows[:, 0, 0:2 * T].rearrange("p (j t) -> p j t", j=2)
        pee.close()

        ps = es.enter_context(nc.psum_tensor("ps", [P, 8, T], F32))
        gates = nc.dram_tensor("gates", (NTG, P, NK, TG), F32, kind="Internal").ap()
        early_acts = nc.dram_tensor("early_acts", (EARLY, P, TD), F32, kind="Internal").ap()

        raw_landed = [sem(f"raw_landed{s}") for s in range(NRAW)]
        hi_made, lo_made = sem("hi_made"), sem("lo_made")
        split_begun = sem("split_begun")
        chunk_used = sem("chunk_used")
        bank_read = [sem("bank_read0"), sem("bank_read1")]
        x_landed = [sem(f"x_landed{i}") for i in range(KT // 2)]
        small_landed, subk_landed = sem("small_landed"), sem("subk_landed")
        consts = sem("consts")
        x_hi, x_lo = sem("x_hi"), sem("x_lo")
        z_done, z_read = sem("z_done"), sem("z_read")
        a_sum, a_exp = sem("a_sum"), sem("a_exp")
        v_copied = sem("v_copied")
        vdec = sem("vdec")
        qk_scaled = sem("qk_scaled")
        v_turned, vtok_copied = sem("v_turned"), sem("vtok_copied")
        k_turned, ktok_copied = sem("k_turned"), sem("ktok_copied")
        scored, masked = sem("scored"), sem("masked")
        kv_done, states_made = sem("kv_done"), sem("states_made")
        o_done, o_copied = sem("o_done"), sem("o_copied")
        mean_done, centred = sem("mean_done"), sem("centred")
        squared, var_done = sem("squared"), sem("var_done")
        rooted, head_done = sem("rooted"), sem("head_done")
        c_ready = sem("c_ready")
        r_copied = sem("r_copied")
        act_step, dve_step = sem("act_step"), sem("dve_step")
        silu_parts = sem("silu_parts")
        mixf, mix_hi, mix_lo = sem("mixf"), sem("mix_hi"), sem("mix_lo")
        res_landed = [sem(f"res_landed{i}") for i in range(4)]
        pre_made = sem("pre_made")
        h_hi, h_lo = sem("h_hi"), sem("h_lo")
        qk_copied, s_done, s_copied = sem("qk_copied"), sem("s_done"), sem("s_copied")
        act_turn = sem("act_turn")
        sc_sub, sc_exp = sem("sc_sub"), sem("sc_exp")
        keys_made, keys_turned, keys_copied = sem("keys_made"), sem("keys_turned"), sem("keys_copied")
        hots_made, g_done, g_copied = sem("hots_made"), sem("g_done"), sem("g_copied")
        gstored = [sem("gstored0"), sem("gstored1")]
        g_landed = [sem(f"g_landed{i}") for i in range(4)]
        a_landed = [sem(f"a_landed{i}") for i in range(4)]
        acts_stored = [sem("acts_stored0"), sem("acts_stored1")]
        acc_ready = sem("acc_ready")
        u_act, s_prod, s_hi, s_lo = sem("u_act"), sem("s_prod"), sem("s_hi"), sem("s_lo")
        part_read = sem("part_read")
        y_sum, y_out = sem("y_sum"), sem("y_out")
        chosen_made, row_f_landed = sem("chosen_made"), sem("row_f_landed")
        h_twice_made, tok_turned, tok_copied = sem("h_twice_made"), sem("tok_turned"), sem("tok_copied")
        rows_ready = sem("rows_ready")
        col_made, rows_used = sem("col_made"), sem("rows_used")
        rows_landed = [sem("rows_landed0"), sem("rows_landed1")]
        dots_kept, dots_gelu = sem("dots_kept"), sem("dots_gelu")
        tok_summed, tok_folded = sem("tok_summed"), sem("tok_folded")
        out_stored = sem("out_stored")

        BA, GG, CB, CG, CBB = 0, HEADS, 3 * HEADS, 3 * HEADS + CT, 3 * HEADS + 2 * CT

        HQ, HK, HV0, HV1, HG0, HC0, HG1, HC1, HR0, HR1 = range(10)

        def kv_of(n):
            return ps[:, 2 + 2 * (n % 2) + n // 4, (n // 2 % 2) * DV:(n // 2 % 2 + 1) * DV]

        def used_by(n):
            if n < TILES_IN:
                return NSPLIT + 2 * n + 2
            if n < TILES_IN + 2 * TILES_OUT:
                return NSPLIT + C_IN + (n - TILES_IN) + 1
            return NSPLIT + C_IN + C_OUT + 2 * (n - TILES_IN - 2 * TILES_OUT) + 2

        def tile_of(h, which):
            return 1 + 10 * h + which

        block = es.enter_context(nc.Block())

        @block.sync
        def _(sp):
            def load_first(c):
                sp.dma_start(raw[:, c, :], stream[c]).then_inc(raw_landed[c], 16)

            load_first(0)
            for i in range(KT // 2):
                half = conv_out if i < KT // 4 else gla_out
                sp.dma_start(half[:, 2 * i % CT:2 * i % CT + 2, :], xT[:, 2 * i:2 * i + 2, :]).then_inc(x_landed[i], 16)
                if i in (1, 4):
                    load_first(1 + i // 4)
            load_first(3)
            body = stream[NRAW:NRAW + (C_HEAD - NRAW) // NRAW * NRAW].rearrange("(i s) p f -> i s p f", s=NRAW)
            with sp.Fori(0, (C_HEAD - NRAW) // NRAW) as i:
                for s in range(NRAW):
                    sp.wait_ge(lo_made, NRAW * i + s + 1)
                    sp.dma_start(raw[:, s, :], body[i, s]).then_inc(raw_landed[s], 16)
            done = NRAW + (C_HEAD - NRAW) // NRAW * NRAW
            for c in range(done, C_HEAD):
                sp.wait_ge(lo_made, c - NRAW + 1)
                sp.dma_start(raw[:, c % NRAW, :], stream[c]).then_inc(raw_landed[c % NRAW], 16)
            gview = gates.rearrange("n p (g e) t -> g e p n t", e=GRP)
            aview = early_acts.rearrange("(g e) p t -> g e p t", e=GRP)

            def load(src, c, s):
                slot = (C_HEAD + s) % NRAW
                sp.wait_ge(lo_made, c - (NRAW - 1))
                sp.dma_start(raw[:, slot, :], src).then_inc(raw_landed[slot], 16)

            def load_gates(g, e):
                sp.wait_ge(s_prod, GRP * g + (e + 1))
                sp.dma_start(gtile[:, e, :].rearrange("p (n t) -> p n t", t=TG), gview[g, e]).then_inc(g_landed[e], 16)

            def load_early(g):
                for e in range(GRP):
                    load_gates(g, e)
                    sp.dma_start(atile[:, e, :], aview[g, e]).then_inc(a_landed[e], 16)

            early = stream[C_EARLY:C_LATE].rearrange("(i s) p f -> i s p f", s=NRAW)
            def load_u(lo, hi):
                with sp.Fori(lo, hi) as i:
                    for s in range(NRAW):
                        load(early[i, s], NRAW * i + (C_EARLY + s), s)

            turns = 2 * EARLY // NRAW
            load_u(0, turns - 1)
            for half in range(2):
                sp.wait_ge(gstored[half], 16 * NTG // 2)
                sp.wait_ge(acts_stored[half], 16 * (EARLY - EARLY_TAIL) // 2)
            load_early(0)
            load_u(turns - 1, turns)
            late = stream[C_LATE:C_MAIN].rearrange("(g s) p f -> g s p f", g=EGRP)
            for s in range(NRAW):
                load(late[0, s], C_LATE + s, s)
            load_early(1)
            for s in range(NRAW, PARTS):
                load(late[0, s], C_LATE + s, s)
            for half in range(2):
                sp.wait_ge(acts_stored[half], 16 * EARLY // 2)
            with sp.Fori(1, EGRP - 1) as g:
                load_early(g + 1)
                for s in range(PARTS):
                    load(late[g, s], PARTS * g + (C_LATE + s), s)
            for s in range(PARTS):
                load(late[EGRP - 1, s], PARTS * (EGRP - 1) + C_LATE + s, s)
            main = stream[C_MAIN:C_ALL].rearrange("(g s) p f -> g s p f", g=NGRP - EGRP)
            with sp.Fori(0, NGRP - EGRP) as g:
                for s in range(C_GRP):
                    load(main[g, s], C_GRP * g + (C_MAIN + s), s)
                    if s % 2 == 0 and s < 2 * GRP:
                        load_gates(g + EGRP, s // 2)
            for i in range(KT // 2):
                sp.wait_ge(y_out, 2 * i + 2)
                sp.dma_start(out[:, 2 * i:2 * i + 2, :], acc[:, 2 * i:2 * i + 2, :]).then_inc(out_stored, 16)
            sp.wait_ge(out_stored, 16 * KT // 2)

        @block.gpsimd
        def _(pool):
            pool.memset(ident[:, :], 0.0)
            pool.memset(causal[:, :, :], 1.0)
            pool.memset(reset[:, :], 1.0)
            pool.memset(eps_col[:, :], EPS)
            pool.memset(mean_of[:, 0, :], 1.0 / DV)
            pool.memset(mean_of[:, 1, :], 1.0 / (CT * P))
            pool.memset(mean_of[:, 2, :], 1.0 / D)
            pool.iota(iota[:, :], pattern=[[1, P]], base=0, channel_multiplier=0,
                      allow_small_or_imprecise_dtypes=True).then_inc(consts, 1)
            pool.wait_ge(consts, 1)
            pool.affine_select(out=ident[:, :], in_=ident[:, :], compare_op=ALU.not_equal, fill=1.0, base=0,
                               pattern=[[-1, P]], channel_multiplier=1)
            pool.memset(reset[:, :].rearrange("p (n c) -> p n c", c=GC)[:, :, 0:1], 0.0)
            pool.affine_select(out=causal[:, :, :], in_=causal[:, :, :], compare_op=ALU.is_ge, fill=0.0,
                               base=0, pattern=[[0, TB], [1, P]], channel_multiplier=-1).then_inc(consts, 1)
            pool.wait_ge(consts, 2)
            pool.memset(causal[0:GC, :, GC:P], 0.0).then_inc(consts, 1)
            pool.wait_ge(consts, 3)

            def split(slot, k, landed, c1):
                pool.wait_ge(chunk_used, c1)
                pool.wait_ge(raw_landed[slot], landed)
                pool.sem_inc(split_begun, 1)
                pool.tensor_scalar(whi[:, k, :], raw[:, slot, :], 1.0, 0.0, ALU.mult, ALU.add).then_inc(hi_made, 1)
                pool.wait_ge(hi_made, c1)
                pool.sem_inc(split_begun, 1)
                pool.tensor_tensor(wlo[:, k, :], raw[:, slot, :], whi[:, k, :].bitcast(F32),
                                   ALU.subtract).then_inc(lo_made, 1)

            def gather(table, n, s, idx):
                pool.wait_ge(rows_used, n + 1)
                pool.sem_inc(split_begun, 1)
                pool.tensor_copy(row_col[:, s:s + 1], idx).then_inc(col_made, 1)
                pool.wait_ge(col_made, n + 1)
                pool.sem_inc(split_begun, 1)
                pool.indirect_dma_start(rows[:, s, :], None, table,
                                        bass.IndirectOffsetOnAxis(ap=row_col[:, s:s + 1], axis=0)).then_inc(rows_landed[s], 16)

            with pool.Fori(0, C_MAIN // NRAW) as i:
                for s in range(NRAW):
                    split(s, s % NSPLIT, 16 * i + 16, NRAW * i + s + 1)
            for c in range(C_MAIN // NRAW * NRAW, C_MAIN):
                split(c % NRAW, c % NSPLIT, 16 * (c // NRAW + 1), c + 1)
            pool.wait_ge(rows_ready, 1)
            numbers = row_idx[:, :].rearrange("p (i s) -> p i s", s=2)
            per = 2 * C_GRP * PAIRS_G // NRAW
            for t, table in enumerate((u_rows, v_rows)):
                with pool.Fori(0, per) as i:
                    for s in range(NRAW):
                        c = C_MAIN + t * 2 * C_GRP * PAIRS_G + s
                        split(c % NRAW, c % NSPLIT, 16 * i + 16 * (c // NRAW + 1), NRAW * i + c + 1)
                        if s % 2 == 1:
                            gather(table, 2 * i + (t * RANKS + s // 2), s // 2, numbers[:, i, s // 2:s // 2 + 1])
            with pool.Fori(0, 2 * C_GRP * (PAIRS - 2 * PAIRS_G) // NRAW) as i:
                for s in range(NRAW):
                    c = C_MAIN + 4 * C_GRP * PAIRS_G + s
                    split(c % NRAW, c % NSPLIT, 16 * i + 16 * (c // NRAW + 1), NRAW * i + c + 1)

        @block.tensor
        def _(pe):
            pe.sem_inc(chunk_used, NSPLIT)

            def tile(c0, bank, wait_x=None, between=None, tokens=T):
                o, hi, lo = ps[:, bank, 0:tokens], xhi[:, :, 0:tokens], xlo[:, :, 0:tokens]
                for half in range(2):
                    if between and half == 1:
                        between()
                    pe.wait_ge(lo_made, c0 + half + 1)
                    for j in range(HALF):
                        k = half * HALF + j
                        if wait_x:
                            pe.wait_ge(wait_x, k + 1)
                        w, wl = whi[:, half, j * P:(j + 1) * P], wlo[:, half, j * P:(j + 1) * P]
                        pe.matmul(o, w, hi[:, k, :], start=(k == 0), stop=False)
                        pe.matmul(o, w, lo[:, k, :], start=False, stop=False)
                        last = pe.matmul(o, wl, hi[:, k, :], start=False, stop=(k == KT - 1))
                        if j == HALF - 1 and half == 0:
                            last.then_inc(chunk_used, 1)
                last.then_inc(chunk_used, 1)

            def tile_n(n, wait_x=None):
                if n >= 2:
                    pe.wait_ge(bank_read[n % 2], n // 2)
                tile(used_by(n) - NSPLIT - 2, n % 2, wait_x)

            pe.wait_ge(consts, 3)
            tile_n(0, x_lo)
            pe.wait_ge(small_landed, 16 * 6)
            for h in range(HEADS):
                if h == 0:
                    pe.wait_ge(a_exp, 1)
                if h >= 1:
                    pe.wait_ge(o_copied, h)
                pe.matmul(ps[:, 7, :], wa2[:, h * P:(h + 1) * P], a_lr[0:16, :], start=True,
                          stop=True).then_inc(z_done, 1)
                for w in (HQ, HK, HV0, HV1):
                    tile_n(tile_of(h, w))
                if h >= 1:
                    pe.wait_ge(rooted, h)
                pe.wait_ge(v_copied, h + 1)
                for j in range(2):
                    for b in range(TB):
                        last = pe.transpose(ps[:, 2 + j, b * P:(b + 1) * P], vT[:, j, b * P:(b + 1) * P], ident[:, :])
                last.then_inc(v_turned, 1)
                tile_n(tile_of(h, HG0))
                pe.wait_ge(qk_scaled, h + 1)
                for b in range(TB):
                    last = pe.transpose(ps[:, 4, b * P:(b + 1) * P], ex[:, 2, b * P:(b + 1) * P], ident[:, :])
                last.then_inc(k_turned, 1)
                for b in range(TB):
                    last = pe.matmul(ps[:, 5, b * P:(b + 1) * P], ex[:, 1, b * P:(b + 1) * P],
                                     ex[:, 0, b * P:(b + 1) * P], start=True, stop=True)
                last.then_inc(scored, 1)
                tile_n(tile_of(h, HC0))
                pe.wait_ge(vtok_copied, h + 1)
                pe.wait_ge(ktok_copied, h + 1)
                pe.wait_ge(masked, h + 1)
                for n in range(NGC - 1):
                    r = slice((n % 2) * GC, (n % 2) * GC + GC)
                    last = pe.matmul(kv_of(n), ktok[r, n // 2, :],
                                     vtok[r, n // 2, :], start=True, stop=True)
                last.then_inc(kv_done, 1)
                tile_n(tile_of(h, HG1))
                pe.wait_ge(states_made, h + 1)
                for j in range(2):
                    for b in range(TB):
                        pe.matmul(ps[:, 6 + j, b * P:(b + 1) * P], vtok[:, b, j * P:(j + 1) * P],
                                  sT[:, b, :], start=True, stop=False)
                        for n in (2 * b, 2 * b + 1):
                            if n == 0:
                                continue
                            last = pe.matmul(ps[:, 6 + j, n * GC:(n + 1) * GC], states[:, n - 1, j * P:(j + 1) * P],
                                             ex[:, 3, n * GC:(n + 1) * GC], start=False, stop=(n % 2 == 1))
                last.then_inc(o_done, 1)
                tile_n(tile_of(h, HC1))
                pe.wait_ge(o_copied, h + 1)
                for j in range(2):
                    last = pe.matmul(ps[:, 2, :], mean_of[:, 0, :], o_sb[:, j, :], start=(j == 0), stop=(j == 1))
                last.then_inc(mean_done, 1)
                tile_n(tile_of(h, HR0))
                pe.wait_ge(squared, h + 1)
                for j in range(2):
                    last = pe.matmul(ps[:, 3, :], mean_of[:, 0, :], osq[:, j, :], start=(j == 0), stop=(j == 1))
                last.then_inc(var_done, 1)
                tile_n(tile_of(h, HR1))

            def out_half(b, i=0, mix=False):
                n, slot = TILES_IN + b, (C_IN + b) % NSPLIT
                pe.wait_ge(bank_read[n % 2], i + n // 2)
                pe.wait_ge(lo_made, 2 * i + (C_IN + b + 1))
                for j in range(HALF):
                    k = b // TILES_OUT * HALF + j
                    if mix:
                        pe.wait_ge(mix_lo, k + 1)
                    w, wl = whi[:, slot, j * P:(j + 1) * P], wlo[:, slot, j * P:(j + 1) * P]
                    pe.matmul(ps[:, n % 2, :], w, xhi[:, k, :], start=(j == 0), stop=False)
                    pe.matmul(ps[:, n % 2, :], w, xlo[:, k, :], start=False, stop=False)
                    last = pe.matmul(ps[:, n % 2, :], wl, xhi[:, k, :], start=False, stop=(j == HALF - 1))
                last.then_inc(chunk_used, 1)

            def out_halves(lo, hi):
                with pe.Fori(0, (hi - lo) // 2) as i:
                    for b in (lo, lo + 1):
                        out_half(b, i)

            out_half(0, mix=True)
            out_halves(1, 5)
            out_half(5)
            for k in range(CT):
                pe.wait_ge(vdec, k + 1)
                last = pe.matmul(ps[:, 2, :], mean_of[:, 1, :], conv_out[:, k, :], start=(k == 0), stop=(k == CT - 1))
            last.then_inc(mean_done, 1)
            for b in range(6, 9):
                out_half(b)
            for k in range(CT):
                pe.wait_ge(squared, HEADS + k + 1)
                pe.matmul(ps[:, 3, :], mean_of[:, 1, :], vT[:, k % 2, :], start=(k == 0),
                          stop=(k == CT - 1)).then_inc(v_turned, 1)
            out_halves(9, TILES_OUT - 1)
            out_half(TILES_OUT - 1)
            out_half(TILES_OUT, mix=True)
            out_halves(TILES_OUT + 1, 2 * TILES_OUT - 1)
            out_half(2 * TILES_OUT - 1)
            pe.wait_ge(pre_made, TILES_OUT)
            pe.matmul(ps[:, 2, :], mean_of[:, 2, :], presum[:, :], start=True, stop=True).then_inc(mean_done, 1)
            for k in range(KT):
                pe.wait_ge(squared, HEADS + CT + k + 1)
                pe.matmul(ps[:, 3, :], mean_of[:, 2, :], lsq[:, k % 2, :], start=(k == 0),
                          stop=(k == KT - 1)).then_inc(v_turned, 1)
            def key_scores(m, i=0):
                pe.wait_ge(qk_copied, 2 * i + (m + 1))
                if m >= 2:
                    pe.wait_ge(s_copied, 2 * i + (m - 1))
                for b in range(TB):
                    last = pe.matmul(ps[:, 2 + m % 2, b * P:(b + 1) * P], qk[:, m % 2, b * P:(b + 1) * P],
                                     subk[:, 2 * i + m, :], start=True, stop=True)
                last.then_inc(s_done, 1)

            def query(m, i=0, wait_x=None):
                n = TILES_IN + 2 * TILES_OUT + m
                pe.wait_ge(bank_read[n % 2], i + n // 2)
                tile(4 * i + (C_IN + C_OUT + 2 * m), n % 2, wait_x)

            query(0, wait_x=h_lo)
            query(1)
            pe.wait_ge(subk_landed, 16)
            key_scores(0)
            query(2)
            key_scores(1)
            with pe.Fori(0, (TILES_Q - 4) // 2) as i:
                for m in (3, 4):
                    query(m, i)
                    key_scores(m - 1, i)
            query(TILES_Q - 1)
            key_scores(TILES_Q - 2)
            key_scores(TILES_Q - 1)
            with pe.Fori(0, EARLY_FREE // 2) as i:
                for e in range(2):
                    pe.wait_ge(u_act, 2 * i + (e + 1))
                    tile(4 * i + (C_EARLY + 2 * e), e, tokens=TD)
            pe.wait_ge(keys_made, 1)
            for i in range(3):
                for b in range(TB):
                    last = pe.transpose(ps[:, 4 + i, b * P:(b + 1) * P], keyf[:, i, b, :], ident[:, :])
            last.then_inc(keys_turned, 1)
            pe.wait_ge(keys_copied, 1)
            pe.sem_inc(g_done, 4)
            per = TG // QB
            et = len(BATCHES) // 2
            with pe.Fori(0, NTG // 2) as i:
                made = [0]

                def batches(n):
                    for _ in range(n):
                        s = made[0] % 4
                        pe.wait_ge(hots_made, 2 * per * i + (made[0] + 1))
                        pe.wait_ge(g_copied, 2 * per * i + (made[0] + 1))
                        for q in range(QB):
                            last = pe.matmul(ps[:, 4 + s, q * P:(q + 1) * P], hotL[:, s, q, :], hotR[:, s, q, :],
                                             start=True, stop=True)
                        last.then_inc(g_done, 1)
                        made[0] += 1

                for e in range(2 * et):
                    pe.wait_ge(u_act, 2 * et * i + (EARLY_FREE + e + 1))
                    tile(4 * et * i + (C_EARLY + 2 * EARLY_FREE + 2 * e), e % 2,
                         between=lambda: batches(BATCHES[2 * e % len(BATCHES)]), tokens=TD)
                    batches(BATCHES[(2 * e + 1) % len(BATCHES)])

            with pe.Fori(0, EARLY_TAIL // 2 - 1) as i:
                for e in range(2):
                    pe.wait_ge(u_act, 2 * i + (EARLY - EARLY_TAIL + e + 1))
                    tile(4 * i + (C_LATE - 2 * EARLY_TAIL + 2 * e), e, tokens=TD)
            pe.wait_ge(h_twice_made, 1)
            for k in range(KT):
                last = pe.transpose(ps[:, 2 + k // 4, k % 4 * P:(k % 4 + 1) * P],
                                    h_twice[:, k, :, :].rearrange("p f t -> p (f t)"), ident[:, :])
            last.then_inc(tok_turned, 1)
            for e in range(2):
                pe.wait_ge(u_act, EARLY - 2 + e + 1)
                tile(C_LATE - 4 + 2 * e, e, tokens=TD)

            def v_parts(g, slot, c0):
                with pe.Fori(0, PARTS // 2) as i:
                    for j in range(2):
                        pe.wait_ge(part_read, PARTS * g + 2 * i + (j + 1))
                        pe.wait_ge(lo_made, c0 + 2 * i + (j + 1))
                        for e in range(GRP):
                            pe.wait_ge(s_lo, GRP * g + (e + 1))
                            for d in range(2):
                                cols = slice((2 * e + d) * P, (2 * e + d + 1) * P)
                                o = ps[:, 2 + 2 * j + d, 0:TD]
                                pe.matmul(o, whi[:, j, cols], shi[:, slot, e, :], start=(e == 0), stop=False)
                                pe.matmul(o, whi[:, j, cols], slo[:, slot, e, :], start=False, stop=False)
                                last = pe.matmul(o, wlo[:, j, cols], shi[:, slot, e, :], start=False, stop=(e == GRP - 1))
                        last.then_inc(chunk_used, 1)

            with pe.Fori(0, EGRP // 2) as gg:
                for slot in range(2):
                    v_parts(2 * gg + slot, slot, 2 * PARTS * gg + (C_LATE + PARTS * slot))
            def pairs(lo, hi):
                with pe.Fori(lo, hi) as gg:
                    for slot in range(2):
                        c0 = 2 * C_GRP * gg + (C_MAIN + C_GRP * slot)
                        with pe.Fori(0, GRP // 2) as i:
                            for e in range(2):
                                pe.wait_ge(u_act, 2 * GRP * gg + 2 * i + (EGRP * GRP + GRP * slot + e + 1))
                                tile(c0 + 4 * i + 2 * e, e, tokens=TD)
                        v_parts(2 * gg + (EGRP + slot), slot, c0 + 2 * GRP)

            pairs(0, 2 * PAIRS_G + 1)
            pe.wait_ge(tok_summed, 1)
            for k in range(KT):
                last = pe.matmul(ps[:, 6 + k // 8, k % 8 * TR:(k % 8 + 1) * TR], tok[:, k * P:(k + 1) * P], fold[:, :],
                                 start=True, stop=True)
            last.then_inc(tok_folded, 1)
            pairs(2 * PAIRS_G + 1, PAIRS)
            pe.wait_ge(y_sum, 1)
            pe.matmul(ps[:, 6, :], mean_of[:, 2, :], tile_sum[:, :], start=True, stop=True).then_inc(mean_done, 1)
            for k in range(KT):
                pe.wait_ge(squared, HEADS + CT + KT + k + 1)
                pe.matmul(ps[:, 7, :], mean_of[:, 2, :], ysq[:, k % 2, :], start=(k == 0),
                          stop=(k == KT - 1)).then_inc(v_turned, 1)

        @block.scalar
        def _(act):
            steps = [0]

            def step(ins):
                steps[0] += 1
                ins.then_inc(act_step, 1)
                act.wait_ge(act_step, steps[0])

            act.dma_start(wa2[:, :], w_a2).then_inc(small_landed, 16)
            act.dma_start(fvec[:, 0:HEADS], b_a).then_inc(small_landed, 16)
            act.dma_start(fvec[:, GG:CB], gla_g).then_inc(small_landed, 16)
            act.dma_start(fvec[:, CB:CB + 3 * CT], vecs_conv).then_inc(small_landed, 16)
            act.dma_start(cw[:, :, :], conv_w).then_inc(small_landed, 16)
            act.dma_start(lnv[:, :, :], ln_vecs).then_inc(small_landed, 16)

            def evacuate(n, out_ap, func=ACT.Copy, **kw):
                act.wait_ge(chunk_used, used_by(n))
                return act.activation(out_ap, ps[:, n % 2, :], func, **kw)

            for i in range(KT):
                act.wait_ge(x_landed[i // 2], 16)
                src = conv_out[:, i, :] if i < CT else gla_out[:, i - CT, :]
                act.activation(xhi[:, i, :], src, ACT.Copy).then_inc(x_hi, 1)
            act.wait_ge(small_landed, 16 * 6)
            evacuate(0, a_lr[:, :]).then_inc(bank_read[0], 1)
            act.wait_ge(bank_read[0], 1)
            act.sem_inc(a_exp, 1)
            for h in range(HEADS):
                def n_of(w):
                    return tile_of(h, w)
                act.wait_ge(z_done, h + 1)
                step(act.activation(t0[:, :], ps[:, 7, :], ACT.Identity, bias=fvec[:, BA + h:BA + h + 1]))
                step(act.activation(t1[:, :], t0[:, :], ACT.Abs))
                step(act.activation(t1[:, :], t1[:, :], ACT.Exp, scale=-1.0))
                act.activation(t1[:, :], t1[:, :], ACT.Ln, bias=1.0).then_inc(z_read, 1)
                act.wait_ge(a_sum, 2 * h + 1)
                act.activation(ex[:, 0, :], d1[:, :], ACT.Exp, scale=1.0 / TAU)
                act.activation(ex[:, 1, :], d1[:, :], ACT.Exp, scale=-1.0 / TAU)
                act.activation(ex[:, 3, :], bcum[:, :], ACT.Exp, scale=1.0 / TAU)
                act.wait_ge(a_sum, 2 * h + 2)
                act.activation(ex[:, 2, :], d2[:, :], ACT.Exp, scale=-1.0 / TAU).then_inc(a_exp, 1)
                evacuate(n_of(HQ), qT[:, :], scale=float(P) ** -0.5).then_inc(bank_read[n_of(HQ) % 2], 1)
                if h >= 1:
                    act.wait_ge(c_ready, 2 * h)
                evacuate(n_of(HK), kT[:, :]).then_inc(bank_read[n_of(HK) % 2], 1)
                evacuate(n_of(HV0), vT[:, 0, :]).then_inc(bank_read[n_of(HV0) % 2], 1)
                evacuate(n_of(HV1), vT[:, 1, :]).then_inc(bank_read[n_of(HV1) % 2], 1)
                act.wait_ge(bank_read[n_of(HV1) % 2], (n_of(HV1)) // 2 + 1)
                act.wait_ge(bank_read[n_of(HV0) % 2], (n_of(HV0)) // 2 + 1)
                act.sem_inc(v_copied, 1)
                act.wait_ge(v_turned, h + 1)
                for j in range(2):
                    last = act.activation(vtok[:, :, j * P:(j + 1) * P],
                                          ps[:, 2 + j, :].rearrange("p (b v) -> p b v", v=P), ACT.Copy)
                last.then_inc(vtok_copied, 1)
                act.wait_ge(qk_scaled, h + 1)
                evacuate(n_of(HG0), sg[:, :], ACT.Sigmoid).then_inc(bank_read[n_of(HG0) % 2], 1)
                act.wait_ge(k_turned, h + 1)
                act.activation(ktok[:, :, :], ps[:, 4, :].rearrange("p (b k) -> p b k", k=P), ACT.Copy).then_inc(ktok_copied, 1)
                act.wait_ge(c_ready, 2 * h + 1)
                evacuate(n_of(HG1), sg[:, :], ACT.Sigmoid).then_inc(bank_read[n_of(HG1) % 2], 1)
                act.wait_ge(o_done, h + 1)
                if h >= 1:
                    act.wait_ge(head_done, h)
                act.activation(o_sb[:, :, :], ps[:, 6:8, :], ACT.Copy).then_inc(o_copied, 1)
                act.wait_ge(centred, h + 1)
                act.activation(osq[:, :, :], o_sb[:, :, :], ACT.Square).then_inc(squared, 1)
                for j in range(2):
                    evacuate(n_of(HR0 + j), srr[:, j, :], ACT.Sigmoid)
                    act.activation(rr[:, j, :], ps[:, n_of(HR0 + j) % 2, :], ACT.Copy).then_inc(bank_read[n_of(HR0 + j) % 2], 1)
                    if j == 0:
                        act.wait_ge(var_done, h + 1)
                        act.activation(rstd[:, :], ps[:, 3, :], ACT.Sqrt, bias=eps_col[:, 0:1]).then_inc(rooted, 1)
                act.wait_ge(bank_read[n_of(HR0) % 2], n_of(HR0) // 2 + 1)
                act.wait_ge(bank_read[n_of(HR1) % 2], n_of(HR1) // 2 + 1)
                act.sem_inc(r_copied, 1)

            for k in range(CT):
                act.wait_ge(head_done, k // 2 + 1)
                act.activation(xhi[:, k, :], gla_out[:, k, :], ACT.Copy).then_inc(mix_hi, 1)
            act.wait_ge(mix_lo, CT)
            for i in range(4):
                act.dma_start(pre[:, 4 * i:4 * i + 4, :], xT[:, 4 * i:4 * i + 4, :]).then_inc(res_landed[i], 16)
            for k in range(CT):
                act.wait_ge(centred, HEADS + k + 1)
                if k >= 2:
                    act.wait_ge(v_turned, HEADS + k - 1)
                act.activation(vT[:, k % 2, :], conv_out[:, k, :], ACT.Square).then_inc(squared, 1)
            act.wait_ge(v_turned, HEADS + CT)
            act.activation(rstd[:, :], ps[:, 3, :], ACT.Sqrt, bias=eps_col[:, 0:1]).then_inc(rooted, 1)
            for k in range(CT):
                act.wait_ge(silu_parts, k + 1)
                if k >= 2:
                    act.wait_ge(mixf, k - 1)
                act.activation(rr[:, k % 2, :], conv_out[:, k, :], ACT.Identity, scale=fvec[:, CG + k:CG + k + 1],
                               bias=fvec[:, CBB + k:CBB + k + 1]).then_inc(r_copied, 1)
                act.activation(srr[:, k % 2, :], conv_out[:, k, :], ACT.Sigmoid, scale=fvec[:, CG + k:CG + k + 1],
                               bias=fvec[:, CBB + k:CBB + k + 1]).then_inc(r_copied, 1)
            for k in range(CT):
                act.wait_ge(mixf, k + 1)
                act.activation(xhi[:, CT + k, :], conv_out[:, k, :], ACT.Copy).then_inc(mix_hi, 1)
            act.activation(warm[:, :], eps_col[:, :], ACT.Sqrt)
            for k in range(KT):
                act.wait_ge(centred, HEADS + CT + k + 1)
                if k >= 2:
                    act.wait_ge(v_turned, HEADS + CT + k - 1)
                act.activation(lsq[:, k % 2, :], pre[:, k, :], ACT.Square).then_inc(squared, 1)
            act.wait_ge(v_turned, HEADS + CT + KT)
            act.activation(rstd[:, :], ps[:, 3, :], ACT.Sqrt, bias=eps_col[:, 0:1]).then_inc(rooted, 1)
            for k in range(KT):
                act.wait_ge(silu_parts, CT + k + 1)
                act.activation(xhi[:, k, :], pre[:, k, :], ACT.Identity, bias=lnv[:, 1, k:k + 1]).then_inc(h_hi, 1)
            def copy_query(m, i=0):
                n = TILES_IN + 2 * TILES_OUT + m
                act.wait_ge(chunk_used, 4 * i + used_by(n))
                if m >= 2:
                    act.wait_ge(s_done, 2 * i + (m - 1))
                act.sem_inc(act_turn, 1)
                act.activation(qk[:, m % 2, :], ps[:, n % 2, :], ACT.Copy).then_inc(bank_read[n % 2], 1)
                act.wait_ge(bank_read[n % 2], i + (n // 2 + 1))
                act.sem_inc(qk_copied, 1)

            def copy_scores(m, i=0):
                act.wait_ge(s_done, 2 * i + (m + 1))
                act.sem_inc(act_turn, 1)
                act.activation(score[:, 2 * i + m, :, :], ps[:, 2 + m % 2, :].rearrange("p (b k) -> p b k", k=NK),
                               ACT.Copy).then_inc(s_copied, 1)

            act.wait_ge(h_lo, KT)
            act.dma_start(subk[:, :, :], sub_k).then_inc(subk_landed, 16)
            copy_query(0)
            for m in (1, 2):
                copy_query(m)
                copy_scores(m - 1)
            with act.Fori(0, (TILES_Q - 4) // 2) as i:
                for m in (3, 4):
                    copy_query(m, i)
                    copy_scores(m - 1, i)
            copy_query(TILES_Q - 1)
            for m in (TILES_Q - 2, TILES_Q - 1):
                copy_scores(m)
            act.sem_inc(u_act, 2)

            def early_gelu(t, turn, e):
                act.wait_ge(chunk_used, 2 * t + (NSPLIT + C_EARLY + 2))
                if turn is not None:
                    act.wait_ge(acts_stored[e], turn)
                act.sem_inc(act_turn, 1)
                act.activation(act_u[:, e, :], ps[:, e, 0:TD], ACT.Gelu).then_inc(u_act, 1)
                act.wait_ge(u_act, t + 3)
                act.sem_inc(act_turn, 1)

            for t in range(2):
                early_gelu(t, None, t)
                act.dma_start(early_acts[t], act_u[:, t, :]).then_inc(acts_stored[t], 16)
            act.wait_ge(sc_sub, 1)
            act.activation(gexp[:, :, :], best[:, :, :], ACT.Exp).then_inc(sc_exp, 1)
            first = early_acts[0:EARLY_FREE].rearrange("(i e) p t -> i e p t", e=2)
            with act.Fori(1, EARLY_FREE // 2) as i:
                for e in range(2):
                    early_gelu(2 * i + e, 16 * i, e)
                    act.dma_start(first[i, e], act_u[:, e, :]).then_inc(acts_stored[e], 16)
            act.wait_ge(keys_turned, 1)
            act.activation(keyT[:, :, :], ps[:, 4:7, :], ACT.Copy).then_inc(keys_copied, 1)
            act.wait_ge(keys_copied, 1)
            act.sem_inc(g_copied, 4)
            act.wait_ge(chosen_made, 1)
            for f in range(FOLD):
                act.dma_start(row_f[f * TR:(f + 1) * TR, :, :],
                              chosen[P - TR:P, :, f * RANKS:(f + 1) * RANKS]).then_inc(row_f_landed, 16)
            per = TG // QB
            et = len(BATCHES) // 2
            rest = early_acts[EARLY_FREE:EARLY - EARLY_TAIL].rearrange("(i e) p t -> i e p t", e=2 * et)
            blocks = gates.rearrange("(i half) p k t -> i half p k t", half=2)

            def gate_stages(i, first_turn):
                made = [0]

                def batches(n):
                    for _ in range(n):
                        b = made[0]
                        half, q0 = b // per, b % per * QB
                        if b % per == 0 and not first_turn:
                            act.wait_ge(gstored[half], 16 * i)
                        act.wait_ge(g_done, 2 * per * i + (b + 5))
                        act.sem_inc(act_turn, 1)
                        act.activation(gstage[:, half, :, q0:q0 + QB], ps[:, 4 + b % 4, :].rearrange("p (q k) -> p k q", q=QB),
                                       ACT.Copy).then_inc(g_copied, 1)
                        made[0] += 1
                        if made[0] % per == 0:
                            act.wait_ge(g_copied, 2 * per * i + (made[0] + 4))
                            act.dma_start(blocks[i, half], gstage[:, half, :, :]).then_inc(gstored[half], 16)

                for e in range(2 * et):
                    batches(BATCHES[2 * e % len(BATCHES)])
                    early_gelu(2 * et * i + (EARLY_FREE + e), 16 * et * i + 16 * (EARLY_FREE // 2 + e // 2), e % 2)
                    act.dma_start(rest[i, e], act_u[:, e % 2, :]).then_inc(acts_stored[e % 2], 16)
                    batches(BATCHES[(2 * e + 1) % len(BATCHES)])

            def round_s(g, slot, e):
                act.wait_ge(s_prod, GRP * g + (e + GRP + 1))
                act.sem_inc(act_turn, 1)
                act.activation(shi[:, slot, e, :], s_f[:, e % 2, :], ACT.Copy).then_inc(s_hi, 1)

            gate_stages(0, True)
            with act.Fori(1, NTG // 2) as i:
                gate_stages(i, False)
            tail = early_acts[EARLY - EARLY_TAIL:EARLY].rearrange("(i e) p t -> i e p t", e=2)
            with act.Fori(0, EARLY_TAIL // 2 - 1) as i:
                for e in range(2):
                    early_gelu(2 * i + (EARLY - EARLY_TAIL + e), 16 * i + 16 * (EARLY - EARLY_TAIL) // 2, e)
                    act.dma_start(tail[i, e], act_u[:, e, :]).then_inc(acts_stored[e], 16)
            act.wait_ge(tok_turned, 1)
            act.activation(tok[:, :].rearrange("p (j t) -> p j t", j=4), ps[:, 2:6, :], ACT.Copy).then_inc(tok_copied, 1)
            for e in range(2):
                if e == 1:
                    for half in range(2):
                        act.wait_ge(gstored[half], 16 * NTG // 2)
                    for t in range(GRP):
                        round_s(0, 0, t)
                early_gelu(EARLY - 2 + e, 16 * (EARLY // 2 - 1), e)
                act.dma_start(early_acts[EARLY - 2 + e], act_u[:, e, :]).then_inc(acts_stored[e], 16)
            for e in range(GRP):
                round_s(1, 1, e)
            with act.Fori(1, EGRP // 2) as gg:
                for slot in range(2):
                    act.wait_ge(chunk_used, 2 * PARTS * gg + (NSPLIT + C_LATE + PARTS * (slot - 1)))
                    for e in range(GRP):
                        round_s(2 * gg + slot, slot, e)
            def pairs(lo, hi):
                with act.Fori(lo, hi) as gg:
                    for slot in range(2):
                        for e in range(GRP):
                            idx = 2 * GRP * gg + (EGRP * GRP + GRP * slot + e)
                            act.wait_ge(chunk_used, 2 * C_GRP * gg + (NSPLIT + C_MAIN + C_GRP * slot + 2 * e + 2))
                            act.wait_ge(s_prod, idx + (GRP - 1))
                            act.sem_inc(act_turn, 1)
                            act.activation(act_u[:, e % 2, :], ps[:, e % 2, 0:TD], ACT.Gelu).then_inc(u_act, 1)
                            round_s(2 * gg + (EGRP + slot), slot, e)

            for half in range(2):
                act.wait_ge(acts_stored[half], 16 * EARLY // 2)
            pairs(0, PAIRS_G)
            act.wait_ge(dots_kept, 2 * PAIRS_G)
            act.activation(row_dot[:, :], row_dot[:, :], ACT.Gelu).then_inc(dots_gelu, 1)
            pairs(PAIRS_G, PAIRS)
            act.activation(warm[:, :], eps_col[:, :], ACT.Sqrt)
            for k in range(KT):
                act.wait_ge(centred, HEADS + CT + KT + k + 1)
                if k >= 2:
                    act.wait_ge(v_turned, HEADS + CT + KT + k - 1)
                act.activation(ysq[:, k % 2, :], acc[:, k, :], ACT.Square).then_inc(squared, 1)
            act.wait_ge(v_turned, HEADS + CT + 2 * KT)
            act.activation(rstd[:, :], ps[:, 7, :], ACT.Sqrt, bias=eps_col[:, 0:1]).then_inc(rooted, 1)
            for k in range(KT):
                act.wait_ge(y_sum, k + 2)
                act.activation(acc[:, k, :], acc[:, k, :], ACT.Identity, bias=lnv[:, 3, k:k + 1]).then_inc(y_out, 1)

        @block.vector
        def _(dve):
            steps = [0]

            def step(ins):
                steps[0] += 1
                ins.then_inc(dve_step, 1)
                dve.wait_ge(dve_step, steps[0])

            for i in range(KT):
                dve.wait_ge(x_hi, i + 1)
                src = conv_out[:, i, :] if i < CT else gla_out[:, i - CT, :]
                dve.tensor_tensor(xlo[:, i, :], src, xhi[:, i, :].bitcast(F32), ALU.subtract).then_inc(x_lo, 1)
            dve.wait_ge(x_lo, KT)
            dve.wait_ge(small_landed, 16 * 6)
            dve.wait_ge(consts, 3)
            dve.memset(cpad[:, :, 0:TAPS - 1], 0.0)
            step(dve.memset(sT[:, :, :], 0.0))

            def chunks(a):
                return a.rearrange("p (n c) -> p n c", c=GC)

            def conv(m, j, lo=0, hi=TAPS):
                acc_c = conv_out[:, m, :]
                if lo == 0:
                    step(dve.tensor_scalar(acc_c, cpad[:, j, 0:T], cw[:, m, 0:1], fvec[:, CB + m:CB + m + 1],
                                           ALU.mult, ALU.add))
                for k in range(max(lo, 1), hi):
                    ins = dve.scalar_tensor_tensor(out=acc_c, in0=cpad[:, j, k:k + T], scalar=cw[:, m, k:k + 1],
                                                   in1=acc_c, op0=ALU.mult, op1=ALU.add)
                    if k < TAPS - 1:
                        step(ins)
                if hi == TAPS:
                    ins.then_inc(vdec, 1)
                    dve.wait_ge(vdec, m + 1)

            for h in range(HEADS):
                def n_of(w):
                    return tile_of(h, w)
                dve.wait_ge(z_read, h + 1)
                step(dve.scalar_tensor_tensor(out=t1[:, :], in0=t0[:, :], scalar=0.0, in1=t1[:, :],
                                              op0=ALU.min, op1=ALU.subtract))
                step(dve.tensor_tensor_scan(bcum[:, :], reset[:, :], t1[:, :], 0.0, ALU.mult, ALU.add))
                b3 = chunks(bcum[:, :])
                dve.tensor_tensor(chunks(d1[:, :]), b3, b3[:, :, GC // 2:GC // 2 + 1].to_broadcast([P, NGC, GC]),
                                  ALU.subtract).then_inc(a_sum, 1)
                dve.tensor_tensor(chunks(d2[:, :]), b3, b3[:, :, GC - 1:GC].to_broadcast([P, NGC, GC]),
                                  ALU.subtract).then_inc(a_sum, 1)
                dve.wait_ge(a_exp, h + 2)
                dve.wait_ge(bank_read[n_of(HQ) % 2], n_of(HQ) // 2 + 1)
                dve.wait_ge(bank_read[n_of(HK) % 2], n_of(HK) // 2 + 1)
                step(dve.tensor_copy(d1[:, 0:NGC], chunks(ex[:, 3, :])[:, :, GC - 1]))
                for i, src in ((0, qT), (1, kT), (2, kT), (3, qT)):
                    last = dve.tensor_tensor(ex[:, i, :], ex[:, i, :], src[:, :], ALU.mult)
                last.then_inc(qk_scaled, 1)
                dve.wait_ge(scored, h + 1)
                dve.copy_predicated(sT[:, :, :], causal[:, :, :].bitcast(U32),
                                    ps[:, 5, :].rearrange("p (b q) -> p b q", q=P)).then_inc(masked, 1)
                def gated(j, w):
                    dve.wait_ge(chunk_used, used_by(n_of(w)))
                    dve.wait_ge(bank_read[n_of(w - 1) % 2], n_of(w - 1) // 2 + 1)
                    dve.tensor_tensor(cpad[:, j, TAPS - 1:], ps[:, n_of(w) % 2, :], sg[:, :],
                                      ALU.mult).then_inc(bank_read[n_of(w) % 2], 1)
                    dve.wait_ge(bank_read[n_of(w) % 2], n_of(w) // 2 + 1)
                    dve.sem_inc(c_ready, 1)
                gated(0, HC0)
                dve.wait_ge(kv_done, h + 1)
                for n in range(NGC - 1):
                    kv = kv_of(n)
                    if n == 0:
                        step(dve.tensor_copy(states[:, 0, :], kv))
                    else:
                        ins = dve.scalar_tensor_tensor(out=states[:, n, :], in0=states[:, n - 1, :],
                                                       scalar=d1[:, n:n + 1], in1=kv, op0=ALU.mult, op1=ALU.add)
                        if n < NGC - 2:
                            step(ins)
                ins.then_inc(states_made, 1)
                conv(2 * h, 0)
                gated(1, HC1)
                dve.wait_ge(mean_done, h + 1)
                dve.wait_ge(o_copied, h + 1)
                for j in range(2):
                    last = dve.tensor_tensor(o_sb[:, j, :], o_sb[:, j, :], ps[:, 2, :], ALU.subtract)
                last.then_inc(centred, 1)
                ends = (CUT1, CUT2) if h == HEADS - 1 else (TAPS, TAPS)
                conv(2 * h + 1, 1, 0, ends[0])
                dve.wait_ge(rooted, h + 1)
                step(dve.reciprocal(rstd[:, :], rstd[:, :]))
                dve.wait_ge(centred, h + 1)
                for j in range(2):
                    last = dve.scalar_tensor_tensor(out=o_sb[:, j, :], in0=o_sb[:, j, :],
                                                    scalar=fvec[:, GG + 2 * h + j:GG + 2 * h + j + 1],
                                                    in1=rstd[:, :], op0=ALU.mult, op1=ALU.mult)
                step(last)
                if h == HEADS - 1:
                    conv(2 * h + 1, 1, *ends)
                dve.wait_ge(r_copied, h + 1)
                step(dve.tensor_tensor(rr[:, :, :], rr[:, :, :], srr[:, :, :], ALU.mult))
                dve.tensor_tensor(gla_out[:, 2 * h:2 * h + 2, :], o_sb[:, :, :], rr[:, :, :],
                                  ALU.mult).then_inc(head_done, 1)

            def centre(buf, k):
                dve.tensor_tensor(buf[:, k, :], buf[:, k, :], ps[:, 2, :], ALU.subtract).then_inc(centred, 1)

            def split_mix(k):
                dve.wait_ge(mix_hi, k + 1)
                src = gla_out[:, k, :] if k < CT else conv_out[:, k - CT, :]
                dve.tensor_tensor(xlo[:, k, :], src, xhi[:, k, :].bitcast(F32), ALU.subtract).then_inc(mix_lo, 1)

            def add_half(m):
                n = TILES_IN + m
                dve.wait_ge(chunk_used, used_by(n))
                dve.wait_ge(res_landed[m // 4], 16)
                dve.scalar_tensor_tensor(out=pre[:, m, :], in0=pre[:, m, :], scalar=ALPHA, in1=ps[:, n % 2, :],
                                         op0=ALU.mult, op1=ALU.add).then_inc(bank_read[n % 2], 1)

            for k in range(CT):
                split_mix(k)
            conv(2 * HEADS - 1, 1, CUT2)
            for hm in range(0, 6):
                add_half(hm)
            dve.wait_ge(mean_done, HEADS + 1)
            for k in range(CT):
                centre(conv_out, k)
            for hm in range(6, 9):
                add_half(hm)
            dve.wait_ge(rooted, HEADS + 1)
            step(dve.reciprocal(rstd[:, :], rstd[:, :]))
            for k in range(CT):
                dve.wait_ge(squared, HEADS + k + 1)
                dve.tensor_tensor(conv_out[:, k, :], conv_out[:, k, :], rstd[:, :], ALU.mult).then_inc(silu_parts, 1)
            for k in range(CT):
                dve.wait_ge(r_copied, HEADS + 2 * k + 2)
                dve.tensor_tensor(conv_out[:, k, :], rr[:, k % 2, :], srr[:, k % 2, :], ALU.mult).then_inc(mixf, 1)
                if k % 2 == 1 and 9 + k // 2 < 12:
                    add_half(9 + k // 2)
            for k in range(CT, KT):
                split_mix(k)
                if k % 2 == 1 and 12 + (k - CT) // 2 < TILES_OUT:
                    add_half(12 + (k - CT) // 2)
            def finish(m, i=0):
                n = TILES_IN + TILES_OUT + m
                dve.wait_ge(chunk_used, 2 * i + used_by(n))
                dve.tensor_tensor(pre[:, 2 * i + m, :], pre[:, 2 * i + m, :], ps[:, n % 2, :],
                                  ALU.add).then_inc(bank_read[n % 2], 1)
                dve.wait_ge(bank_read[n % 2], i + (n // 2 + 1))
                if m == 0:
                    dve.tensor_copy(presum[:, :], pre[:, 0, :]).then_inc(pre_made, 1)
                else:
                    dve.wait_ge(pre_made, 2 * i + m)
                    dve.tensor_tensor(presum[:, :], presum[:, :], pre[:, 2 * i + m, :], ALU.add).then_inc(pre_made, 1)

            finish(0)
            with dve.Fori(0, (TILES_OUT - 2) // 2) as i:
                for m in (1, 2):
                    finish(m, i)
            finish(TILES_OUT - 1)

            def rest_of_h(k):
                dve.wait_ge(h_hi, k + 1)
                dve.scalar_tensor_tensor(out=xlo[:, k, :], in0=pre[:, k, :], scalar=lnv[:, 1, k:k + 1],
                                         in1=xhi[:, k, :].bitcast(F32), op0=ALU.add, op1=ALU.subtract).then_inc(h_lo, 1)

            dve.wait_ge(mean_done, HEADS + 2)
            for k in range(KT):
                centre(pre, k)
            dve.wait_ge(rooted, HEADS + 2)
            step(dve.reciprocal(rstd[:, :], rstd[:, :]))
            for k in range(KT):
                dve.wait_ge(squared, HEADS + CT + k + 1)
                dve.scalar_tensor_tensor(out=pre[:, k, :], in0=pre[:, k, :], scalar=lnv[:, 0, k:k + 1],
                                         in1=rstd[:, :], op0=ALU.mult, op1=ALU.mult).then_inc(silu_parts, 1)
                if k >= 1:
                    rest_of_h(k - 1)
            rest_of_h(KT - 1)

            def top16(src, spare, vals, idx):
                step(dve.max(vals[:, 0:8], src))
                dve.max_index(idx[:, 0:8], vals[:, 0:8], src)
                step(dve.match_replace(spare, vals[:, 0:8], src, LOWEST))
                step(dve.max(vals[:, 8:16], spare))
                step(dve.max_index(idx[:, 8:16], vals[:, 8:16], spare))

            dve.wait_ge(h_lo, KT)
            for m in range(TILES_Q):
                dve.wait_ge(s_copied, m + 1)
                for b in range(TB):
                    top16(score[:, m, b, :], cut[:, :], topv[:, b, m, :], topi[:, b, m, :])
                if m % 2 == 0:
                    continue
                h = m // 2
                for b in range(TB):
                    step(dve.tensor_tensor(cand[:, :].rearrange("p (i j) -> p i j", j=TOPK),
                                           topv[:, b, m - 1, :].unsqueeze(2).to_broadcast([P, TOPK, TOPK]),
                                           topv[:, b, m, :].unsqueeze(1).to_broadcast([P, TOPK, TOPK]), ALU.add))
                    r = slice(h * TOPK, (h + 1) * TOPK)
                    top16(cand[:, :], cut2[:, :], best[:, b, r], posi[:, b, r])
            b3 = best[:, :, :].rearrange("p b (h k) -> p (b h) k", k=TOPK)
            step(dve.tensor_copy(gsum[:, :, :], b3[:, :, 0:1]))
            dve.tensor_tensor(b3, b3, gsum[:, :, :].to_broadcast([P, TB * PH, TOPK]), ALU.subtract).then_inc(sc_sub, 1)
            step(dve.tensor_copy(topf[:, :, :, :], topi[:, :, :, :]))
            for half in range(2):
                if half == 0:
                    step(dve.tensor_single_scalar(posx[:, :, :], posi[:, :, :], 4, ALU.logical_shift_right))
                else:
                    step(dve.tensor_single_scalar(posx[:, :, :], posi[:, :, :], TOPK - 1, ALU.bitwise_and))
                step(dve.tensor_copy(posf[:, :, :], posx[:, :, :]))
                for b in range(TB):
                    step(dve.tensor_tensor(pick[:, :, :], posf[:, b, :].unsqueeze(2).to_broadcast([P, PH * TOPK, TOPK]),
                                           iota[:, 0:TOPK].unsqueeze(1).to_broadcast([P, PH * TOPK, TOPK]), ALU.is_equal))
                    p4 = pick[:, :, :].rearrange("p (h k) j -> p h k j", k=TOPK)
                    keys = topf[:, b, :, :].rearrange("p (h two) j -> p h two j", two=2)[:, :, half, :]
                    step(dve.tensor_tensor(p4, p4, keys.unsqueeze(2).to_broadcast([P, PH, TOPK, TOPK]), ALU.mult))
                    step(dve.tensor_reduce(keyf[:, half, b, :], pick[:, :, :], AX.X, ALU.add))
            dve.wait_ge(sc_exp, 1)
            e3 = gexp[:, :, :].rearrange("p b (h k) -> p (b h) k", k=TOPK)
            step(dve.tensor_reduce(gsum[:, :, 0], e3, AX.X, ALU.add))
            step(dve.reciprocal(gsum[:, :, 0], gsum[:, :, 0]))
            dve.tensor_tensor(keyf[:, 2, :, :].rearrange("p b (h k) -> p (b h) k", k=TOPK), e3,
                              gsum[:, :, :].to_broadcast([P, TB * PH, TOPK]), ALU.mult).then_inc(keys_made, 1)
            dve.wait_ge(keys_made, 1)
            dve.scalar_tensor_tensor(out=chosen[:, 0, :], in0=keyf[:, 0, TB - 1, :], scalar=float(NK),
                                     in1=keyf[:, 1, TB - 1, :], op0=ALU.mult, op1=ALU.add)
            dve.tensor_copy(chosen[:, 1, :], keyf[:, 2, TB - 1, :]).then_inc(chosen_made, 1)
            dve.tensor_tensor(fold[:, :], ident[:, 0:TR], ident[:, TR:2 * TR], ALU.add)
            dve.wait_ge(keys_copied, 1)
            kv4 = keyT[:, :, :].rearrange("p c (i s q) -> p c i s q", s=4, q=QB)
            with dve.Fori(0, TD // (4 * QB)) as i:
                for s in range(4):
                    dve.wait_ge(g_done, 4 * i + (s + 1))
                    for q in range(QB):
                        dve.tensor_scalar(hotL[:, s, q, :], iota[:, :], kv4[:, 0, i, s, q:q + 1],
                                          kv4[:, 2, i, s, q:q + 1], ALU.is_equal, ALU.mult)
                        last = dve.tensor_scalar(hotR[:, s, q, :], iota[:, :], kv4[:, 1, i, s, q:q + 1], None, ALU.is_equal)
                    last.then_inc(hots_made, 1)
            for half in range(2):
                dve.wait_ge(gstored[half], 16 * NTG // 2)
            dve.sem_inc(s_prod, GRP)
            for f in range(FOLD):
                last = dve.tensor_tensor(h_twice[:, :, f, :], xhi[:, :, TD:T].bitcast(F32),
                                         xlo[:, :, TD:T].bitcast(F32), ALU.add)
            last.then_inc(h_twice_made, 1)
            dve.wait_ge(row_f_landed, 16 * FOLD)
            dve.tensor_copy(row_idx[:, :], row_f[:, 0, :]).then_inc(rows_ready, 1)
            for k in range(KT):
                last = dve.tensor_scalar(acc[:, k, :], xhi[:, k, :].bitcast(F32), ALPHA, None, ALU.mult)
            step(last)
            for k in range(KT):
                last = dve.scalar_tensor_tensor(out=acc[:, k, :], in0=xlo[:, k, :].bitcast(F32), scalar=ALPHA,
                                                in1=acc[:, k, :], op0=ALU.mult, op1=ALU.add)
            last.then_inc(acc_ready, 1)
            dve.wait_ge(acc_ready, 1)
            dve.wait_ge(tok_copied, 1)
            dve.sem_inc(part_read, 2)

            def multiply(g, e, src):
                dve.wait_ge(g_landed[e], 16 * g + 16)
                dve.tensor_tensor(s_f[:, e % 2, :], src, gtile[:, e, :], ALU.mult).then_inc(s_prod, 1)

            def rest_of_s(g, slot, e):
                dve.wait_ge(s_hi, GRP * g + (e + 1))
                dve.tensor_tensor(slo[:, slot, e, :], s_f[:, e % 2, :], shi[:, slot, e, :].bitcast(F32),
                                  ALU.subtract).then_inc(s_lo, 1)

            def add_part(j, used):
                dve.wait_ge(chunk_used, used)
                dve.tensor_tensor(acc[:, 2 * j:2 * j + 2, 0:TD], acc[:, 2 * j:2 * j + 2, 0:TD],
                                  ps[:, 2 + 2 * (j % 2):4 + 2 * (j % 2), 0:TD], ALU.add).then_inc(part_read, 1)

            def early_s(g, slot, e):
                dve.wait_ge(a_landed[e], 16 * g + 16)
                multiply(g, e, atile[:, e, :])
                rest_of_s(g, slot, e)

            for e in range(GRP):
                early_s(0, 0, e)
            with dve.Fori(0, EGRP // 2 - 1) as gg:
                for slot in range(2):
                    for j in range(PARTS):
                        add_part(j, 2 * PARTS * gg + (NSPLIT + C_LATE + PARTS * slot + j + 1))
                        if j < GRP:
                            early_s(2 * gg + (slot + 1), 1 - slot, j)
            for slot in range(2):
                for j in range(PARTS):
                    add_part(j, PARTS * (EGRP - 2 + slot) + (NSPLIT + C_LATE + j + 1))
                    if j < GRP and slot == 0:
                        early_s(EGRP - 1, 1, j)
                if slot == 0:
                    dve.sem_inc(rows_used, 2)
            weight = row_dot[:, :].rearrange("p (g n) -> p g n", n=2 * ROWS_GRP)

            def dot(gg, r):
                dve.wait_ge(rows_landed[r % 2], 16 * ROWS_GRP * gg + 16 * (r // 2 + 1))
                dve.tensor_tensor_reduce(rows[:, r % 2, :], rows[:, r % 2, :], tok[:, :], 1.0, 0.0, ALU.mult, ALU.add,
                                         accum_out=dot_buf[:, r % ROWS_GRP:r % ROWS_GRP + 1]).then_inc(rows_used, 1)

            def add_row(gg, r):
                dve.wait_ge(rows_landed[r % 2], 16 * ROWS_GRP * gg + 16 * (r // 2 + 1))
                dve.wait_ge(rows_used, 2 * ROWS_GRP * gg + (r + 2))
                dve.scalar_tensor_tensor(out=tok[:, :], in0=rows[:, r % 2, :], scalar=weight[:, gg - PAIRS_G, r:r + 1],
                                         in1=tok[:, :], op0=ALU.mult, op1=ALU.add).then_inc(rows_used, 1)

            def sum_tiles(j):
                dve.wait_ge(part_read, NGRP * PARTS + 2 - PARTS + (j + 1))
                if j == 0:
                    step(dve.tensor_tensor(tile_sum[:, :], acc[:, 0, :], acc[:, 1, :], ALU.add))
                    return
                for k in (2 * j, 2 * j + 1):
                    step(dve.tensor_tensor(tile_sum[:, :], tile_sum[:, :], acc[:, k, :], ALU.add))

            def pairs(lo, hi, use_row=None, keep=False, final=False):
                with dve.Fori(lo, hi) as gg:
                    for slot in range(2):
                        for e in range(GRP):
                            g = 2 * gg + (EGRP + slot)
                            dve.wait_ge(u_act, 2 * GRP * gg + (EGRP * GRP + GRP * slot + e + 3))
                            multiply(g, e, act_u[:, e % 2, :])
                            rest_of_s(g, slot, e)
                            if use_row:
                                use_row(gg, slot * ROWS_GRP + e)
                        for j in range(PARTS):
                            add_part(j, 2 * C_GRP * gg + (NSPLIT + C_MAIN + C_GRP * slot + 2 * GRP + j + 1))
                            if final and slot == 1:
                                sum_tiles(j)
                            if use_row and j % 2 == 1:
                                use_row(gg, slot * ROWS_GRP + GRP + j // 2)
                        if keep:
                            dve.wait_ge(rows_used, 2 * ROWS_GRP * gg + (ROWS_GRP * (slot + 1) + 2))
                            dve.tensor_copy(weight[:, gg, slot * ROWS_GRP:(slot + 1) * ROWS_GRP],
                                            dot_buf[:, :]).then_inc(dots_kept, 1)
                            dve.wait_ge(dots_kept, 2 * gg + (slot + 1))

            pairs(0, PAIRS_G, dot, keep=True)
            dve.memset(tok[:, :], 0.0)
            dve.wait_ge(dots_gelu, 1)
            step(dve.tensor_tensor(row_dot[:, :], row_dot[:, :], row_f[:, 1, :], ALU.mult))
            pairs(PAIRS_G, 2 * PAIRS_G, add_row)
            dve.wait_ge(rows_used, 2 * RANKS + 2)
            dve.sem_inc(tok_summed, 1)
            pairs(2 * PAIRS_G, 2 * PAIRS_G + 1)
            dve.wait_ge(tok_folded, 1)
            step(dve.tensor_tensor(acc[:, :, TD:T], acc[:, :, TD:T],
                                   ps[:, 6:8, :].rearrange("p j (k t) -> p (j k) t", t=TR), ALU.add))
            pairs(2 * PAIRS_G + 1, PAIRS - 1)
            pairs(PAIRS - 1, PAIRS, final=True)
            dve.sem_inc(y_sum, 1)
            dve.wait_ge(mean_done, HEADS + 3)
            for k in range(KT):
                dve.tensor_tensor(acc[:, k, :], acc[:, k, :], ps[:, 6, :], ALU.subtract).then_inc(centred, 1)
            dve.wait_ge(rooted, HEADS + 3)
            step(dve.reciprocal(rstd[:, :], rstd[:, :]))
            for k in range(KT):
                dve.wait_ge(squared, HEADS + CT + KT + k + 1)
                dve.scalar_tensor_tensor(out=acc[:, k, :], in0=acc[:, k, :], scalar=lnv[:, 2, k:k + 1],
                                         in1=rstd[:, :], op0=ALU.mult, op1=ALU.mult).then_inc(y_sum, 1)


def pack(w):
    m = w.shape[1] // P
    return w.reshape(2, HALF, P, m, P).transpose(3, 0, 2, 1, 4).reshape(2 * m, P, CHUNK)


def halves(chunks):
    return np.concatenate([chunks[0::2], chunks[1::2]])


def pack_tables(u, v):
    u = u.reshape(NK, NGRP, GRP, 2, HALF, P).transpose(1, 2, 3, 5, 4, 0).reshape(NGRP, 2 * GRP, P, CHUNK)
    v = v.reshape(NK, NGRP, GRP, PARTS, 2 * P).transpose(1, 3, 0, 2, 4).reshape(NGRP, PARTS, P, CHUNK)
    parts = [u[:EGRP], v[:EGRP], np.concatenate([u[EGRP:], v[EGRP:]], axis=1)]
    return np.concatenate([p.reshape(-1, P, CHUNK) for p in parts])


def columns(v):
    return v.reshape(-1, P).T


def mixer_order(w_in):
    q, k, v, r, a, c_val, c_gate = np.split(w_in, [512, 1024, 2048, 3072, 3088, 4112], axis=1)
    tiles = [a, np.zeros((D, P - a.shape[1]), w_in.dtype)]
    for h in range(HEADS):
        tiles += [q[:, h * P:(h + 1) * P], k[:, h * P:(h + 1) * P], v[:, h * DV:(h + 1) * DV]]
        for m in (2 * h, 2 * h + 1):
            tiles += [c_gate[:, m * P:(m + 1) * P], c_val[:, m * P:(m + 1) * P]]
        tiles.append(r[:, h * DV:(h + 1) * DV])
    return np.concatenate(tiles, axis=1)


def kernel(x, w_in, w_a2, b_a, gla_norm_g, conv_w, conv_b, conv_ln_g, conv_ln_b, w_out,
           ln1_g, ln1_b, w_q, sub_k1, sub_k2, u_tab, v_tab, ln2_g, ln2_b):
    import concourse.bacc as bacc
    from concourse.bass_utils import run_bass_kernel_spmd

    a = {k: np.asarray(v)[0] for k, v in dict(
        x=x, w_in=w_in, w_a2=w_a2, b_a=b_a, gla_norm_g=gla_norm_g, conv_w=conv_w, conv_b=conv_b,
        conv_ln_g=conv_ln_g, conv_ln_b=conv_ln_b, w_out=w_out, ln1_g=ln1_g, ln1_b=ln1_b, w_q=w_q,
        sub_k1=sub_k1, sub_k2=sub_k2, u_tab=u_tab, v_tab=v_tab, ln2_g=ln2_g, ln2_b=ln2_b).items()}
    data = {
        "stream": np.concatenate([pack(mixer_order(a["w_in"])), halves(pack(a["w_out"])), pack(a["w_q"]),
                                  pack_tables(a["u_tab"], a["v_tab"])]),
        "xT": a["x"].T.reshape(KT, P, T).transpose(1, 0, 2),
        "w_a2": a["w_a2"],
        "b_a": columns(a["b_a"]),
        "conv_w": a["conv_w"].T.reshape(CT, P, TAPS).transpose(1, 0, 2),
        "vecs_conv": np.concatenate([columns(a[k]) for k in ("conv_b", "conv_ln_g", "conv_ln_b")], axis=1),
        "gla_g": columns(a["gla_norm_g"]),
        "ln_vecs": np.stack([columns(a[k]) for k in ("ln1_g", "ln1_b", "ln2_g", "ln2_b")], axis=1),
        "sub_k": np.stack([a["sub_k1"], a["sub_k2"]], axis=1).reshape(2 * PH, NK, P).transpose(2, 0, 1),
        "u_rows": a["u_tab"],
        "v_rows": a["v_tab"],
    }
    nc = bacc.Bacc("TRN2", target_bir_lowering=False, num_devices=1)
    data = {k: np.ascontiguousarray(v) for k, v in data.items()}
    args = [nc.dram_tensor(k, v.shape, mybir.dt.from_np(v.dtype), kind="ExternalInput").ap()
            for k, v in data.items()]
    out = nc.dram_tensor("out", (P, KT, T), F32, kind="ExternalOutput").ap()
    build(nc, *args, out)
    r = run_bass_kernel_spmd(nc, [data], core_ids=[0])
    y = r.results[0]["out"]
    return np.ascontiguousarray(y.transpose(1, 0, 2).reshape(D, T).T).reshape(1, T, D)
```
